# Optimizing a Trainium2 kernel written in Bass

```python
import math
import jax, jax.numpy as jnp
from jax import lax
import numpy as np

D_MODEL = 1024
BATCH = 1
SEQ = 256
DEPTH = 2
DEC_BATCH = 8
DEC_SEQ = 4
PAST_LEN = 2048
PAGE_SIZE = 128

N_EVEN = (DEPTH + 1) // 2
N_ODD = DEPTH // 2
CONV_WIDTH = 3
N_HEADS = 16
HEAD_DIM = D_MODEL // N_HEADS
N_KV_HEADS = 4
HEADS_PER_GROUP = N_HEADS // N_KV_HEADS
N_BRANCHES = 3
CMP_BLOCK = 32
SEL_BLOCK = 64
CMP_PER_SEL = SEL_BLOCK // CMP_BLOCK
N_SELECTED = 16
WINDOW = 512
N_BUCKETS = 32
MAX_DISTANCE = 128
D_FF = 2816
N_EXPERTS = 8
TOP_K = 2
D_FF_EXPERT = 1408
PLE_DIM = 256
QB_SEL = 16
QB_WIN = 128
EPS = 1e-6
NSA_Q_COLS = N_HEADS * HEAD_DIM
NSA_KV_COLS = N_BRANCHES * N_KV_HEADS * 2 * HEAD_DIM
NSA_IN = NSA_Q_COLS + NSA_KV_COLS + N_BRANCHES * N_HEADS
FORCED_SCORE = 1e4
NEG = -1e30

kernel_name = "hybrid_conv_nsa_moe_ple_step"

def rmsnorm(x, g):
    xf = x.astype(jnp.float32)
    y = xf * lax.rsqrt(jnp.mean(xf * xf, axis=-1, keepdims=True) + EPS)
    return (y * g.astype(jnp.float32)).astype(x.dtype)

def masked_softmax(logits, mask, axis=-1):
    p = jax.nn.softmax(jnp.where(mask, logits, NEG), axis=axis)
    return jnp.where(mask, p, 0.0)

def rel_bucket(dist):
    n = jnp.maximum(dist, 0)
    max_exact = N_BUCKETS // 2
    nf = jnp.maximum(n, 1).astype(jnp.float32)
    large = max_exact + (jnp.log(nf / max_exact) / math.log(MAX_DISTANCE / max_exact)
                         * (N_BUCKETS - max_exact)).astype(jnp.int32)
    large = jnp.minimum(large, N_BUCKETS - 1)
    return jnp.where(n < max_exact, n, large)

def rel_bias_heads(rel_bias, rel):
    bias = rel_bias[rel_bucket(rel)].astype(jnp.float32)
    q_n, k_n = rel.shape
    return bias.reshape(q_n, k_n, N_KV_HEADS, HEADS_PER_GROUP).transpose(2, 3, 0, 1)

def conv_mixer(a, state, w_in, w_conv, w_out):
    gb, gc, v = jnp.split(a @ w_in, 3, axis=-1)
    u = gc * v
    u_ext = jnp.concatenate([state.astype(u.dtype), u], axis=1)
    t = a.shape[1]
    conv = w_conv[0] * u_ext[:, 0:t]
    for k in range(1, CONV_WIDTH):
        conv = conv + w_conv[k] * u_ext[:, k:k + t]
    return (gb * conv) @ w_out, u_ext[:, t:]

def nsa_project(a, w_in, q_gain):
    b, t, _ = a.shape
    proj = a @ w_in
    q = proj[..., :NSA_Q_COLS].reshape(b, t, N_KV_HEADS, HEADS_PER_GROUP, HEAD_DIM)
    q = rmsnorm(q, q_gain) * HEAD_DIM ** -0.5
    kv = proj[..., NSA_Q_COLS:NSA_Q_COLS + NSA_KV_COLS].reshape(b, t, N_BRANCHES, N_KV_HEADS, 2, HEAD_DIM)
    gates = jax.nn.sigmoid(proj[..., NSA_Q_COLS + NSA_KV_COLS:].reshape(
        b, t, N_BRANCHES, N_KV_HEADS, HEADS_PER_GROUP))
    return q, kv[:, :, 0], kv[:, :, 1], kv[:, :, 2], gates

def compress(rows, w_cmp):
    b, L = rows.shape[:2]
    nc = L // CMP_BLOCK
    blocks = rows[:, :nc * CMP_BLOCK].reshape(b, nc, CMP_BLOCK, N_KV_HEADS, 2, HEAD_DIM)
    return jnp.einsum('bnlgcd,lgcde->bngce', blocks, w_cmp)

def cmp_branch(q, kv_c, q_pos, rel_bias, k_gain):
    nc = kv_c.shape[1]
    kc = rmsnorm(kv_c[..., 0, :], k_gain)
    vc = kv_c[..., 1, :]
    end_pos = (jnp.arange(nc) + 1) * CMP_BLOCK - 1
    rel = q_pos[:, None] - end_pos[None, :]
    logits = jnp.einsum('btgrd,bngd->bgrtn', q, kc).astype(jnp.float32) + rel_bias_heads(rel_bias, rel)
    p = masked_softmax(logits, rel >= 0)
    out = jnp.einsum('bgrtn,bngd->btgrd', p.astype(vc.dtype), vc)
    return out, p.sum(axis=2)

def sel_attend(q, k, v, k_pos, q_pos, rel_bias):
    logits = jnp.einsum('btgrd,bgtnd->bgtnr', q, k).astype(jnp.float32)
    bucket = rel_bucket(q_pos[None, None, :, None] - k_pos)
    table = rel_bias.reshape(N_BUCKETS, N_KV_HEADS, HEADS_PER_GROUP)
    bias = table[bucket, jnp.arange(N_KV_HEADS)[None, :, None, None]].astype(jnp.float32)
    mask = (k_pos <= q_pos[None, None, :, None])[..., None]
    p = masked_softmax(logits + bias, mask, axis=3)
    return jnp.einsum('bgtnr,bgtnd->btgrd', p.astype(v.dtype), v)

def sel_branch_prompt(q, kv_s, imp_sel, rel_bias, k_gain):
    b, s = q.shape[:2]
    ns = imp_sel.shape[-1]
    n_top = min(N_SELECTED, ns)
    cur = jnp.arange(s) // SEL_BLOCK
    blk = jnp.arange(ns)[None, :]
    forced = (blk == 0) | (blk == cur[:, None]) | (blk == cur[:, None] - 1)
    valid = blk <= cur[:, None]
    score = jnp.where(forced, FORCED_SCORE, jnp.where(valid, imp_sel, -1.0))
    _, idx = lax.top_k(score, n_top)
    kvn = jnp.stack([rmsnorm(kv_s[..., 0, :], k_gain), kv_s[..., 1, :]], axis=-2)
    kv_blocks = kvn.reshape(b, ns, SEL_BLOCK, N_KV_HEADS, 2, HEAD_DIM).transpose(0, 3, 1, 2, 4, 5)
    nqb = s // QB_SEL
    q_b = q.reshape(b, nqb, QB_SEL, N_KV_HEADS, HEADS_PER_GROUP, HEAD_DIM).swapaxes(0, 1)
    idx_b = idx.reshape(b, N_KV_HEADS, nqb, QB_SEL, n_top).transpose(2, 0, 1, 3, 4)
    bi = jnp.arange(b)[:, None, None, None]
    gi = jnp.arange(N_KV_HEADS)[None, :, None, None]

    def step(args):
        qn, idn, n = args
        rows = kv_blocks[bi, gi, idn]
        rows = rows.reshape(b, N_KV_HEADS, QB_SEL, n_top * SEL_BLOCK, 2, HEAD_DIM)
        k_pos = (idn[..., None] * SEL_BLOCK + jnp.arange(SEL_BLOCK)).reshape(
            b, N_KV_HEADS, QB_SEL, n_top * SEL_BLOCK)
        q_pos = n * QB_SEL + jnp.arange(QB_SEL)
        return sel_attend(qn, rows[..., 0, :], rows[..., 1, :], k_pos, q_pos, rel_bias)

    out = lax.map(step, (q_b, idx_b, jnp.arange(nqb)))
    return out.swapaxes(0, 1).reshape(b, s, N_KV_HEADS, HEADS_PER_GROUP, HEAD_DIM)

def sel_branch_sample(q, kv_new, pool, page_table, imp_sel, past_len, rel_bias, k_gain):
    b, t = q.shape[:2]
    page = pool.shape[1]
    ns = imp_sel.shape[-1]
    n_top = min(N_SELECTED - 1, ns)
    blk = jnp.arange(ns)
    forced = (blk == 0) | (blk == ns - 1)
    score = jnp.where(forced, FORCED_SCORE, imp_sel)
    _, idx = lax.top_k(score, n_top)
    start = idx * SEL_BLOCK
    phys = page_table[jnp.arange(b)[:, None, None, None], start // page]
    off = (start % page)[..., None] + jnp.arange(SEL_BLOCK)
    gi = jnp.arange(N_KV_HEADS)[None, :, None, None, None]
    rows = pool[phys[..., None], off, gi]
    rows = rows.reshape(b, N_KV_HEADS, t, n_top * SEL_BLOCK, 2, HEAD_DIM).astype(kv_new.dtype)
    cur = jnp.broadcast_to(kv_new.transpose(0, 2, 1, 3, 4)[:, :, None], (b, N_KV_HEADS, t, t, 2, HEAD_DIM))
    rows = jnp.concatenate([rows, cur], axis=3)
    q_pos = past_len + jnp.arange(t)
    k_pos = jnp.concatenate([
        (start[..., None] + jnp.arange(SEL_BLOCK)).reshape(b, N_KV_HEADS, t, n_top * SEL_BLOCK),
        jnp.broadcast_to(q_pos, (b, N_KV_HEADS, t, t))], axis=3)
    return sel_attend(q, rmsnorm(rows[..., 0, :], k_gain), rows[..., 1, :], k_pos, q_pos, rel_bias)

def win_branch_prompt(q, kv_w, rel_bias, k_gain):
    b, s = q.shape[:2]
    pad = ((0, 0), (WINDOW, 0), (0, 0), (0, 0))
    kpad = jnp.pad(rmsnorm(kv_w[..., 0, :], k_gain), pad)
    vpad = jnp.pad(kv_w[..., 1, :], pad)
    nqb = s // QB_WIN
    span = WINDOW + QB_WIN
    i = jnp.arange(QB_WIN)
    j = jnp.arange(span)
    rel = i[:, None] + WINDOW - j[None, :]
    band = (rel >= 0) & (rel < WINDOW)
    bias = rel_bias_heads(rel_bias, rel)
    q_b = q.reshape(b, nqb, QB_WIN, N_KV_HEADS, HEADS_PER_GROUP, HEAD_DIM).swapaxes(0, 1)

    def step(args):
        qn, n = args
        kn = lax.dynamic_slice_in_dim(kpad, n * QB_WIN, span, axis=1)
        vn = lax.dynamic_slice_in_dim(vpad, n * QB_WIN, span, axis=1)
        logits = jnp.einsum('bqgrd,bjgd->bgrqj', qn, kn).astype(jnp.float32) + bias
        mask = band & (n * QB_WIN - WINDOW + j >= 0)[None, :]
        p = masked_softmax(logits, mask)
        return jnp.einsum('bgrqj,bjgd->bqgrd', p.astype(vn.dtype), vn)

    out = lax.map(step, (q_b, jnp.arange(nqb)))
    return out.swapaxes(0, 1).reshape(b, s, N_KV_HEADS, HEADS_PER_GROUP, HEAD_DIM)

def win_branch_sample(q, kv_new, buf, past_len, rel_bias, k_gain):
    t = q.shape[1]
    wb = buf.shape[1]
    rows = jnp.concatenate([buf.astype(kv_new.dtype), kv_new], axis=1)
    k = rmsnorm(rows[..., 0, :], k_gain)
    v = rows[..., 1, :]
    q_pos = past_len + jnp.arange(t)
    k_pos = past_len - wb + jnp.arange(wb + t)
    rel = q_pos[:, None] - k_pos[None, :]
    logits = jnp.einsum('btgrd,bjgd->bgrtj', q, k).astype(jnp.float32) + rel_bias_heads(rel_bias, rel)
    p = masked_softmax(logits, (rel >= 0) & (rel < WINDOW))
    out = jnp.einsum('bgrtj,bjgd->btgrd', p.astype(v.dtype), v)
    return out, rows[:, t:]

def nsa_merge(gates, o_c, o_s, o_w, w_out):
    o = gates[:, :, 0, ..., None] * o_c + gates[:, :, 1, ..., None] * o_s + gates[:, :, 2, ..., None] * o_w
    b, t = o.shape[:2]
    return o.reshape(b, t, N_HEADS * HEAD_DIM) @ w_out

def nsa_prompt(a, w_in, w_cmp, q_gain, k_gain, w_out, rel_bias):
    b, s, _ = a.shape
    q, kv_c, kv_s, kv_w, gates = nsa_project(a, w_in, q_gain)
    o_c, imp = cmp_branch(q, compress(kv_c, w_cmp), jnp.arange(s), rel_bias, k_gain[0])
    ns = s // SEL_BLOCK
    imp_sel = imp[..., :ns * CMP_PER_SEL].reshape(b, N_KV_HEADS, s, ns, CMP_PER_SEL).sum(-1)
    o_s = sel_branch_prompt(q, kv_s, imp_sel, rel_bias, k_gain[1])
    o_w = win_branch_prompt(q, kv_w, rel_bias, k_gain[2])
    y = nsa_merge(gates, o_c, o_s, o_w, w_out)
    return y, kv_c, kv_s, kv_w[:, s - min(WINDOW, s):]

def nsa_sample(a, pool_cmp, pool_sel, buf_win, page_table, w_in, w_cmp, q_gain, k_gain, w_out, rel_bias):
    b, t, _ = a.shape
    past_len = page_table.shape[1] * pool_cmp.shape[1]
    q, kv_c, kv_s, kv_w, gates = nsa_project(a, w_in, q_gain)
    q_pos = past_len + jnp.arange(t)
    rows_c = pool_cmp[page_table].reshape(b, past_len, N_KV_HEADS, 2, HEAD_DIM).astype(kv_c.dtype)
    n_extra = (t // CMP_BLOCK) * CMP_BLOCK
    if n_extra:
        rows_c = jnp.concatenate([rows_c, kv_c[:, :n_extra]], axis=1)
    o_c, imp = cmp_branch(q, compress(rows_c, w_cmp), q_pos, rel_bias, k_gain[0])
    ns = past_len // SEL_BLOCK
    imp_sel = imp[..., :ns * CMP_PER_SEL].reshape(b, N_KV_HEADS, t, ns, CMP_PER_SEL).sum(-1)
    o_s = sel_branch_sample(q, kv_s, pool_sel, page_table, imp_sel, past_len, rel_bias, k_gain[1])
    o_w, new_buf = win_branch_sample(q, kv_w, buf_win, past_len, rel_bias, k_gain[2])
    y = nsa_merge(gates, o_c, o_s, o_w, w_out)
    return y, kv_c, kv_s, new_buf

def dense_swiglu(a, w_gate, w_up, w_down):
    return (jax.nn.silu(a @ w_gate) * (a @ w_up)) @ w_down

def moe_swiglu(a, router, w_gate, w_up, w_down):
    logits = (a @ router).astype(jnp.float32)
    top_v, top_i = lax.top_k(logits, TOP_K)
    top_w = jax.nn.softmax(top_v, axis=-1)
    gate = jnp.sum(jax.nn.one_hot(top_i, N_EXPERTS, dtype=jnp.float32) * top_w[..., None], axis=-2)
    out = jnp.zeros_like(a)
    for e in range(N_EXPERTS):
        h = jax.nn.silu(a @ w_gate[e]) * (a @ w_up[e])
        out = out + gate[..., e:e + 1].astype(a.dtype) * (h @ w_down[e])
    return out

def ple_add(h, p_i, gain, w_proj, w_gate):
    g = jax.nn.sigmoid(rmsnorm(h, gain) @ w_gate)
    return h + g * (p_i @ w_proj)

def setup_inputs(seed: int = 0) -> dict:
    key = jax.random.key(seed)
    ks = iter(jax.random.split(key, 40))

    def nrm(shape, scale=1.0):
        return jax.random.normal(next(ks), shape, jnp.float32) * scale

    def gain(shape):
        return 1.0 + 0.1 * nrm(shape)

    n_pages = PAST_LEN // PAGE_SIZE
    n_used = DEC_BATCH * n_pages
    n_pool = n_used + (n_used + 3) // 4
    wb = min(WINDOW, PAST_LEN)
    x_prompt = nrm((BATCH, SEQ, D_MODEL))
    x_sample = nrm((DEC_BATCH, DEC_SEQ, D_MODEL))
    state_conv = nrm((N_EVEN, DEC_BATCH, CONV_WIDTH - 1, D_MODEL))
    cache_cmp = nrm((N_ODD, n_pool, PAGE_SIZE, N_KV_HEADS, 2, HEAD_DIM))
    cache_sel = nrm((N_ODD, n_pool, PAGE_SIZE, N_KV_HEADS, 2, HEAD_DIM))
    state_win = nrm((N_ODD, DEC_BATCH, wb, N_KV_HEADS, 2, HEAD_DIM))
    page_table = jax.random.permutation(next(ks), n_pool)[:n_used].reshape(DEC_BATCH, n_pages).astype(jnp.int32)
    p_prompt = nrm((DEPTH, BATCH, SEQ, PLE_DIM))
    p_sample = nrm((DEPTH, DEC_BATCH, DEC_SEQ, PLE_DIM))
    return {
        "x_prompt": x_prompt, "x_sample": x_sample,
        "state_conv": state_conv, "cache_cmp": cache_cmp, "cache_sel": cache_sel,
        "state_win": state_win, "page_table": page_table,
        "p_prompt": p_prompt, "p_sample": p_sample,
        "norm_mix": gain((DEPTH, D_MODEL)),
        "norm_ffn": gain((DEPTH, D_MODEL)),
        "norm_ple": gain((DEPTH, D_MODEL)),
        "conv_w_in": nrm((N_EVEN, D_MODEL, 3 * D_MODEL), D_MODEL ** -0.5),
        "conv_w": nrm((N_EVEN, CONV_WIDTH, D_MODEL), CONV_WIDTH ** -0.5),
        "conv_w_out": nrm((N_EVEN, D_MODEL, D_MODEL), D_MODEL ** -0.5),
        "nsa_w_in": nrm((N_ODD, D_MODEL, NSA_IN), D_MODEL ** -0.5),
        "nsa_w_cmp": nrm((N_ODD, CMP_BLOCK, N_KV_HEADS, 2, HEAD_DIM, HEAD_DIM), (CMP_BLOCK * HEAD_DIM) ** -0.5),
        "nsa_q_norm": gain((N_ODD, HEAD_DIM)),
        "nsa_k_norm": gain((N_ODD, N_BRANCHES, HEAD_DIM)),
        "nsa_w_out": nrm((N_ODD, N_HEADS * HEAD_DIM, D_MODEL), D_MODEL ** -0.5),
        "rel_bias": nrm((N_BUCKETS, N_HEADS), 0.5),
        "ffn_w_gate": nrm((N_EVEN, D_MODEL, D_FF), D_MODEL ** -0.5),
        "ffn_w_up": nrm((N_EVEN, D_MODEL, D_FF), D_MODEL ** -0.5),
        "ffn_w_down": nrm((N_EVEN, D_FF, D_MODEL), D_FF ** -0.5),
        "moe_router": nrm((N_ODD, D_MODEL, N_EXPERTS), D_MODEL ** -0.5),
        "moe_w_gate": nrm((N_ODD, N_EXPERTS, D_MODEL, D_FF_EXPERT), D_MODEL ** -0.5),
        "moe_w_up": nrm((N_ODD, N_EXPERTS, D_MODEL, D_FF_EXPERT), D_MODEL ** -0.5),
        "moe_w_down": nrm((N_ODD, N_EXPERTS, D_FF_EXPERT, D_MODEL), D_FF_EXPERT ** -0.5),
        "ple_w_proj": nrm((DEPTH, PLE_DIM, D_MODEL), PLE_DIM ** -0.5),
        "ple_w_gate": nrm((DEPTH, D_MODEL, D_MODEL), D_MODEL ** -0.5),
    }

def reference(x_prompt, x_sample, state_conv, cache_cmp, cache_sel, state_win, page_table,
              p_prompt, p_sample, norm_mix, norm_ffn, norm_ple, conv_w_in, conv_w, conv_w_out,
              nsa_w_in, nsa_w_cmp, nsa_q_norm, nsa_k_norm, nsa_w_out, rel_bias,
              ffn_w_gate, ffn_w_up, ffn_w_down, moe_router, moe_w_gate, moe_w_up, moe_w_down,
              ple_w_proj, ple_w_gate):
    h_p, h_s = x_prompt, x_sample
    b_p = x_prompt.shape[0]
    conv_p, conv_s, cmp_p, cmp_s, sel_p, sel_s, win_p, win_s = ([] for _ in range(8))
    for i in range(DEPTH):
        li = i // 2
        a_p = rmsnorm(h_p, norm_mix[i])
        a_s = rmsnorm(h_s, norm_mix[i])
        if i % 2 == 0:
            zero_state = jnp.zeros((b_p, CONV_WIDTH - 1, D_MODEL), x_prompt.dtype)
            y_p, st_p = conv_mixer(a_p, zero_state, conv_w_in[li], conv_w[li], conv_w_out[li])
            y_s, st_s = conv_mixer(a_s, state_conv[li], conv_w_in[li], conv_w[li], conv_w_out[li])
            conv_p.append(st_p)
            conv_s.append(st_s)
        else:
            y_p, c_p, s_p, w_p = nsa_prompt(a_p, nsa_w_in[li], nsa_w_cmp[li], nsa_q_norm[li],
                                            nsa_k_norm[li], nsa_w_out[li], rel_bias)
            y_s, c_s, s_s, w_s = nsa_sample(a_s, cache_cmp[li], cache_sel[li], state_win[li], page_table,
                                            nsa_w_in[li], nsa_w_cmp[li], nsa_q_norm[li],
                                            nsa_k_norm[li], nsa_w_out[li], rel_bias)
            cmp_p.append(c_p)
            cmp_s.append(c_s)
            sel_p.append(s_p)
            sel_s.append(s_s)
            win_p.append(w_p)
            win_s.append(w_s)
        h_p = h_p + y_p
        h_s = h_s + y_s
        f_p = rmsnorm(h_p, norm_ffn[i])
        f_s = rmsnorm(h_s, norm_ffn[i])
        if i % 2 == 0:
            h_p = h_p + dense_swiglu(f_p, ffn_w_gate[li], ffn_w_up[li], ffn_w_down[li])
            h_s = h_s + dense_swiglu(f_s, ffn_w_gate[li], ffn_w_up[li], ffn_w_down[li])
        else:
            h_p = h_p + moe_swiglu(f_p, moe_router[li], moe_w_gate[li], moe_w_up[li], moe_w_down[li])
            h_s = h_s + moe_swiglu(f_s, moe_router[li], moe_w_gate[li], moe_w_up[li], moe_w_down[li])
        h_p = ple_add(h_p, p_prompt[i], norm_ple[i], ple_w_proj[i], ple_w_gate[i])
        h_s = ple_add(h_s, p_sample[i], norm_ple[i], ple_w_proj[i], ple_w_gate[i])
    return (h_p, h_s, jnp.stack(conv_p), jnp.stack(conv_s), jnp.stack(cmp_p), jnp.stack(cmp_s),
            jnp.stack(sel_p), jnp.stack(sel_s), jnp.stack(win_p), jnp.stack(win_s))


_drawn_inputs = setup_inputs


def setup_inputs(seed=0):
    import zlib

    import numpy as np

    out = dict(_drawn_inputs(seed))
    spreads = {}
    factors = {'cache_sel': 3.175}
    for name, (base, spread) in spreads.items():
        noise = np.random.default_rng([zlib.crc32(name.encode()), seed]).standard_normal(out[name].shape)
        drawn = base * np.exp(spread * noise) if base else spread * noise
        out[name] = __import__('jax').numpy.asarray(drawn.astype(out[name].dtype))
    for name, factor in factors.items():
        out[name] = (out[name] * factor).astype(out[name].dtype)
    return out
```

```python
import math
from contextlib import ExitStack

import numpy as np
import concourse.bass as bass
from concourse import mybir

D = 1024
T = 288
TP = 256
B = 8
STEPS = 4
C = D // 128
HEADS = 16
GROUPS = 4
R = 4
HD = 64
PAGES = 16
POOL = 160
FE = 1408
FC = FE // 128
EXPERTS = 8
HALVES = 2
BUCKETS = 32
EPS = 1e-6
NEG = -1e30
KEYS = 2048
WIN = 512
NB = 64
GS, DS, PS = 11, 4, 6
GT = 1024
DT = FC * 128
OHL = 511


def bucket(dist):
    n = np.maximum(dist, 0)
    nf = np.maximum(n, 1).astype(np.float32)
    large = 16 + (np.log(nf / np.float32(16)) / np.float32(math.log(8.0)) * np.float32(16)).astype(np.int32)
    return np.where(n < 16, n, np.minimum(large, BUCKETS - 1))


def result_order():
    o = [("tp", i) for i in range(8)] + [("tc",)] + [("ts", i) for i in range(6)]
    for b in range(B):
        o += [("ck", b), ("cv", b)]
    o += [("css", 0), ("css", 1)] + [("ct", p) for p in range(4)]
    o += [("norm", 0)]
    for c in range(C):
        o += [("gc", c), ("v", c), ("gb", c)]
    o += [("co", c) for c in range(C)] + [("norm", 1)]
    o += [("f", 0, k) for k in range(HALVES * (2 * FC + C))]
    o += [("norm", 2)]
    for c in range(C):
        o += [("pg", 0, c), ("pp", 0, c)]
    o += [("norm", 3)]
    o += [("kv", c) for c in range(4)]
    for c in range(4, 8):
        o += [("kv", c)]
        if c > 4:
            o += [("kss", c - 1)]
    o += [("vt", 0), ("vt", 1), ("vt", 2), ("kss", 7), ("gt",)]
    for j in range(8):
        o += [("q", j)]
        if j:
            o += [("qss", j - 1)]
    o += [("kcp",), ("qss", 7), ("vcp",), ("kcps",)]
    for u in range(17):
        if u < 16:
            o += [("pc", u), ("pl", u, 0), ("pl", u, 1)]
        if u:
            o += [("ptc", u - 1), ("ptp", u - 1, 0), ("ptp", u - 1, 1), ("po", u - 1)]
    for p in range(4):
        o += [("sc", p), ("sn", p), ("wq", p), ("wss", p), ("imp", p)]
        for t in range(4):
            o += [("sq", p, t), ("sss", p, t)]
        o += [("pt", p, i) for i in range(6)]
    o += [("wo", c) for c in range(C)] + [("norm", 4), ("rt",), ("gT",)] + [("gb8", e) for e in range(EXPERTS)]
    o += [("f", 1, k) for k in range(EXPERTS * (2 * FC + C))]
    o += [("norm", 5)]
    for c in range(C):
        o += [("pg", 1, c), ("pp", 1, c)]
    return {label: n for n, label in enumerate(o)}


def rstd_order():
    o = [("css", 0), ("css", 1)] + [("norm", i) for i in range(4)] + [("kss", c) for c in range(4, 8)]
    o += [("qss", j) for j in range(8)] + [("kcps",)]
    for p in range(4):
        o += [("wss", p)] + [("sss", p, t) for t in range(4)]
    o += [("norm", 4), ("norm", 5)]
    return {label: n for n, label in enumerate(o)}


def g_tile_order():
    o = []
    for c in range(C):
        o += [("gc", c), ("v", c), ("gb", c)]
    o += [("co", c) for c in range(C)]
    o += [("f", 0, k) for k in range(HALVES * 2 * FC)]
    for i in range(2):
        o += [("pp", 0, i)] + [("pg", 0, 4 * i + k) for k in range(4)]
    o += [("kv", c) for c in range(8)] + [("vt", i) for i in range(4)] + [("q", j) for j in range(8)]
    for p in range(4):
        o += [("wk", p, 0), ("wk", p, 1)]
        o += [("sk", p, t, b2) for t in range(4) for b2 in range(2)]
        for b2 in range(2):
            o += [("wv", p, b2)] + [("sv", p, b2, t) for t in range(4)]
    o += [("wo", c) for c in range(C)]
    o += [("f", 1, k) for k in range(EXPERTS * 2 * FC)]
    for i in range(2):
        o += [("pp", 1, i)] + [("pg", 1, 4 * i + k) for k in range(4)]
    return {label: n for n, label in enumerate(o)}


def trunk(nc, A, O):
    f32 = mybir.dt.float32
    ALU = mybir.AluOpType
    ACT = mybir.ActivationFunctionType
    AX = mybir.AxisListType
    RES = result_order()
    GN = g_tile_order()
    RN = rstd_order()
    LF = (0, HALVES * C)
    PER = 2 * FC + C
    assert PER % PS == 0 and (2 * FC) % GS == 0 and C % DS == 0

    with ExitStack() as ctx:
        def sem(name):
            return ctx.enter_context(nc.semaphore(name))

        used = [0]

        def region(name, n):
            t = ctx.enter_context(nc.sbuf_tensor(name, [128, n], f32))
            used[0] += n
            return t

        hT = region("hT", C * T)[:, :].rearrange("p (c t) -> p c t", t=T)
        aT_ = region("aT", C * T)
        aT = aT_[:, :].rearrange("p (c t) -> p c t", t=T)
        gring = region("gring", GS * GT)
        ident = region("ident", 128)
        ones = region("ones", 128)
        bones = region("bones", 128)
        bo32 = region("bo32", 32)
        rsum = region("rsum", 128)
        tri = region("tri", 1024)[:, :].rearrange("p (i j) -> p i j", j=32)
        pmask = region("pmask", 16)[:, :].rearrange("p (i n) -> p i n", n=8)
        wgate = region("wgate", C * 48)[:, :].rearrange("p (c n) -> p c n", n=48)
        rout = region("rout", C * 8)[:, :].rearrange("p (c n) -> p c n", n=8)
        gains = region("gains", 6 * C)
        convw = region("convw", 3 * C)
        state = region("state", C * 16)[:, :].rearrange("p (c b k) -> p c b k", b=B, k=2)
        gq = region("gq", 1)
        gqs = region("gqs", 1)
        gk = region("gk", 3)
        pT = region("pT", 2 * 2 * T)[:, :].rearrange("p (l k t) -> p l k t", l=2, k=2)
        sg_ = region("sg", 2 * T)
        sg = sg_[:, :].rearrange("p (i t) -> p i t", t=T)
        tmp_ = region("tmp", 2 * T)
        tmp = tmp_[:, :].rearrange("p (i t) -> p i t", t=T)
        rs_ = region("rs", 2 * T)
        rs = rs_[:, :].rearrange("p (i t) -> p i t", t=T)
        epsc = region("epsc", 1)
        small = region("small", 416)
        tabP = region("tabP", HEADS * 256)[:, :].rearrange("p (h k) -> p h k", k=256)
        tabC = region("tabC", 256)[:, :].rearrange("p (i n h) -> p i n h", i=2, n=8)
        tS = region("tS", KEYS)
        tW = region("tW", WIN)
        tN = region("tN", 4 * 32)[:, :].rearrange("p (a k) -> p a k", k=32)
        tCs = region("tCs", 128)
        kcn_ = region("kcn", 2 * B * NB)
        kcn = kcn_[:, :].rearrange("p (a n) -> p a n", a=2)
        vcs = region("vcs", 4 * 256)[:, :].rearrange("p (a n) -> p a n", a=4)
        gtok = region("gtok", 3 * 48)[:, :].rearrange("p (i n) -> p i n", n=48)
        grow = region("grow", 12)[:, :].rearrange("p (a n) -> p a n", n=3)
        Q = region("Q", 11136)
        q1 = Q[:, 0:2304].rearrange("p (c t) -> p c t", t=T)
        kvT = Q[:, 2304:4608].rearrange("p (c t) -> p c t", t=T)
        kn = Q[:, 4608:5760].rearrange("p (c t) -> p c t", t=T)
        vtok = Q[:, 5760:7296].rearrange("p (i n) -> p i n", n=512)
        QB = Q[:, 7296:8832].rearrange("p (r b a m) -> p r b a m", r=3, b=B, a=2)
        oT = Q[:, 8832:11136].rearrange("p (c t) -> p c t", t=T)
        qraw = oT
        dring = Q[:, 0:DS * DT]
        hff = Q[:, 5632:5632 + FC * T].rearrange("p (c t) -> p c t", t=T)
        sqn = Q[:, 5632:5632 + C * T].rearrange("p (c t) -> p c t", t=T)
        zT = Q[:, 8800:8800 + C * T].rearrange("p (c t) -> p c t", t=T)
        gbc = zT
        sqs = [zT if i in (2, 5) else sqn for i in range(6)]
        cbufs = [gring[:, 0:4096], gring[:, 4096:8192], Q[:, 0:4096], Q[:, 4096:8192]]
        kcscale = [Q[:, 9216 + 512 * a:9728 + 512 * a] for a in range(2)]
        kcsq = Q[:, 8192:8192 + 1024].rearrange("p (a n) -> p a n", a=2)
        ohs = Q[:, 5632:8352]
        masks = Q[:, 8352:9120]
        ohv = Q[0:BUCKETS + 1, 9120:9120 + OHL]
        lt = Q[:, 9640:9768]
        rbx = Q[0:BUCKETS + 1, 9768:9784]
        X = region("X", 10816)
        wc = X[:, 0:8192].rearrange("p (k e) -> p k e", e=64)
        UE = 2 + TP + B * 6
        uext = X[:, 8192:8192 + C * UE].rearrange("p (c t) -> p c t", t=UE)
        vraw = X[:, 8192:8192 + 1024].rearrange("p (a n) -> p a n", a=2)
        cstage = X[:, 10640:10784]
        kvp = X[:, 8192:8192 + 8 * TP].rearrange("p (c t) -> p c t", t=TP)
        S = X[:, 0:KEYS + 32]
        SW = X[:, 2080:2080 + WIN + 32]
        SC = X[:, 2624:2752]
        SCg = X[:, 2752:2880]
        ksq = X[:, 2880:4928].rearrange("p (i n) -> p i n", i=2)
        rsb = [X[:, 4928:5440], X[:, 8384:8896]]
        PT = X[:, 5440:8384].rearrange("p (k m) -> p k m", m=128)
        Sp = X[:, 2880:4416].rearrange("p (i n) -> p i n", i=2)
        PTp = X[:, 4416:5952].rearrange("p (i r n) -> p i r n", i=2, r=2)
        PTc = X[0:8, 5952:6464].rearrange("p (i n) -> p i n", i=2)
        Scp = X[:, 6464:6496].rearrange("p (u i n) -> p u i n", u=2, i=2)
        sel8 = X[:, 0:EXPERTS * 128]
        cnt1 = aT_[:, 0:1024].rearrange("p (i j) -> p i j", j=32)
        cnt2 = aT_[:, 1024:2048].rearrange("p (i j) -> p i j", j=32)
        vcp = sg_[0:8, 0:256]
        kcp = sg_[:, 256:272].rearrange("p (a n) -> p a n", a=2)
        kcpn = sg_[:, 272:288].rearrange("p (a n) -> p a n", a=2)
        nmp = small[:, 0:12].rearrange("p (u i r) -> p u i r", u=2, i=2)
        smp = small[:, 12:24].rearrange("p (u i r) -> p u i r", u=2, i=2)
        scp = small[:, 24:36].rearrange("p (u i r) -> p u i r", u=2, i=2)
        mxs = small[:, 36:39]
        sms = small[:, 40:43]
        fac = small[:, 44:47]
        score = small[:, 48:80]
        rank = small[:, 80:112]
        blkm = small[:, 112:144]
        half = small[:, 144:208]
        rl = small[:, 208:232].rearrange("p (i e) -> p i e", e=8)
        rk = small[:, 232:256].rearrange("p (i e) -> p i e", e=8)
        rmx = small[:, 256:259]
        rsm = small[:, 260:263]
        rg = small[:, 264:288].rearrange("p (i e) -> p i e", e=8)
        gT = tmp_[0:8, 0:T]
        cmp8 = [small[:, 288 + 64 * i:352 + 64 * i].rearrange("p (i j) -> p i j", j=8) for i in range(2)]

        banks = [ctx.enter_context(nc.psum_tensor(f"bank{i}", [128, 512], f32)) for i in range(PS)]
        oP = [ctx.enter_context(nc.psum_tensor(f"oP{i}", [128, 512], f32)) for i in range(2)]

        psum_full = [sem(f"psum_full{i}") for i in range(PS)]
        psum_drained = [sem(f"psum_drained{i}") for i in range(PS)]
        g_in = [sem(f"g_in{i}") for i in range(GS)]
        d_in = [sem(f"d_in{i}") for i in range(DS)]
        c_in = [sem(f"c_in{i}") for i in range(4)]
        keys_used, values_used = sem("keys_used"), sem("values_used")
        consts_in, wcmp_in, lt_in, sel8_in = sem("consts_in"), sem("wcmp_in"), sem("lt_in"), sem("sel8_in")
        lt_clear, rb_mask, eps_set, rstd_ready = sem("lt_clear"), sem("rb_mask"), sem("eps_set"), sem("rstd_ready")
        sq_ready, a_ready = sem("sq_ready"), sem("a_ready")
        conv_staged, win_stored = sem("conv_staged"), sem("win_stored")
        sig_ready, hff_ready, hsq_ready = sem("sig_ready"), sem("hff_ready"), sem("hsq_ready")
        kcn_ready, kn_ready, q_ready = sem("kcn_ready"), sem("kn_ready"), sem("q_ready")
        kvp_in, gates_out, gates_in = sem("kvp_in"), sem("gates_out"), sem("gates_in")
        qb_ready = sem("qb_ready")
        pmax_ready, pexp_ready, pscaled = sem("pmax_ready"), sem("pexp_ready"), sem("pscaled")
        smax_ready, sexp_ready, cprob_ready, sscaled = sem("smax_ready"), sem("sexp_ready"), sem("cprob_ready"), sem("sscaled")
        ksq_ready, so_ready = sem("ksq_ready"), sem("so_ready")
        rg_ready, rmax_ready, rexp_ready = sem("rg_ready"), sem("rmax_ready"), sem("rexp_ready")
        stored, rows_stored = sem("stored"), sem("rows_stored")
        dve_step, act_step = sem("dve_step"), sem("act_step")

        NCONST = 20

        def bank(label, k=0):
            return banks[(RES[label] + k) % PS]

        def turn(label, e=0, k=0):
            return (RES[label] + k) // PS + (PER // PS) * e

        def full(eng, label, e=0, k=0):
            eng.wait_ge(psum_full[(RES[label] + k) % PS], turn(label, e, k) + 1)

        def drained(eng, label, e=0, k=0):
            eng.wait_ge(psum_drained[(RES[label] + k) % PS], turn(label, e, k) + 1)

        def bank_free(eng, label, e=0, k=0):
            if RES[label] + k >= PS:
                eng.wait_ge(psum_drained[(RES[label] + k) % PS], turn(label, e, k))

        def fill(ins, label, k=0):
            ins.then_inc(psum_full[(RES[label] + k) % PS], 1)

        def drain(ins, label, k=0):
            ins.then_inc(psum_drained[(RES[label] + k) % PS], 1)

        def gslot(label, k=0):
            s = (GN[label] + k) % GS
            return gring[:, s * GT:(s + 1) * GT]

        def g_arrived(eng, label, e=0, k=0):
            n = GN[label] + k
            eng.wait_ge(g_in[n % GS], landed[n] + 16 * (2 * FC // GS) * e)

        landed = []
        for n, label in enumerate(GN):
            landed.append((landed[n - GS] if n >= GS else 0) + (64 if label[0] in ("sk", "sv") else 16))

        def g_released(eng, label):
            kind = label[0]
            if kind == "pp":
                full(eng, ("pp", label[1], 4 * label[2] + 3))
            elif kind == "vt":
                full(eng, ("vt", 2))
            elif kind == "f":
                full(eng, ("f", label[1], label[2] // (2 * FC) * PER + label[2] % (2 * FC)))
            elif kind == "wk":
                full(eng, ("wss", label[1]))
            elif kind == "sk":
                full(eng, ("sss", label[1], label[2]))
            elif kind in ("wv", "sv"):
                p, b2 = label[1:3]
                eng.wait_ge(values_used, 10 * p + 5 * b2 + (1 if kind == "wv" else 2 + label[3]))
            else:
                full(eng, label)

        def update_of(kind, c):
            return [None, ("co", c), None, ("pp", 0, c), ("wo", c), None][kind]

        def h_updated(eng, kind, c):
            if kind == 0:
                return
            if kind in (2, 5):
                layer, last = (0, HALVES - 1) if kind == 2 else (1, EXPERTS - 1)
                drained(eng, ("f", layer, 0), last, 2 * FC + c)
            else:
                drained(eng, update_of(kind, c))

        block = ctx.enter_context(nc.Block())

        @block.sync
        def _(sp):
            def page(b, i):
                return sp.value_load(A["page_table"][0:1, b * PAGES + i:b * PAGES + i + 1], min_val=0, max_val=POOL - 1)

            sp.dma_start(wc[:, 0:64, :], A["w_cmp"][:, 0:64, :]).then_inc(wcmp_in, 16)
            for b in range(B):
                kb, vb = (2 * b) % 4, (2 * b + 1) % 4
                if b == 1:
                    full(sp, ("ts", 5))
                if b >= 2:
                    full(sp, ("cv", b - 2))
                for i in range(PAGES):
                    v = page(b, i)
                    src = A["cache_cmp"][:, bass.ds(v, 1), :, :].rearrange("c a p n -> c (a p) n")
                    sp.dma_start(cbufs[kb][:, i * 256:(i + 1) * 256], src[0, :, :]).then_inc(c_in[kb], 16)
                    sp.dma_start(cbufs[vb][:, i * 256:(i + 1) * 256], src[1, :, :]).then_inc(c_in[vb], 16)
                if b == 0:
                    sp.dma_start(wc[:, 64:128, :], A["w_cmp"][:, 64:128, :]).then_inc(wcmp_in, 16)
            full(sp, ("cv", B - 2))
            g_labels = list(GN)

            def g_load(label, src):
                n = GN[label]
                if n >= GS:
                    g_released(sp, g_labels[n - GS])
                sp.dma_start(gslot(label)[:, :], src).then_inc(g_in[n % GS], 16)

            def g_pages(label, b, first, pool):
                n = GN[label]
                g_released(sp, g_labels[n - GS])
                for i in range(4):
                    v = page(b, first + i)
                    sp.dma_start(gslot(label)[:, i * 256:(i + 1) * 256],
                                 pool[bass.ds(v, 1), :, :].rearrange("a p n -> (a p) n")).then_inc(g_in[n % GS], 16)

            for c in range(C):
                for i, name in enumerate(("gc", "v", "gb")):
                    g_load((name, c), A["conv_in"][3 * c + i])
            for c in range(C):
                g_load(("co", c), A["conv_out"][c])

            def expert_loads(layer, turns, gu, down):
                L = ("f", layer, 0)
                with sp.Fori(0, turns) as e:
                    for k in range(2 * FC):
                        full(sp, L, e, k - GS if k >= GS else k + GS - PER)
                        sp.dma_start(gslot(L, k)[:, :], gu[bass.ds(e, 1), k].rearrange("a p n -> (a p) n"))\
                          .then_inc(g_in[(GN[L] + k) % GS], 16)
                    for k in range(C):
                        n = LF[layer] + k
                        full(sp, L, e, 2 * FC + (k - DS if k >= DS else k + C - DS - PER))
                        sp.dma_start(dring[:, (n % DS) * DT:(n % DS + 1) * DT],
                                     down[bass.ds(e, 1), k].rearrange("a p n -> (a p) n")).then_inc(d_in[n % DS], 16)

            full(sp, ("css", 1))
            full(sp, ("co", C - 1))
            expert_loads(0, HALVES, A["dense_gu"], A["dense_down"])

            def ple_loads(layer):
                for i in range(2):
                    g_load(("pp", layer, i), A["ple_proj"][layer, i])
                    for k in range(4):
                        g_load(("pg", layer, 4 * i + k), A["ple_gate"][layer, 4 * i + k])

            ple_loads(0)
            for c in range(8):
                g_load(("kv", c), A["nsa_kv"][c])
            for i in range(4):
                g_load(("vt", i), A["nsa_vt"][i])
            for j in range(8):
                g_load(("q", j), A["nsa_q"][j])
            for p in range(4):
                for b2 in range(2):
                    g_load(("wk", p, b2), A["win_k"][2 * p + b2])
                for t in range(4):
                    for b2 in range(2):
                        g_pages(("sk", p, t, b2), 2 * p + b2, 4 * t, A["cache_selk"])
                for b2 in range(2):
                    g_load(("wv", p, b2), A["win_v"][2 * p + b2])
                    for t in range(4):
                        g_pages(("sv", p, b2, t), 2 * p + b2, 4 * t, A["cache_selv"])
            for c in range(C):
                g_load(("wo", c), A["nsa_out"][c])
            drained(sp, ("wo", C - 1))
            sp.wait_ge(rows_stored, 16 * 4)
            sp.dma_start(sel8[0:8, :], A["sel8"]).then_inc(sel8_in, 16)
            expert_loads(1, EXPERTS, A["moe_gu"], A["moe_down"])
            ple_loads(1)
            for c in range(C):
                drained(sp, ("pp", 1, c))
                sp.dma_start(O["h"][:, c, :], hT[:, c, :]).then_inc(stored, 16)
            sp.wait_ge(stored, 16 * C)
            sp.wait_ge(win_stored, 16 * B)

        @block.gpsimd
        def _(pool):
            pool.memset(lt[:, :], 0.0).then_inc(lt_clear, 1)
            pool.wait_ge(lt_clear, 1)
            for t in range(STEPS):
                for b2 in range(2):
                    dst = lt[32 * t:32 * t + 32, 64 * b2 + t:64 * b2 + 64:4]
                    pool.dma_start(dst, A["rel_bias"][:, :], allow_slow_non_contiguous=True).then_inc(lt_in, 16)
            drained(pool, ("co", 0))
            for b in range(B):
                n = (WIN - STEPS) * 512
                src = A["state_win"][b, STEPS:WIN, :].rearrange("s n -> (s n)").rearrange("(a n) -> a n", a=16)
                dst = O["win_old"][b].rearrange("s n -> (s n)").rearrange("(a n) -> a n", a=16)
                pool.dma_start(dst, src).then_inc(win_stored, 16)
            pool.wait_ge(conv_staged, 2)
            pool.dma_start(O["conv"][:, :], cstage[:, :]).then_inc(rows_stored, 16)
            for c4 in range(4):
                drained(pool, ("kv", c4))
            for c in range(2):
                for g in range(GROUPS):
                    for l2 in range(2):
                        pool.dma_start(kvp[64 * l2:64 * l2 + 64, 4 * c + g, 0:TP - l2],
                                       kvT[64 * (g % 2):64 * (g % 2) + 64, 2 * c + g // 2, l2:TP]).then_inc(kvp_in, 16)
            for c in range(4, 8):
                drained(pool, ("kv", c))
            pool.dma_start(O["kvT"][:, :, :], kvT[:, :, :]).then_inc(rows_stored, 16)
            for i in range(3):
                drained(pool, ("vt", i))
            pool.dma_start(O["vtok"][:, 0:2, :], vtok[:, 0:2, :]).then_inc(rows_stored, 16)
            pool.dma_start(O["vtok"][0:32, 2, :], vtok[0:32, 2, :]).then_inc(rows_stored, 16)
            drained(pool, ("gt",))
            for b in range(B):
                src = gtok[STEPS * b:STEPS * b + STEPS, 2, :].rearrange("t (r h) -> t r h", r=3)
                pool.dma_start(A["gscratch"][b].rearrange("h t r -> t r h"), src,
                               allow_slow_non_contiguous=True).then_inc(gates_out, 16)
            pool.wait_ge(gates_out, 16 * B)
            for p in range(4):
                src = A["gscratch"][2 * p:2 * p + 2].rearrange("b h t r -> (b h t) r")
                pool.dma_start(grow[:, p, :], src).then_inc(gates_in, 16)

        @block.scalar
        def _(act):
            step = [0]

            def chain(ins):
                step[0] += 1
                ins.then_inc(act_step, 1)

            loads = [(ohs[:, :], "ohs"), (masks[:, :], "masks"), (ohv, "ohv"), (rbx[0:BUCKETS, :], "rel_bias"), (ident[:, :], "ident"),
                     (ones[:, :], "ones"), (bones[:, :], "bones"), (bo32[:, :], "bo32"), (rsum[:, :], "rsum"),
                     (tri, "tri"), (pmask, "pmask"), (hT, "x"), (state, "state"),
                     (gains[:, :], "gains"), (convw[:, :], "convw"), (pT, "p"), (gq[:, :], "gq"), (gk[:, :], "gk"),
                     (wgate, "wgate"), (rout, "rout")]
            assert len(loads) == NCONST
            for dst, name in loads:
                act.dma_start(dst, A[name]).then_inc(consts_in, 16)

            act.wait_ge(eps_set, 1)

            def rstd(dst, src, label):
                full(act, label)
                drain(act.activation(dst, src, ACT.Ln, bias=epsc[:, :]), label)
                drained(act, label)
                act.activation(dst, dst, ACT.Exp, scale=-0.5).then_inc(rstd_ready, 1)

            def row_scale(m):
                if 2 <= m < 6:
                    act.wait_ge(kn_ready, 2 * (m - 1))
                elif m >= 6:
                    act.wait_ge(q_ready, m - 5)
                label = ("kss", m + 4) if m < 4 else ("qss", m - 4) if m < 12 else ("kcps",)
                n = T if m < 12 else 16
                rstd(rs[:, m % 2, 0:n], bank(label)[:, 0:n], label)

            for i in range(8):
                full(act, ("tp", i))
                drain(act.activation(tabP[:, :, 32 * i:32 * i + 32],
                                     bank(("tp", i))[:, :].rearrange("p (k h) -> p h k", h=16), ACT.Copy), ("tp", i))
            full(act, ("tc",))
            drain(act.activation(tabC, bank(("tc",))[:, 0:256].rearrange("p (i n h) -> p i n h", i=2, n=8), ACT.Copy), ("tc",))
            for i in range(4):
                full(act, ("ts", i))
                drain(act.activation(tS[:, 512 * i:512 * i + 512], bank(("ts", i))[:, :], ACT.Copy), ("ts", i))

            for b in range(B):
                full(act, ("ck", b))
                src = bank(("ck", b))[:, 0:128].rearrange("p (a n) -> p a n", a=2)
                chain(act.activation(kcn[:, :, NB * b:NB * b + NB], src, ACT.Copy))
                if b == 0:
                    full(act, ("ts", 5))
                    drained(act, ("ts", 4))
                    drained(act, ("ts", 5))
                drain(act.activation(kcsq[:, :, NB * b:NB * b + NB], src, ACT.Square), ("ck", b))
                full(act, ("cv", b))
                drain(act.activation(vraw[:, :, NB * b:NB * b + NB], bank(("cv", b))[:, 0:128].rearrange("p (a n) -> p a n", a=2),
                                     ACT.Copy), ("cv", b))
            for a in range(2):
                rstd(kcscale[a], bank(("css", a))[:, :], ("css", a))
            for p in range(4):
                full(act, ("ct", p))
                drain(act.activation(vcs[:, p, :], bank(("ct", p))[:, 0:256], ACT.Copy), ("ct", p))

            def norm_squares(i):
                for c in range(C):
                    h_updated(act, i, c)
                    if i == 0 and c == 0:
                        act.wait_ge(consts_in, 16 * NCONST)
                        full(act, ("css", 1))
                    act.activation(sqs[i][:, c, :], hT[:, c, :], ACT.Square).then_inc(sq_ready, 1)
                rstd(rs[:, 0, :], bank(("norm", i))[:, 0:T], ("norm", i))

            norm_squares(0)
            for c in range(C):
                full(act, ("gc", c))
                if c >= 2:
                    drained(act, ("v", c - 2))
                drain(act.activation(sg[:, c % 2, :], bank(("gc", c))[:, 0:T], ACT.Copy), ("gc", c))
            norm_squares(1)

            def expert_gates(layer, turns):
                with act.Fori(0, turns) as e:
                    for f in range(FC):
                        full(act, ("f", layer, 0), e, 2 * f)
                        drained(act, ("f", layer, 0), e, 2 * (f - 2) + 1 if f >= 2 else 2 * (f % 2 + FC - 2 + (FC % 2) * (1 - 2 * f)) + 1 - PER)
                        act.activation(sg[:, f % 2, :],
                                       bank(("f", layer, 0), 2 * f)[:, 0:T], ACT.Sigmoid).then_inc(sig_ready, 1)

            def ple_gates(layer):
                for c in range(C):
                    full(act, ("pg", layer, c))
                    if c >= 2:
                        drained(act, ("pp", layer, c - 2))
                    drain(act.activation(sg[:, c % 2, :], bank(("pg", layer, c))[:, 0:T], ACT.Sigmoid), ("pg", layer, c))

            expert_gates(0, HALVES)
            norm_squares(2)
            ple_gates(0)
            norm_squares(3)

            def square(label, n, half):
                if n >= 2:
                    full(act, half)
                chain_ready = act.activation(tmp[:, n % 2, :], bank(label)[:, 0:T], ACT.Square)
                chain_ready.then_inc(hsq_ready, 1)

            for c in range(8):
                full(act, ("kv", c))
                if c < 4:
                    drain(act.activation(kvT[:, c, :], bank(("kv", c))[:, 0:T], ACT.Copy), ("kv", c))
                else:
                    square(("kv", c), c - 4, ("kss", c - 2) if c >= 6 else None)
                    drain(act.activation(kvT[:, c, :], bank(("kv", c))[:, 0:T], ACT.Copy), ("kv", c))
                    if c > 4:
                        row_scale(c - 5)
            for i in range(3):
                n = 128 if i < 2 else 32
                full(act, ("vt", i))
                drain(act.activation(vtok[0:n, i, :], bank(("vt", i))[0:n, :], ACT.Copy), ("vt", i))
            row_scale(3)
            full(act, ("gt",))
            chain(act.activation(gtok[0:32, 2, :], bank(("gt",))[0:32, 96:144], ACT.Sigmoid))
            act.wait_ge(act_step, step[0])
            drain(act.activation(gtok[:, 0:2, :], bank(("gt",))[:, 0:96].rearrange("p (i n) -> p i n", i=2),
                                 ACT.Sigmoid), ("gt",))
            for j in range(8):
                full(act, ("q", j))
                square(("q", j), 4 + j, ("qss", j - 2) if j >= 2 else ("kss", 6 + j))
                drain(act.activation(qraw[:, j, :], bank(("q", j))[:, 0:T], ACT.Copy), ("q", j))
                if j:
                    row_scale(3 + j)
            full(act, ("kcp",))
            full(act, ("qss", 6))
            src = bank(("kcp",))[:, 0:16].rearrange("p (a n) -> p a n", a=2)
            act.activation(tmp_[:, 0:16].rearrange("p (a n) -> p a n", a=2), src, ACT.Square).then_inc(hsq_ready, 1)
            drain(act.activation(kcp, src, ACT.Copy), ("kcp",))
            row_scale(11)
            full(act, ("vcp",))
            drain(act.activation(vcp, bank(("vcp",))[0:8, 0:256], ACT.Copy), ("vcp",))

            row_scale(12)

            for u in range(17):
                if u < 16:
                    w = u % 2
                    for i in range(2):
                        nk = 128 * (i + 1)
                        act.wait_ge(pmax_ready, 3 * u + 1 + i)
                        o = 256 * i
                        for r in range(2):
                            ins = act.activation(Sp[:, w, o + r * nk:o + (r + 1) * nk], Sp[:, w, o + r * nk:o + (r + 1) * nk],
                                                 ACT.Exp, bias=nmp[:, w, i, r + 1:r + 2], accum_out=smp[:, w, i, r + 1:r + 2])
                            ins.then_inc(pexp_ready, 1)
                    act.wait_ge(pmax_ready, 3 * u + 3)
                    for i in range(2):
                        act.activation(Scp[:, w, i, :], Scp[:, w, i, :], ACT.Exp, bias=nmp[:, w, i, 0:1],
                                       accum_out=smp[:, w, i, 0:1]).then_inc(pexp_ready, 1)
                if u:
                    w = (u - 1) % 2
                    full(act, ("ptc", u - 1))
                    drain(act.activation(PTc[:, w, :], bank(("ptc", u - 1))[0:8, 0:256], ACT.Copy), ("ptc", u - 1))
                    for i in range(2):
                        full(act, ("ptp", u - 1, i))
                        n = 128 * (i + 1)
                        drain(act.activation(PTp[:, w, :, 128 * i:128 * i + n],
                                             bank(("ptp", u - 1, i))[:, 0:2 * n].rearrange("p (r n) -> p r n", r=2),
                                             ACT.Copy), ("ptp", u - 1, i))
            full(act, ("po", 15))

            def exps(p, r, view):
                act.wait_ge(smax_ready, 3 * p + 1 + {0: 0, 2: 1, 1: 2}[r])
                act.activation(view, view, ACT.Exp, bias=mxs[:, r:r + 1], accum_out=sms[:, r:r + 1]).then_inc(sexp_ready, 1)

            for p in range(4):
                def key_squares(label, n):
                    g_arrived(act, label)
                    if n % 2 == 0:
                        if p or n:
                            act.wait_ge(keys_used, 5 * p + n // 2)
                    elif n == 1:
                        if p:
                            full(act, ("sss", p - 1, 3))
                    else:
                        full(act, ("sss", p, (n - 5) // 2) if n > 3 else ("wss", p))
                    act.activation(ksq[:, n % 2, :], gslot(label)[:, :], ACT.Square).then_inc(ksq_ready, 1)

                before = [("wk", p, 0), ("wk", p, 1)] + [("sk", p, t, b2) for t in range(4) for b2 in range(2)]
                key_squares(before[0], 0)
                key_squares(before[1], 1)
                exps(p, 0, SC[:, :])

                def key_scale(i):
                    label = ("sss", p, i - 1) if i else ("wss", p)
                    if i > 1:
                        drained(act, ("sq", p, i - 3) if i > 2 else ("wq", p))
                    elif p:
                        drained(act, ("sq", p - 1, 2 + i))
                    rstd(rsb[(5 * p + i) % 2], bank(label)[:, :], label)

                key_scale(0)
                key_squares(before[2], 2)
                key_squares(before[3], 3)
                full(act, ("imp", p))
                ins = act.activation(SCg[:, :], bank(("imp", p))[:, 0:128], ACT.Copy)
                drain(ins, ("imp", p))
                exps(p, 2, SW[:, :])
                for t in range(4):
                    if t < 3:
                        key_squares(before[2 * t + 4], 2 * t + 4)
                    key_scale(t + 1)
                    if t < 3:
                        key_squares(before[2 * t + 5], 2 * t + 5)
                exps(p, 1, S[:, :])
                for i in range(6):
                    full(act, ("pt", p, i))
                    src = bank(("pt", p, i))
                    if i == 0:
                        ins = act.activation(PT[:, 0:4, :], src[:, :].rearrange("p (k m) -> p k m", k=4), ACT.Copy)
                    elif i == 1:
                        chain(act.activation(PT[:, 4, :], src[:, 0:128], ACT.Copy))
                        act.wait_ge(act_step, step[0])
                        ins = act.activation(PT[0:32, 5:7, :], src[0:32, 128:384].rearrange("p (k m) -> p k m", k=2), ACT.Copy)
                    else:
                        k = 7 + 4 * (i - 2)
                        ins = act.activation(PT[:, k:k + 4, :], src[:, :].rearrange("p (k m) -> p k m", k=4), ACT.Copy)
                    drain(ins, ("pt", p, i))

            norm_squares(4)
            act.wait_ge(rmax_ready, 1)
            for i in range(3):
                act.activation(rg[:, i, :], rl[:, i, :], ACT.Exp, bias=rmx[:, i:i + 1]).then_inc(rexp_ready, 1)
            for e in range(EXPERTS):
                full(act, ("gb8", e))
                drain(act.activation(gbc[:, e, :], bank(("gb8", e))[:, 0:T], ACT.Copy), ("gb8", e))
            expert_gates(1, EXPERTS)
            norm_squares(5)
            ple_gates(1)

        @block.vector
        def _(dve):
            step = [0]

            def chain(ins):
                step[0] += 1
                ins.then_inc(dve_step, 1)

            def settled():
                dve.wait_ge(dve_step, step[0])

            def scaled_by(label):
                dve.wait_ge(rstd_ready, RN[label] + 1)

            dve.memset(epsc[:, :], EPS).then_inc(eps_set, 1)
            dve.memset(rbx[BUCKETS:BUCKETS + 1, :], NEG).then_inc(rb_mask, 1)
            dve.wait_ge(consts_in, 16 * NCONST)
            full(dve, ("ts", 4))
            drain(dve.tensor_tensor(tW[:, :], bank(("ts", 4))[:, :], masks[:, 0:512], ALU.add), ("ts", 4))
            full(dve, ("ts", 5))
            chain(dve.tensor_tensor(tN, bank(("ts", 5))[:, 0:32].unsqueeze(1).to_broadcast([128, 4, 32]),
                                    masks[:, 512:640].rearrange("p (a k) -> p a k", a=4), ALU.add))
            drain(dve.tensor_tensor(tCs[:, :], bank(("ts", 5))[:, 32:160], masks[:, 640:768], ALU.add), ("ts", 5))
            chain(dve.tensor_scalar(gqs[:, :], gq[:, :], HD ** -0.5, None, ALU.mult))

            for a in range(2):
                scaled_by(("css", a))
                dve.scalar_tensor_tensor(kcn[:, a, :], kcn[:, a, :], gk[:, 0:1], kcscale[a], ALU.mult, ALU.mult).then_inc(kcn_ready, 1)

            def norm(i):
                scaled_by(("norm", i))
                for c in range(C):
                    dve.scalar_tensor_tensor(aT[:, c, :], hT[:, c, :], gains[:, C * i + c:C * i + c + 1], rs[:, 0, :],
                                             ALU.mult, ALU.mult).then_inc(a_ready, 1)

            norm(0)
            chain(dve.memset(uext[:, :, 0:2], 0.0))
            us = uext[:, :, 258:UE].rearrange("p c (b k) -> p c b k", b=B)
            for c in range(C):
                chain(dve.tensor_copy(us[:, c, :, 0:2], state[:, c, :, :]))
            for c in range(C):
                drained(dve, ("gc", c))
                full(dve, ("v", c))
                v = bank(("v", c))
                chain(dve.tensor_tensor(uext[:, c, 2:258], sg[:, c % 2, 0:TP], v[:, 0:TP], ALU.mult))
                drain(dve.tensor_tensor(us[:, c, :, 2:6], sg[:, c % 2, TP:T].rearrange("p (b k) -> p b k", b=B),
                                        v[:, TP:T].rearrange("p (b k) -> p b k", b=B), ALU.mult), ("v", c))
                settled()
                drained(dve, ("v", c))
                cw = [convw[:, C * k + c:C * k + c + 1] for k in range(3)]
                tp, tsm = tmp[:, c % 2, 0:TP], tmp[:, c % 2, TP:T].rearrange("p (b k) -> p b k", b=B)
                chain(dve.tensor_scalar(tp, uext[:, c, 0:256], cw[0], None, ALU.mult))
                chain(dve.tensor_scalar(tsm, us[:, c, :, 0:4], cw[0], None, ALU.mult))
                for k in (1, 2):
                    settled()
                    chain(dve.scalar_tensor_tensor(tp, uext[:, c, k:k + 256], cw[k], tp, ALU.mult, ALU.add))
                    chain(dve.scalar_tensor_tensor(tsm, us[:, c, :, k:k + 4], cw[k], tsm, ALU.mult, ALU.add))
                settled()
                full(dve, ("gb", c))
                drain(dve.tensor_tensor(zT[:, c, :], bank(("gb", c))[:, 0:T], tmp[:, c % 2, :], ALU.mult), ("gb", c))
            dve.tensor_copy(cstage[:, 0:16].rearrange("p (c k) -> p c k", c=C), uext[:, :, 256:258]).then_inc(conv_staged, 1)
            dve.tensor_copy(cstage[:, 16:144].rearrange("p (c b k) -> p c b k", c=C, b=B), us[:, :, :, 4:6]).then_inc(conv_staged, 1)

            def add_to_h(label, c, e=0, k=0):
                full(dve, label, e, k)
                drain(dve.tensor_tensor(hT[:, c, :], hT[:, c, :], bank(label, k)[:, 0:T], ALU.add), label, k)

            for c in range(C):
                add_to_h(("co", c), c)
            norm(1)

            def experts(layer, turns):
                with dve.Fori(0, turns) as e:
                    for f in range(FC):
                        gl, ul = 2 * f, 2 * f + 1
                        n0 = FC * HALVES * layer
                        L = ("f", layer, 0)
                        dve.wait_ge(sig_ready, n0 + f + 1 + FC * e)
                        s = sg[:, f % 2, :]
                        drain(dve.tensor_tensor(s, s, bank(L, gl)[:, 0:T], ALU.mult), L, gl)
                        drained(dve, L, e, gl)
                        full(dve, L, e, ul)
                        m = tmp[:, f % 2, :]
                        if layer == 0:
                            drain(dve.tensor_tensor(hff[:, f, :], s, bank(L, ul)[:, 0:T], ALU.mult), L, ul)
                        else:
                            drain(dve.tensor_tensor(m, s, bank(L, ul)[:, 0:T], ALU.mult), L, ul)
                            drained(dve, L, e, ul)
                            g = gbc[:, bass.ds(e, 1), :].rearrange("p a t -> p (a t)")
                            dve.tensor_tensor(hff[:, f, :], m, g, ALU.mult).then_inc(hff_ready, 1)
                    for c in range(C):
                        add_to_h(("f", layer, 0), c, e, 2 * FC + c)

            def ple(layer):
                for c in range(C):
                    drained(dve, ("pg", layer, c))
                    full(dve, ("pp", layer, c))
                    s = sg[:, c % 2, :]
                    chain(dve.tensor_tensor(s, s, bank(("pp", layer, c))[:, 0:T], ALU.mult))
                    settled()
                    drain(dve.tensor_tensor(hT[:, c, :], hT[:, c, :], s, ALU.add), ("pp", layer, c))

            experts(0, HALVES)
            norm(2)
            ple(0)
            norm(3)

            def key_norm(c):
                scaled_by(("kss", c))
                drained(dve, ("kv", c))
                br = 1 + (c - 4) // 2
                dve.scalar_tensor_tensor(kn[:, c - 4, 0:TP], kvT[:, c, 0:TP], gk[:, br:br + 1], rs[:, c % 2, 0:TP],
                                         ALU.mult, ALU.mult).then_inc(kn_ready, 1)
                dve.tensor_tensor(kn[:, c - 4, TP:T], kvT[:, c, TP:T], rs[:, c % 2, TP:T], ALU.mult).then_inc(kn_ready, 1)

            for c in range(4, 8):
                key_norm(c)
            for j in range(8):
                scaled_by(("qss", j))
                drained(dve, ("q", j))
                dve.scalar_tensor_tensor(q1[:, j, :], qraw[:, j, :], gqs[:, :], rs[:, j % 2, :], ALU.mult, ALU.mult).then_inc(q_ready, 1)
            chain(dve.memset(QB, 0.0))
            settled()
            dve.wait_ge(q_ready, 8)
            for r in range(3):
                for a in range(2):
                    for g2 in range(2):
                        h = slice(64 * g2, 64 * g2 + 64)
                        dst = QB[h, r, :, a, 16 * g2:16 * g2 + 16].rearrange("p b (r t) -> p b r t", r=R)
                        src = q1[h, 4 * a:4 * a + 4, TP:T].rearrange("p r (b t) -> p b r t", b=B)
                        if r:
                            ins = dve.tensor_scalar(dst, src, gk[h, r:r + 1], None, ALU.mult)
                        else:
                            ins = dve.tensor_copy(dst, src)
                        ins.then_inc(qb_ready, 1)
            scaled_by(("kcps",))
            drained(dve, ("kcp",))
            dve.scalar_tensor_tensor(kcpn, kcp, gk[:, 0:1], rs[:, 0, 0:16].rearrange("p (a n) -> p a n", a=2),
                                     ALU.mult, ALU.mult).then_inc(kcn_ready, 1)
            drained(dve, ("gt",))

            def prompt_scores(u):
                w, j, g2 = u % 2, u // 2, u % 2
                head = (2 * (j // 4) + g2) * R + j % 4
                if u >= 2:
                    full(dve, ("ptp", u - 2, 1))
                for i in range(2):
                    nk = 128 * (i + 1)
                    full(dve, ("pl", u, i))
                    s = Sp[:, w, 256 * i:256 * i + 2 * nk].rearrange("p (r k) -> p r k", r=2)
                    drain(dve.tensor_tensor(s, bank(("pl", u, i))[:, 0:2 * nk].rearrange("p (r k) -> p r k", r=2),
                                            tabP[:, head, 256 - nk:256].unsqueeze(1).to_broadcast([128, 2, nk]), ALU.add),
                          ("pl", u, i))
                    drained(dve, ("pl", u, i))
                    chain(dve.tensor_reduce(nmp[:, w, i, 1:3], s, AX.X, ALU.max))
                    settled()
                    dve.tensor_scalar(nmp[:, w, i, 1:3], nmp[:, w, i, 1:3], -1.0, None, ALU.mult).then_inc(pmax_ready, 1)
                drain_bias = tabC[:, :, :, head]
                full(dve, ("pc", u))
                drain(dve.tensor_tensor(Scp[:, w, :, :], bank(("pc", u))[:, 0:16].rearrange("p (i n) -> p i n", i=2),
                                        drain_bias, ALU.add), ("pc", u))
                drained(dve, ("pc", u))
                chain(dve.tensor_reduce(nmp[:, w, :, 0], Scp[:, w, :, :], AX.X, ALU.max))
                settled()
                dve.tensor_scalar(nmp[:, w, :, 0], nmp[:, w, :, 0], -1.0, None, ALU.mult).then_inc(pmax_ready, 1)

            def prompt_scale(u):
                w, j, g2 = u % 2, u // 2, u % 2
                head = (2 * (j // 4) + g2) * R + j % 4
                dve.wait_ge(pexp_ready, 6 * (u + 1))
                chain(dve.reciprocal(scp[:, w], smp[:, w]))
                chain(dve.tensor_tensor(Scp[:, w], Scp[:, w], pmask, ALU.mult))
                settled()
                gates = gtok[:, 0:2, head:48:16]
                chain(dve.tensor_tensor(scp[:, w], scp[:, w], gates, ALU.mult))
                settled()
                for i in range(2):
                    nk = 128 * (i + 1)
                    for r in range(2):
                        o = 256 * i + r * nk
                        dve.tensor_scalar(Sp[:, w, o:o + nk], Sp[:, w, o:o + nk], scp[:, w, i, r + 1:r + 2], None,
                                          ALU.mult).then_inc(pscaled, 1)
                    dve.tensor_scalar(Scp[:, w, i, :], Scp[:, w, i, :], scp[:, w, i, 0:1], None,
                                      ALU.mult).then_inc(pscaled, 1)

            def prompt_out(u):
                j, g2 = u // 2, u % 2
                h = slice(64 * g2, 64 * g2 + 64)
                full(dve, ("po", u))
                drain(dve.tensor_copy(oT[h, j, 0:TP], bank(("po", u))[h, 0:TP]), ("po", u))

            for u in range(18):
                if u < 16:
                    prompt_scores(u)
                if 1 <= u <= 16:
                    prompt_scale(u - 1)
                if u >= 2:
                    prompt_out(u - 2)

            dve.wait_ge(gates_in, 16 * 4)
            for p in range(4):
                def soft(r, view, count):
                    chain(dve.tensor_reduce(mxs[:, r:r + 1], view, AX.X, ALU.max))
                    settled()
                    dve.tensor_scalar(mxs[:, r:r + 1], mxs[:, r:r + 1], -1.0, None, ALU.mult).then_inc(smax_ready, 1)

                def recip(r, count):
                    dve.wait_ge(sexp_ready, 3 * p + count)
                    chain(dve.reciprocal(fac[:, r:r + 1], sms[:, r:r + 1]))
                    settled()

                def gate(r):
                    chain(dve.tensor_tensor(fac[:, r:r + 1], fac[:, r:r + 1], grow[:, p, r:r + 1], ALU.mult))
                    settled()

                if p:
                    full(dve, ("pt", p - 1, 5))
                full(dve, ("sc", p))
                drain(dve.tensor_tensor(SC[:, :], bank(("sc", p))[:, 0:128], tCs[:, :], ALU.add), ("sc", p))
                drained(dve, ("sc", p))
                soft(0, SC[:, :], 1)
                full(dve, ("sn", p))
                sn = bank(("sn", p))
                chain(dve.tensor_tensor(S[:, KEYS:KEYS + 32], sn[:, 0:32], tN[:, p, :], ALU.add))
                drain(dve.tensor_tensor(SW[:, WIN:WIN + 32], sn[:, 32:64], tN[:, p, :], ALU.add), ("sn", p))
                recip(0, 1)
                dve.tensor_scalar(SC[:, :], SC[:, :], fac[:, 0:1], None, ALU.mult).then_inc(cprob_ready, 1)
                scaled_by(("wss", p))
                full(dve, ("wq", p))
                drain(dve.tensor_tensor(SW[:, 0:WIN], bank(("wq", p))[:, :], rsb[5 * p % 2], ALU.mult), ("wq", p))
                drained(dve, ("wq", p))
                chain(dve.tensor_tensor(SW[:, 0:WIN], SW[:, 0:WIN], tW[:, :], ALU.add))
                settled()
                drained(dve, ("sn", p))
                drained(dve, ("imp", p))
                chain(dve.tensor_tensor(half[:, :], SCg[:, 0:64], SCg[:, 64:128], ALU.add))
                settled()
                hv = half[:, :].rearrange("p (k m) -> p k m", m=2)
                chain(dve.tensor_tensor(score[:, :], hv[:, :, 0], hv[:, :, 1], ALU.add))
                settled()
                chain(dve.memset(score[:, 0:1], 1e4))
                chain(dve.memset(score[:, 31:32], 1e4))
                settled()
                soft(2, SW[:, :], 2)
                other = score[:, :].unsqueeze(1).to_broadcast([128, 32, 32])
                own = score[:, :].unsqueeze(2).to_broadcast([128, 32, 32])
                chain(dve.tensor_tensor(cnt1, other, own, ALU.is_gt))
                chain(dve.tensor_tensor(cnt2, other, own, ALU.is_equal))
                settled()
                chain(dve.tensor_tensor(cnt2, cnt2, tri, ALU.mult))
                settled()
                chain(dve.tensor_tensor(cnt1, cnt1, cnt2, ALU.add))
                settled()
                chain(dve.tensor_reduce(rank[:, :], cnt1, AX.X, ALU.add))
                settled()
                chain(dve.tensor_scalar(blkm[:, :], rank[:, :], 14.5, NEG, ALU.is_gt, ALU.mult))
                dve.tensor_scalar(SCg[:, :], SC[:, :], grow[:, p, 0:1], None, ALU.mult).then_inc(sscaled, 1)
                for t in range(4):
                    scaled_by(("sss", p, t))
                    full(dve, ("sq", p, t))
                    st = S[:, 512 * t:512 * t + 512]
                    drain(dve.tensor_tensor(st, bank(("sq", p, t))[:, :], rsb[(5 * p + 1 + t) % 2], ALU.mult), ("sq", p, t))
                    drained(dve, ("sq", p, t))
                    chain(dve.tensor_tensor(st, st, tS[:, 512 * t:512 * t + 512], ALU.add))
                    settled()
                    sv = st.rearrange("p (k m) -> p k m", k=8)
                    chain(dve.tensor_tensor(sv, sv, blkm[:, 8 * t:8 * t + 8].unsqueeze(2).to_broadcast([128, 8, 64]), ALU.add))
                settled()
                soft(1, S[:, :], 3)
                recip(2, 2)
                gate(2)
                dve.tensor_scalar(SW[:, :], SW[:, :], fac[:, 2:3], None, ALU.mult).then_inc(sscaled, 1)
                recip(1, 3)
                gate(1)
                dve.tensor_scalar(S[:, :], S[:, :], fac[:, 1:2], None, ALU.mult).then_inc(sscaled, 1)
            dve.wait_ge(values_used, 40)
            for a in range(2):
                for g2 in range(2):
                    h = slice(64 * g2, 64 * g2 + 64)
                    src = oP[a][h, 0:32 * B].rearrange("p (b g r t) -> p g b r t", b=B, g=2, r=R)[:, g2]
                    dst = oT[h, 4 * a:4 * a + 4, TP:T].rearrange("p r (b t) -> p b r t", b=B)
                    dve.tensor_copy(dst, src).then_inc(so_ready, 1)
            for c in range(C):
                add_to_h(("wo", c), c)
            norm(4)

            chain(dve.memset(rl, 0.0))
            settled()
            full(dve, ("rt",))
            chain(dve.tensor_copy(rl[:, 0:2, :], bank(("rt",))[:, 0:16].rearrange("p (i e) -> p i e", i=2)))
            drain(dve.tensor_copy(rl[0:32, 2, :], bank(("rt",))[0:32, 16:24]), ("rt",))
            settled()
            drained(dve, ("rt",))
            chain(dve.tensor_reduce(rmx[:, :], rl, AX.X, ALU.max))
            settled()
            dve.tensor_scalar(rmx[:, :], rmx[:, :], -1.0, None, ALU.mult).then_inc(rmax_ready, 1)
            for i in range(3):
                other = rl[:, i, :].unsqueeze(1).to_broadcast([128, 8, 8])
                own = rl[:, i, :].unsqueeze(2).to_broadcast([128, 8, 8])
                chain(dve.tensor_tensor(cmp8[0], other, own, ALU.is_gt))
                chain(dve.tensor_tensor(cmp8[1], other, own, ALU.is_equal))
                settled()
                chain(dve.tensor_tensor(cmp8[1], cmp8[1], tri[:, 0:8, 0:8], ALU.mult))
                settled()
                chain(dve.tensor_tensor(cmp8[0], cmp8[0], cmp8[1], ALU.add))
                settled()
                chain(dve.tensor_reduce(rk[:, i, :], cmp8[0], AX.X, ALU.add))
                settled()
            dve.wait_ge(rexp_ready, 3)
            chain(dve.scalar_tensor_tensor(rg, rk, 1.5, rg, ALU.is_lt, ALU.mult))
            settled()
            chain(dve.tensor_reduce(rsm[:, :], rg, AX.X, ALU.add))
            settled()
            chain(dve.reciprocal(rsm[:, :], rsm[:, :]))
            settled()
            dve.tensor_tensor(rg, rg, rsm[:, :].unsqueeze(2).to_broadcast([128, 3, 8]), ALU.mult).then_inc(rg_ready, 1)
            full(dve, ("gT",))
            drain(dve.tensor_copy(gT, bank(("gT",))[0:8, 0:T]), ("gT",))
            full(dve, ("gb8", 7))
            experts(1, EXPERTS)
            norm(5)
            ple(1)

        @block.tensor
        def _(pe):
            def g_linear(label, rhs, e=0, k=0, ready=None):
                g_arrived(pe, label, e, k)
                bank_free(pe, label, e, k)
                tile = gslot(label, k)
                for i in range(C):
                    if ready is not None:
                        pe.wait_ge(a_ready, ready + i + 1)
                    ins = pe.matmul(bank(label, k)[:, 0:T], tile[:, 128 * i:128 * i + 128], rhs[:, i, :],
                                    start=i == 0, stop=i == C - 1)
                fill(ins, label, k)

            def norm(i):
                label = ("norm", i)
                bank_free(pe, label)
                for c in range(C):
                    pe.wait_ge(sq_ready, C * i + c + 1)
                    ins = pe.matmul(bank(label)[:, 0:T], ones[:, :], sqs[i][:, c, :], start=c == 0, stop=c == C - 1)
                fill(ins, label)

            pe.wait_ge(consts_in, 16 * NCONST)
            pe.wait_ge(rb_mask, 1)
            for i in range(8):
                bank_free(pe, ("tp", i))
                for k in range(32):
                    y = 383 - (32 * i + k)
                    ins = pe.matmul(bank(("tp", i))[:, 16 * k:16 * k + 16], ohv[:, y:y + 128], rbx, start=True, stop=True)
                fill(ins, ("tp", i))
            bank_free(pe, ("tc",))
            for i in range(2):
                for n in range(8):
                    y = 128 * i - 32 * n - 31 + 255
                    ins = pe.matmul(bank(("tc",))[:, 16 * (8 * i + n):16 * (8 * i + n) + 16], ohv[:, y:y + 128], rbx,
                                    start=True, stop=True)
            fill(ins, ("tc",))
            pe.wait_ge(lt_in, 16 * 8)
            for i in range(6):
                n = 512 if i < 5 else 160
                bank_free(pe, ("ts", i))
                fill(pe.matmul(bank(("ts", i))[:, 0:n], lt, ohs[:, 512 * i:512 * i + n], start=True, stop=True), ("ts", i))

            pe.wait_ge(wcmp_in, 32)
            for b in range(B):
                kb, vb = (2 * b) % 4, (2 * b + 1) % 4
                pe.wait_ge(c_in[kb], 16 * PAGES * (b // 2 + 1))
                bank_free(pe, ("ck", b))
                src = cbufs[kb].rearrange("p (i g l n) -> p i g l n", i=PAGES, g=GROUPS, l=16)
                for g in range(GROUPS):
                    h, a = 64 * (g % 2), g // 2
                    for l in range(16):
                        ins = pe.matmul(bank(("ck", b))[h:h + 64, NB * a:NB * a + NB], wc[:, 16 * g + l, :], src[:, :, g, l, :],
                                        start=l == 0, stop=l == 15)
                fill(ins, ("ck", b))
                pe.wait_ge(c_in[vb], 16 * PAGES * (b // 2 + 1))
                bank_free(pe, ("cv", b))
                src = cbufs[vb].rearrange("p (i g l n) -> p i g l n", i=PAGES, g=GROUPS, l=16)
                for g in range(GROUPS):
                    h, a = 64 * (g % 2), g // 2
                    for l in range(16):
                        ins = pe.matmul(bank(("cv", b))[h:h + 64, NB * a:NB * a + NB], wc[:, 64 + 16 * g + l, :],
                                        src[:, :, g, l, :], start=l == 0, stop=l == 15)
                fill(ins, ("cv", b))
            for a in range(2):
                bank_free(pe, ("css", a))
                drained(pe, ("ck", 7))
                fill(pe.matmul(bank(("css", a))[:, :], bones[:, :], kcsq[:, a, :], start=True, stop=True), ("css", a))

            drained(pe, ("cv", 6))
            drained(pe, ("cv", 7))
            for p in range(4):
                bank_free(pe, ("ct", p))
                for a in range(2):
                    ins = pe.transpose(bank(("ct", p))[:, 128 * a:128 * a + 128], vraw[:, a, 128 * p:128 * p + 128], ident[:, :])
                fill(ins, ("ct", p))

            norm(0)
            for c in range(C):
                for name in ("gc", "v", "gb"):
                    g_linear((name, c), aT, ready=0 if c == 0 and name == "gc" else None)
            for c in range(C):
                if c == 0:
                    for k in range(C):
                        drained(pe, ("gb", k))
                g_linear(("co", c), zT)
            norm(1)

            def experts(layer, turns, ready):
                pe.wait_ge(a_ready, ready)
                with pe.Fori(0, turns) as e:
                    L = ("f", layer, 0)
                    for k in range(2 * FC):
                        g_linear(L, aT, e, k)
                    for c in range(C):
                        n = LF[layer] + c
                        pe.wait_ge(d_in[n % DS], 16 * (n // DS + 1) + 16 * (C // DS) * e)
                        tile = dring[:, (n % DS) * DT:(n % DS + 1) * DT]
                        bank_free(pe, L, e, 2 * FC + c)
                        for f in range(FC):
                            if c == 0:
                                if layer:
                                    pe.wait_ge(hff_ready, f + 1 + FC * e)
                                else:
                                    drained(pe, L, e, 2 * f + 1)
                            ins = pe.matmul(bank(L, 2 * FC + c)[:, 0:T], tile[:, 128 * f:128 * f + 128], hff[:, f, :],
                                            start=f == 0, stop=f == FC - 1)
                        fill(ins, L, 2 * FC + c)

            def ple(layer, ready):
                for c in range(C):
                    g_arrived(pe, ("pp", layer, c // 4))
                    g_linear(("pg", layer, c), aT, ready=ready if c == 0 else None)
                    bank_free(pe, ("pp", layer, c))
                    tile = gslot(("pp", layer, c // 4))
                    for k in range(2):
                        o = (2 * (c % 4) + k) * 128
                        ins = pe.matmul(bank(("pp", layer, c))[:, 0:T], tile[:, o:o + 128], pT[:, layer, k, :],
                                        start=k == 0, stop=k == 1)
                    fill(ins, ("pp", layer, c))

            experts(0, HALVES, 2 * C)
            norm(2)
            ple(0, 2 * C)
            norm(3)

            def block_sums(label, n):
                bank_free(pe, label)
                pe.wait_ge(hsq_ready, n + 1)
                fill(pe.matmul(bank(label)[:, 0:T], bones[:, :], tmp[:, n % 2, :], start=True, stop=True), label)

            for c in range(8):
                g_linear(("kv", c), aT, ready=3 * C if c == 0 else None)
                if c > 4:
                    block_sums(("kss", c - 1), c - 5)
            for i in range(3):
                bank_free(pe, ("vt", i))
            for q in range(4):
                g_arrived(pe, ("vt", q))
                tile = gslot(("vt", q))
                for k in range(2):
                    for i in range(3):
                        n = 128 if i < 2 else 32
                        ins = pe.matmul(bank(("vt", i))[0:n, :], aT[:, 2 * q + k, 128 * i:128 * i + n],
                                        tile[:, 512 * k:512 * k + 512], start=q == 0 and k == 0, stop=q == 3 and k == 1)
                        if q == 3 and k == 1:
                            fill(ins, ("vt", i))
            block_sums(("kss", 7), 3)
            bank_free(pe, ("gt",))
            for i in range(3):
                n = 128 if i < 2 else 32
                for c in range(C):
                    ins = pe.matmul(bank(("gt",))[0:n, 48 * i:48 * i + 48], aT[:, c, 128 * i:128 * i + n], wgate[:, c, :],
                                    start=c == 0, stop=c == C - 1)
            fill(ins, ("gt",))
            for j in range(8):
                g_linear(("q", j), aT)
                if j:
                    block_sums(("qss", j - 1), 4 + j - 1)
            pe.wait_ge(kvp_in, 16 * 16)
            bank_free(pe, ("kcp",))
            for g in range(GROUPS):
                h, a = 64 * (g % 2), g // 2
                for l in range(16):
                    ins = pe.matmul(bank(("kcp",))[h:h + 64, 8 * a:8 * a + 8], wc[:, 16 * g + l, :], kvp[:, g, 2 * l:TP:32],
                                    start=l == 0, stop=l == 15)
            fill(ins, ("kcp",))
            block_sums(("qss", 7), 11)
            bank_free(pe, ("vcp",))
            for g in range(GROUPS):
                for l in range(16):
                    ins = pe.matmul(bank(("vcp",))[0:8, 64 * g:64 * g + 64], kvp[:, 4 + g, 2 * l:TP:32], wc[:, 64 + 16 * g + l, :],
                                    start=l == 0, stop=l == 15)
            fill(ins, ("vcp",))
            bank_free(pe, ("kcps",))
            pe.wait_ge(hsq_ready, 13)
            fill(pe.matmul(bank(("kcps",))[:, 0:16], bones[:, :], tmp_[:, 0:16], start=True, stop=True), ("kcps",))

            pe.wait_ge(kn_ready, 8)
            pe.wait_ge(q_ready, 8)
            pe.wait_ge(kcn_ready, 3)
            for u in range(17):
                if u < 16:
                    j, g2 = u // 2, u % 2
                    a = j // 4
                    h = slice(64 * g2, 64 * g2 + 64)
                    bank_free(pe, ("pc", u))
                    for i in range(2):
                        ins = pe.matmul(bank(("pc", u))[:, 8 * i:8 * i + 8], q1[h, j, 128 * i:128 * i + 128], kcpn[h, a, :],
                                        start=True, stop=True)
                    fill(ins, ("pc", u))
                    for i in range(2):
                        nk = 128 * (i + 1)
                        bank_free(pe, ("pl", u, i))
                        for r in range(2):
                            ins = pe.matmul(bank(("pl", u, i))[:, r * nk:(r + 1) * nk], q1[h, j, 128 * i:128 * i + 128],
                                            kn[h, 2 * r + a, 0:nk], start=True, stop=True)
                        fill(ins, ("pl", u, i))
                if u:
                    v = u - 1
                    w, j, g2 = v % 2, v // 2, v % 2
                    g = 2 * (j // 4) + g2
                    pe.wait_ge(pscaled, 6 * (v + 1))
                    bank_free(pe, ("ptc", v))
                    for i in range(2):
                        ins = pe.transpose(bank(("ptc", v))[0:8, 128 * i:128 * i + 128], Scp[:, w, i, :], ident[:, :])
                    fill(ins, ("ptc", v))
                    for i in range(2):
                        bank_free(pe, ("ptp", v, i))
                        for k in range(2 * (i + 1)):
                            ins = pe.transpose(bank(("ptp", v, i))[:, 128 * k:128 * k + 128],
                                               Sp[:, w, 256 * i + 128 * k:256 * i + 128 * k + 128], ident[:, :])
                        fill(ins, ("ptp", v, i))
                    bank_free(pe, ("po", v))
                    drained(pe, ("ptc", v))
                    drained(pe, ("ptp", v, 0))
                    drained(pe, ("ptp", v, 1))
                    drained(pe, ("vcp",))
                    o = bank(("po", v))
                    h = slice(64 * g2, 64 * g2 + 64)
                    for r in range(2):
                        pe.matmul(o[h, 0:256], vtok[:, 0, 256 * r + 64 * g:256 * r + 64 * g + 64], PTp[:, w, r, 0:256],
                                  start=r == 0, stop=False)
                        pe.matmul(o[h, 128:256], vtok[:, 1, 256 * r + 64 * g:256 * r + 64 * g + 64], PTp[:, w, r, 256:384],
                                  start=False, stop=False)
                    fill(pe.matmul(o[h, 0:256], vcp[:, 64 * g:64 * g + 64], PTc[:, w, :], start=False, stop=True), ("po", v))

            pe.wait_ge(qb_ready, 12)
            for p in range(4):
                def rows(b2, a):
                    return slice(64 * b2 + 32 * a, 64 * b2 + 32 * a + 32)

                bank_free(pe, ("sc", p))
                for b2 in range(2):
                    for a in range(2):
                        ins = pe.matmul(bank(("sc", p))[rows(b2, a), 0:128], QB[:, 0, 2 * p + b2, a, :],
                                        kcn[:, a, 128 * p:128 * p + 128], start=True, stop=True)
                fill(ins, ("sc", p))
                bank_free(pe, ("sn", p))
                for b2 in range(2):
                    for a in range(2):
                        for r in range(2):
                            ins = pe.matmul(bank(("sn", p))[rows(b2, a), 32 * r:32 * r + 32], QB[:, 1 + r, 2 * p + b2, a, :],
                                            kn[:, 2 * r + a, TP:T], start=True, stop=True)
                fill(ins, ("sn", p))

                def key_tile(q, s, tile, n, b2, r, view, last):
                    pe.wait_ge(ksq_ready, 10 * p + n + 1)
                    g_arrived(pe, tile)
                    for a in range(2):
                        i1 = pe.matmul(bank(q)[rows(b2, a), :], QB[:, r, 2 * p + b2, a, :], view(gslot(tile), a),
                                       start=True, stop=True)
                        i2 = pe.matmul(bank(s)[rows(b2, a), :], bo32[:, :], view(ksq[:, n % 2, :], a), start=True, stop=True)
                        if a == 0:
                            continue
                        if last:
                            fill(i1, q)
                            fill(i2, s)
                        else:
                            i2.then_inc(keys_used, 1)

                def win_view(t, a):
                    return t[:, 512 * a:512 * a + 512]

                def page_view(t, a):
                    return t.rearrange("p (i a n) -> p i a n", i=4, a=2)[:, :, a, :]

                bank_free(pe, ("wq", p))
                bank_free(pe, ("wss", p))
                for b2 in range(2):
                    key_tile(("wq", p), ("wss", p), ("wk", p, b2), b2, b2, 2, win_view, b2 == 1)
                bank_free(pe, ("imp", p))
                pe.wait_ge(cprob_ready, p + 1)
                fill(pe.matmul(bank(("imp", p))[:, 0:128], rsum[:, :], SC[:, :], start=True, stop=True), ("imp", p))
                for t in range(4):
                    bank_free(pe, ("sq", p, t))
                    bank_free(pe, ("sss", p, t))
                    for b2 in range(2):
                        key_tile(("sq", p, t), ("sss", p, t), ("sk", p, t, b2), 2 + 2 * t + b2, b2, 1, page_view, b2 == 1)
                pe.wait_ge(sscaled, 3 * p + 2)
                for i in range(6):
                    if i == 1:
                        pe.wait_ge(sscaled, 3 * p + 3)
                    bank_free(pe, ("pt", p, i))
                    o = bank(("pt", p, i))
                    if i == 0:
                        parts = [(0, SCg[:, :])] + [(128 * (k + 1), SW[:, 128 * k:128 * k + 128]) for k in range(3)]
                    elif i == 1:
                        parts = [(0, SW[:, 384:512]), (128, SW[:, 512:544]), (256, S[:, KEYS:KEYS + 32])]
                    else:
                        parts = [(128 * k, S[:, 512 * (i - 2) + 128 * k:512 * (i - 2) + 128 * k + 128]) for k in range(4)]
                    for col, src in parts:
                        n = src.shape[1]
                        ins = pe.transpose(o[0:n, col:col + 128], src, ident[:, :])
                    fill(ins, ("pt", p, i))
                for i in range(6):
                    drained(pe, ("pt", p, i))

                for b2 in range(2):
                    b = 2 * p + b2

                    def values(k, v, first=False, last=False, parts=128):
                        for a in range(2):
                            ins = pe.matmul(oP[a][:, 32 * b:32 * b + 32], v[0:parts, 128 * a:128 * a + 128],
                                            PT[0:parts, k, rows(b2, a)], start=first, stop=last)
                        return ins

                    values(0, vcs[:, p, :], first=True)
                    values(5, vtok[:, 2, 256:512], parts=32)
                    values(6, vtok[:, 2, 0:256], parts=32)
                    g_arrived(pe, ("wv", p, b2))
                    for k in range(4):
                        ins = values(1 + k, gslot(("wv", p, b2))[:, 256 * k:256 * k + 256])
                    ins.then_inc(values_used, 1)
                    for t in range(4):
                        g_arrived(pe, ("sv", p, b2, t))
                        for k in range(4):
                            ins = values(7 + 4 * t + k, gslot(("sv", p, b2, t))[:, 256 * k:256 * k + 256], last=t == 3 and k == 3)
                        ins.then_inc(values_used, 1)

            pe.wait_ge(so_ready, 4)
            drained(pe, ("po", 15))
            for c in range(C):
                g_linear(("wo", c), oT)
            norm(4)
            bank_free(pe, ("rt",))
            pe.wait_ge(a_ready, 5 * C)
            for i in range(3):
                n = 128 if i < 2 else 32
                for c in range(C):
                    ins = pe.matmul(bank(("rt",))[0:n, 8 * i:8 * i + 8], aT[:, c, 128 * i:128 * i + n], rout[:, c, :],
                                    start=c == 0, stop=c == C - 1)
            fill(ins, ("rt",))
            bank_free(pe, ("gT",))
            pe.wait_ge(rg_ready, 1)
            for i in range(3):
                n = 128 if i < 2 else 32
                ins = pe.transpose(bank(("gT",))[0:8, 128 * i:128 * i + n], rg[0:n, i, :], ident[0:n, 0:n])
            fill(ins, ("gT",))
            drained(pe, ("gT",))
            pe.wait_ge(sel8_in, 16)
            for e in range(EXPERTS):
                bank_free(pe, ("gb8", e))
                fill(pe.matmul(bank(("gb8", e))[:, 0:T], sel8[0:8, 128 * e:128 * e + 128], gT, start=True, stop=True), ("gb8", e))
            drained(pe, ("gb8", 7))
            experts(1, EXPERTS, 5 * C)
            norm(5)
            ple(1, 5 * C)


def constants():
    f = np.float32
    eye = np.eye(128, dtype=f)
    k = {"ident": eye, "ones": np.full((128, 128), 1.0 / D, f)}
    half = np.arange(128) // 64
    k["bones"] = (half[:, None] == half[None, :]).astype(f) / f(HD)
    k["bo32"] = (half[:, None] == (np.arange(32) // 16)[None, :]).astype(f) / f(HD)
    row = np.arange(128)
    b2, head, step = row // 64, row // 4 % 16, row % 4
    key = (b2 * 4 + head // R) * 4 + step
    k["rsum"] = (key[:, None] == key[None, :]).astype(f)
    i = np.arange(32)
    k["tri"] = np.ascontiguousarray(np.broadcast_to((i[None, :] < i[:, None]).astype(f), (128, 32, 32)))
    q = np.arange(256).reshape(2, 128).T
    k["pmask"] = (q[:, :, None] >= np.arange(8) * 32 + 31).astype(f)
    k["sel8"] = np.repeat(np.eye(8, dtype=f), 128, axis=1)
    dist = np.arange(OHL) - 255
    oh = np.zeros((BUCKETS + 1, OHL), f)
    oh[np.where(dist < 0, BUCKETS, bucket(dist)), np.arange(OHL)] = 1
    k["ohv"] = oh
    t = np.arange(STEPS)[:, None]
    new = np.tile(np.arange(STEPS), B)
    ends = np.tile((np.arange(NB) + 1) * 32 - 1, 2)
    rel = np.concatenate([KEYS + t - np.arange(KEYS), KEYS + t - (KEYS - WIN + np.arange(WIN)),
                          np.maximum(t - new, 0), KEYS + t - ends], axis=1)
    k["ohs"] = (bucket(rel)[:, None, :] == np.arange(BUCKETS)[None, :, None]).astype(f).reshape(128, -1)
    m = np.zeros((128, 768), bool)
    m[:, 0:WIN] = WIN + step[:, None] - np.arange(WIN) < WIN
    tok = np.arange(32)
    for p in range(4):
        m[:, WIN + 32 * p:WIN + 32 * p + 32] = (tok // 4 == 2 * p + b2[:, None]) & (tok % 4 <= step[:, None])
    m[:, 640:768] = np.arange(128) // NB == b2[:, None]
    k["masks"] = np.where(m, f(0), f(NEG))
    return k


def kernel(x_prompt, x_sample, state_conv, cache_cmp, cache_sel, state_win, page_table, p_prompt, p_sample, norm_mix,
           norm_ffn, norm_ple, conv_w_in, conv_w, conv_w_out, nsa_w_in, nsa_w_cmp, nsa_q_norm, nsa_k_norm, nsa_w_out,
           rel_bias, ffn_w_gate, ffn_w_up, ffn_w_down, moe_router, moe_w_gate, moe_w_up, moe_w_down, ple_w_proj, ple_w_gate):
    import concourse.bacc as bacc
    from concourse.bass_utils import run_bass_kernel_spmd

    def chunks(w):
        w = np.asarray(w)
        return w.reshape(w.shape[0] // 128, 128, w.shape[1] // 128, 128).transpose(2, 1, 0, 3).reshape(w.shape[1] // 128, 128, -1)

    def features(a):
        a = np.asarray(a)
        return a.reshape(a.shape[0], -1, 128).transpose(2, 1, 0)

    def gate_up(g, u):
        g, u = chunks(g), chunks(u)
        return np.stack([g, u], axis=1).reshape(2 * g.shape[0], 128, -1)

    a = {k: np.asarray(v) for k, v in constants().items()}
    x = np.concatenate([np.asarray(x_prompt).reshape(TP, D), np.asarray(x_sample).reshape(32, D)])
    a["x"] = features(x)
    p = np.concatenate([np.asarray(p_prompt).reshape(2, TP, 256), np.asarray(p_sample).reshape(2, 32, 256)], axis=1)
    a["p"] = np.stack([features(p[0]), features(p[1])], axis=1)
    a["state"] = np.asarray(state_conv)[0].reshape(B, 2, C, 128).transpose(3, 2, 0, 1)
    order = [norm_mix[0], norm_ffn[0], norm_ple[0], norm_mix[1], norm_ffn[1], norm_ple[1]]
    a["gains"] = np.concatenate([np.asarray(g).reshape(C, 128).T for g in order], axis=1)
    a["convw"] = np.asarray(conv_w)[0].reshape(3, C, 128).transpose(2, 0, 1).reshape(128, 24)
    a["gq"] = np.tile(np.asarray(nsa_q_norm)[0], 2).reshape(128, 1)
    a["gk"] = np.tile(np.asarray(nsa_k_norm)[0], (1, 2)).T
    a["rel_bias"] = np.asarray(rel_bias)
    w = chunks(np.asarray(conv_w_in)[0]).reshape(3, C, 128, 1024)
    a["conv_in"] = w[[1, 2, 0]].transpose(1, 0, 2, 3).reshape(3 * C, 128, 1024)
    a["conv_out"] = chunks(np.asarray(conv_w_out)[0])
    g, u, d = (np.asarray(t)[0] for t in (ffn_w_gate, ffn_w_up, ffn_w_down))
    a["dense_gu"] = np.stack([gate_up(g[:, FE * i:FE * i + FE], u[:, FE * i:FE * i + FE]) for i in range(HALVES)])
    a["dense_down"] = np.stack([chunks(d[FE * i:FE * i + FE]) for i in range(HALVES)])
    g, u, d = (np.asarray(t)[0] for t in (moe_w_gate, moe_w_up, moe_w_down))
    a["moe_gu"] = np.stack([gate_up(g[e], u[e]) for e in range(EXPERTS)])
    a["moe_down"] = np.stack([chunks(d[e]) for e in range(EXPERTS)])
    a["ple_gate"] = np.stack([chunks(t) for t in np.asarray(ple_w_gate)])
    a["ple_proj"] = np.stack([chunks(t).reshape(2, 4, 128, 256).transpose(0, 2, 1, 3).reshape(2, 128, 1024)
                              for t in np.asarray(ple_w_proj)])
    w = np.asarray(nsa_w_in)[0]
    q = w[:, :1024].reshape(D, 2, 2, R, HD).transpose(0, 1, 3, 2, 4).reshape(D, 1024)
    a["nsa_q"] = chunks(q)
    kv = w[:, 1024:2560].reshape(D, 3, 4, 2, HD)
    cols = [kv[:, 0, :, 0], kv[:, 0, :, 1], kv[:, 1, :, 0], kv[:, 2, :, 0]]
    a["nsa_kv"] = chunks(np.concatenate([t.reshape(D, 256) for t in cols], axis=1))
    vt = kv[:, 1:3, :, 1].reshape(4, 2, 128, 512)
    a["nsa_vt"] = vt.transpose(0, 2, 1, 3).reshape(4, 128, 1024)
    a["wgate"] = w[:, 2560:].reshape(C, 128, 48).transpose(1, 0, 2)
    a["rout"] = np.asarray(moe_router)[0].reshape(C, 128, 8).transpose(1, 0, 2)
    wo = np.asarray(nsa_w_out)[0].reshape(2, 2, R, HD, D).transpose(0, 2, 1, 3, 4).reshape(1024, D)
    a["nsa_out"] = chunks(wo)
    a["w_cmp"] = np.asarray(nsa_w_cmp)[0].reshape(16, 2, 4, 2, HD, HD).transpose(1, 4, 3, 2, 0, 5).reshape(128, 128, 64)
    c = np.asarray(cache_cmp)[0].reshape(POOL, 4, 16, 2, 4, 2, HD)
    a["cache_cmp"] = c.transpose(5, 0, 3, 6, 4, 2, 1).reshape(2, POOL, 128, 256)
    c = np.asarray(cache_sel)[0]
    a["cache_selk"] = c[:, :, :, 0].reshape(POOL, 128, 2, 2, HD).transpose(0, 3, 4, 2, 1).reshape(POOL, 128, 256)
    a["cache_selv"] = c[:, :, :, 1].reshape(POOL, 128, 256)
    c = np.asarray(state_win)[0]
    a["win_k"] = c[:, :, :, 0].reshape(B, WIN, 2, 2, HD).transpose(0, 3, 4, 2, 1).reshape(B, 128, 1024)
    a["win_v"] = c[:, :, :, 1].reshape(B, 4, 128, 256).transpose(0, 2, 1, 3).reshape(B, 128, 1024)
    a["state_win"] = c.reshape(B, WIN, 512)
    a["page_table"] = np.asarray(page_table).reshape(1, B * PAGES)

    nc = bacc.Bacc("TRN2", target_bir_lowering=False, num_devices=1)
    arrays, A, O = {}, {}, {}
    for name, v in a.items():
        v = np.ascontiguousarray(v)
        arrays["in_" + name] = v
        A[name] = nc.dram_tensor("in_" + name, v.shape, mybir.dt.from_np(v.dtype), kind="ExternalInput").ap()
    A["gscratch"] = nc.dram_tensor("gscratch", (B, HEADS, STEPS, 3), mybir.dt.float32, kind="Internal").ap()
    outs = {"h": (128, C, T), "conv": (128, 144), "kvT": (128, 8, T), "vtok": (128, 3, 512), "win_old": (B, WIN - STEPS, 512)}
    for name, shape in outs.items():
        O[name] = nc.dram_tensor("out_" + name, shape, mybir.dt.float32, kind="ExternalOutput").ap()
    trunk(nc, A, O)
    r = run_bass_kernel_spmd(nc, [arrays], core_ids=[0]).results[0]

    h = r["out_h"].transpose(2, 1, 0).reshape(T, D)
    conv = r["out_conv"]
    conv_p = conv[:, :16].reshape(128, C, 2).transpose(2, 1, 0).reshape(1, 1, 2, D)
    conv_s = conv[:, 16:].reshape(128, C, B, 2).transpose(2, 3, 1, 0).reshape(1, B, 2, D)
    kvt = r["out_kvT"].reshape(2, HD, 4, 2, T).transpose(4, 2, 3, 0, 1).reshape(T, 4, GROUPS, HD)
    vt = r["out_vtok"].transpose(1, 0, 2)
    v = np.concatenate([vt[0], vt[1], vt[2][:32]]).reshape(T, 2, GROUPS, HD)
    cmp_ = np.stack([kvt[:, 0], kvt[:, 1]], axis=2)
    sel = np.stack([kvt[:, 2], v[:, 0]], axis=2)
    win = np.stack([kvt[:, 3], v[:, 1]], axis=2)

    def prompt(t):
        return np.ascontiguousarray(t[:TP]).reshape(1, 1, TP, GROUPS, 2, HD)

    def sample(t):
        return np.ascontiguousarray(t[TP:]).reshape(1, B, STEPS, GROUPS, 2, HD)

    win_old = r["out_win_old"].reshape(1, B, WIN - STEPS, GROUPS, 2, HD)
    return (h[:TP].reshape(1, TP, D), h[TP:].reshape(B, STEPS, D), conv_p, conv_s, prompt(cmp_), sample(cmp_),
            prompt(sel), sample(sel), prompt(win), np.concatenate([win_old, sample(win)], axis=2))
```

```python
import math
from contextlib import ExitStack

import numpy as np
import concourse.bass as bass
from concourse import mybir

D = 1024
T = 288
TP = 256
B = 8
STEPS = 4
C = D // 128
HEADS = 16
GROUPS = 4
R = 4
HD = 64
PAGES = 16
POOL = 160
FE = 1408
FC = FE // 128
EXPERTS = 8
HALVES = 2
BUCKETS = 32
EPS = 1e-6
NEG = -1e30
KEYS = 2048
WIN = 512
NB = 64
CAP = 96
SPLITS = T // CAP
MT = 3 * FC
GS, DS, PS = 11, 4, 6
GT = 1024
DT = FC * 128
OHL = 511


def bucket(dist):
    n = np.maximum(dist, 0)
    nf = np.maximum(n, 1).astype(np.float32)
    large = 16 + (np.log(nf / np.float32(16)) / np.float32(math.log(8.0)) * np.float32(16)).astype(np.int32)
    return np.where(n < 16, n, np.minimum(large, BUCKETS - 1))


M_SCAT = 2
M_SEL = M_SCAT + C
M_GU = M_SEL + 1
M_DOWN = M_GU + FC
MR = M_DOWN + 2


def result_order():
    o = [("tp", i) for i in range(8)] + [("tc",)] + [("ts", i) for i in range(6)]
    for b in range(B):
        o += [("ck", b), ("cv", b)]
    o += [("css", 0), ("css", 1)] + [("ct", p) for p in range(4)]
    o += [("norm", 0)]
    for c in range(C):
        o += [("gc", c), ("v", c), ("gb", c)]
    o += [("co", c) for c in range(C)] + [("norm", 1)]
    o += [("f", 0, k) for k in range(HALVES * (2 * FC + C))]
    o += [("norm", 2)]
    for c in range(C):
        o += [("pg", 0, c), ("pp", 0, c)]
    o += [("norm", 3)]
    o += [("kv", c) for c in range(4)]
    for c in range(4, 8):
        o += [("kv", c)]
        if c > 4:
            o += [("kss", c - 1)]
    o += [("vt", 0), ("vt", 1), ("vt", 2), ("kss", 7), ("gt",)]
    for j in range(8):
        o += [("q", j)]
        if j:
            o += [("qss", j - 1)]
    o += [("kcp",), ("qss", 7), ("vcp",), ("kcps",)]
    for u in range(17):
        if u < 16:
            o += [("pc", u), ("pl", u, 0), ("pl", u, 1)]
        if u:
            o += [("ptc", u - 1), ("ptp", u - 1, 0), ("ptp", u - 1, 1), ("po", u - 1)]
    for p in range(4):
        o += [("sc", p), ("sn", p), ("wq", p), ("wss", p), ("imp", p)]
        for t in range(4):
            o += [("sq", p, t), ("sss", p, t)]
        o += [("pt", p, i) for i in range(6)]
    o += [("wo", c) for c in range(C)] + [("norm", 4), ("rt",)] + [("at", i) for i in range(6)] + [("pos",)]
    o += [("m", k) for k in range(MR)]
    o += [("fs", c) for c in range(C)] + [("norm", 5)]
    for c in range(C):
        o += [("pg", 1, c), ("pp", 1, c)]
    return {label: n for n, label in enumerate(o)}


def rstd_order():
    o = [("css", 0), ("css", 1)] + [("norm", i) for i in range(4)] + [("kss", c) for c in range(4, 8)]
    o += [("qss", j) for j in range(8)] + [("kcps",)]
    for p in range(4):
        o += [("wss", p)] + [("sss", p, t) for t in range(4)]
    o += [("norm", 4), ("norm", 5)]
    return {label: n for n, label in enumerate(o)}


def g_tile_order():
    o = []
    for c in range(C):
        o += [("gc", c), ("v", c), ("gb", c)]
    o += [("co", c) for c in range(C)]
    o += [("f", 0, k) for k in range(HALVES * 2 * FC)]
    for i in range(2):
        o += [("pp", 0, i)] + [("pg", 0, 4 * i + k) for k in range(4)]
    o += [("kv", c) for c in range(8)] + [("vt", i) for i in range(4)] + [("q", j) for j in range(8)]
    for p in range(4):
        o += [("wk", p, 0), ("wk", p, 1)]
        o += [("sk", p, t, b2) for t in range(4) for b2 in range(2)]
        for b2 in range(2):
            o += [("wv", p, b2)]
    o += [("wo", c) for c in range(C)]
    o += [("m", k) for k in range(MT)]
    for i in range(2):
        o += [("pp", 1, i)] + [("pg", 1, 4 * i + k) for k in range(4)]
    return {label: n for n, label in enumerate(o)}


def trunk(nc, A, O):
    f32 = mybir.dt.float32
    ALU = mybir.AluOpType
    ACT = mybir.ActivationFunctionType
    AX = mybir.AxisListType
    RES = result_order()
    GN = g_tile_order()
    RN = rstd_order()
    PER = 2 * FC + C
    assert PER % PS == 0 and (2 * FC) % GS == 0 and C % DS == 0
    assert MR % PS == 0 and MT % GS == 0 and (M_DOWN - M_SEL) % PS == 0 and (M_DOWN + 1 - M_GU) % PS == 0

    with ExitStack() as ctx:
        def sem(name):
            return ctx.enter_context(nc.semaphore(name))

        used = [0]

        def region(name, n):
            t = ctx.enter_context(nc.sbuf_tensor(name, [128, n], f32))
            used[0] += n
            return t

        hT = region("hT", C * T)[:, :].rearrange("p (c t) -> p c t", t=T)
        aT_ = region("aT", C * T)
        aT = aT_[:, :].rearrange("p (c t) -> p c t", t=T)
        gring = region("gring", GS * GT)
        ident = region("ident", 128)
        ones = region("ones", 128)
        bones = region("bones", 128)
        bo32 = region("bo32", 32)
        rsum = region("rsum", 128)
        tri = region("tri", 1024)[:, :].rearrange("p (i j) -> p i j", j=32)
        pmask = region("pmask", 16)[:, :].rearrange("p (i n) -> p i n", n=8)
        wgate = region("wgate", C * 48)[:, :].rearrange("p (c n) -> p c n", n=48)
        rout = region("rout", C * 8)[:, :].rearrange("p (c n) -> p c n", n=8)
        gains = region("gains", 6 * C)
        convw = region("convw", 3 * C)
        state = region("state", C * 16)[:, :].rearrange("p (c b k) -> p c b k", b=B, k=2)
        gq = region("gq", 1)
        gqs = region("gqs", 1)
        gk = region("gk", 3)
        pT = region("pT", 2 * 2 * T)[:, :].rearrange("p (l k t) -> p l k t", l=2, k=2)
        sg_ = region("sg", 2 * T)
        sg = sg_[:, :].rearrange("p (i t) -> p i t", t=T)
        tmp_ = region("tmp", 2 * T)
        tmp = tmp_[:, :].rearrange("p (i t) -> p i t", t=T)
        rs_ = region("rs", 2 * T)
        rs = rs_[:, :].rearrange("p (i t) -> p i t", t=T)
        epsc = region("epsc", 1)
        small = region("small", 416)
        tabP_ = region("tabP", HEADS * 256)
        tabP = tabP_[:, :].rearrange("p (h k) -> p h k", k=256)
        tabC = region("tabC", 256)[:, :].rearrange("p (i n h) -> p i n h", i=2, n=8)
        tS = region("tS", KEYS)
        tW = region("tW", WIN)
        tN = region("tN", 4 * 32)[:, :].rearrange("p (a k) -> p a k", k=32)
        tCs = region("tCs", 128)
        kcn_ = region("kcn", 2 * B * NB)
        kcn = kcn_[:, :].rearrange("p (a n) -> p a n", a=2)
        vcs = region("vcs", 4 * 256)[:, :].rearrange("p (a n) -> p a n", a=4)
        gtok = region("gtok", 3 * 48)[:, :].rearrange("p (i n) -> p i n", n=48)
        grow = region("grow", 12)[:, :].rearrange("p (a n) -> p a n", n=3)
        Q = region("Q", 11136)
        q1 = Q[:, 0:2304].rearrange("p (c t) -> p c t", t=T)
        kvT = Q[:, 2304:4608].rearrange("p (c t) -> p c t", t=T)
        kn = Q[:, 4608:5760].rearrange("p (c t) -> p c t", t=T)
        vtok = Q[:, 5760:7296].rearrange("p (i n) -> p i n", n=512)
        QB = Q[:, 7296:8832].rearrange("p (r b a m) -> p r b a m", r=3, b=B, a=2)
        oT = Q[:, 8832:11136].rearrange("p (c t) -> p c t", t=T)
        qraw = oT
        dring = Q[:, 0:DS * DT]
        hff = Q[:, 5632:5632 + FC * T].rearrange("p (c t) -> p c t", t=T)
        sqn = Q[:, 5632:5632 + C * T].rearrange("p (c t) -> p c t", t=T)
        zT = Q[:, 8800:8800 + C * T].rearrange("p (c t) -> p c t", t=T)
        sqs = [zT if i in (2, 5) else sqn for i in range(6)]
        cbufs = [gring[:, 0:8192], Q[:, 0:8192]]
        vbufs = [t[:, 1024 * i:1024 * i + 1024] for t in (Q, tabP_) for i in range(4)]
        kcscale = [Q[:, 9216 + 512 * a:9728 + 512 * a] for a in range(2)]
        kcsq = Q[:, 8192:8192 + 1024].rearrange("p (a n) -> p a n", a=2)
        ohs = [aT_[:, 0:KEYS], Q[:, 9216:9216 + 672]]
        masks = Q[:, 9888:10656]
        lt = Q[:, 10656:10784]
        rbx = Q[0:BUCKETS + 1, 10784:10800]
        X = region("X", 10816)
        wc = X[:, 0:8192].rearrange("p (k e) -> p k e", e=64)
        UE = 2 + TP + B * 6
        uext = X[:, 8192:8192 + C * UE].rearrange("p (c t) -> p c t", t=UE)
        vraw = X[:, 8192:8192 + 1024].rearrange("p (a n) -> p a n", a=2)
        cstage = X[:, 10640:10784]
        ohv = X[0:BUCKETS + 1, 9216:9216 + OHL]
        kvp = X[:, 8192:8192 + 8 * TP].rearrange("p (c t) -> p c t", t=TP)
        S = X[:, 0:KEYS + 32]
        SW = X[:, 2080:2080 + WIN + 32]
        SC = X[:, 2624:2752]
        SCg = X[:, 2752:2880]
        ksq = X[:, 2880:4928].rearrange("p (i n) -> p i n", i=2)
        rsb = [X[:, 4928:5440], X[:, 8384:8896]]
        PT = X[:, 5440:8384].rearrange("p (k m) -> p k m", m=128)
        Sp = X[:, 2880:4416].rearrange("p (i n) -> p i n", i=2)
        PTp = X[:, 4416:5952].rearrange("p (i r n) -> p i r n", i=2, r=2)
        PTc = X[0:8, 5952:6464].rearrange("p (i n) -> p i n", i=2)
        Scp = X[:, 6464:6496].rearrange("p (u i n) -> p u i n", u=2, i=2)
        atok = X[:, 0:3072].rearrange("p (i n) -> p i n", i=3)
        ae = X[:, 3072:3072 + C * CAP].rearrange("p (c m) -> p c m", m=CAP)
        pick = X[:, 3840:3840 + 3 * CAP].rearrange("p (i m) -> p i m", m=CAP)
        wpick = X[:, 4128:4128 + 3 * CAP].rearrange("p (i m) -> p i m", m=CAP)
        scat = X[0:CAP, 4416:4704]
        he = X[:, 4704:4704 + FC * CAP].rearrange("p (f m) -> p f m", m=CAP)
        sige = X[:, 5760:5760 + FC * CAP].rearrange("p (f m) -> p f m", m=CAP)
        ye = X[0:CAP, 6816:7840]
        before = X[:, 7840:7968]
        count = X[:, 7968:8256]
        ones1 = X[:, 8256:8384]
        routed = X[:, 8384:8408].rearrange("p (i e) -> p i e", e=8)
        pos1 = X[:, 8408:8432].rearrange("p (i e) -> p i e", e=8)
        NI = EXPERTS * SPLITS
        NX = EXPERTS * (SPLITS - 1)
        at = [8432]

        def small_table(n):
            at[0] += n
            return X[0:1, at[0] - n:at[0]]

        xtab = small_table(3 * NX + 2 * NI)
        xthr, xe, xs = (xtab[:, NX * i:NX * i + NX] for i in range(3))
        slot1, e0 = (xtab[:, 3 * NX + NI * i:3 * NX + NI * i + NI] for i in range(2))
        over, okey, items_f = small_table(NX), small_table(NX), small_table(2 * NI + 2)
        osq, ohit, oval = (small_table(n * NX).rearrange("p (i j) -> p i j", j=NX) for n in (NX, NI, NI))
        assert at[0] <= 10816
        cnt1 = aT_[:, 0:1024].rearrange("p (i j) -> p i j", j=32)
        cnt2 = aT_[:, 1024:2048].rearrange("p (i j) -> p i j", j=32)
        vcp = sg_[0:8, 0:256]
        kcp = sg_[:, 256:272].rearrange("p (a n) -> p a n", a=2)
        kcpn = sg_[:, 272:288].rearrange("p (a n) -> p a n", a=2)
        nmp = small[:, 0:12].rearrange("p (u i r) -> p u i r", u=2, i=2)
        smp = small[:, 12:24].rearrange("p (u i r) -> p u i r", u=2, i=2)
        scp = small[:, 24:36].rearrange("p (u i r) -> p u i r", u=2, i=2)
        mxs = small[:, 36:39]
        sms = small[:, 40:43]
        fac = small[:, 44:47]
        score = small[:, 48:80]
        rank = small[:, 80:112]
        blkm = small[:, 112:144]
        half = small[:, 144:208]
        rl = small[:, 208:232].rearrange("p (i e) -> p i e", e=8)
        rk = small[:, 232:256].rearrange("p (i e) -> p i e", e=8)
        rmx = small[:, 256:259]
        rsm = small[:, 260:263]
        rg = small[:, 264:288].rearrange("p (i e) -> p i e", e=8)
        cmp8 = [small[:, 288 + 64 * i:352 + 64 * i].rearrange("p (i j) -> p i j", j=8) for i in range(2)]

        ptab = ctx.enter_context(nc.sbuf_tensor("ptab", [1, B * PAGES], mybir.dt.int32))
        items = ctx.enter_context(nc.sbuf_tensor("items", [1, 2 * NI + 2], mybir.dt.int32))

        banks = [ctx.enter_context(nc.psum_tensor(f"bank{i}", [128, 512], f32)) for i in range(PS)]
        oP = [ctx.enter_context(nc.psum_tensor(f"oP{i}", [128, 512], f32)) for i in range(2)]

        psum_full = [sem(f"psum_full{i}") for i in range(PS)]
        psum_drained = [sem(f"psum_drained{i}") for i in range(PS)]
        g_in = [sem(f"g_in{i}") for i in range(GS)]
        d_in = [sem(f"d_in{i}") for i in range(DS)]
        c_in = [sem(f"c_in{i}") for i in range(2)]
        v_in = [sem(f"v_in{i}") for i in range(8)]
        keys_used, values_used = sem("keys_used"), sem("values_used")
        tables_in, ptab_in = sem("tables_in"), sem("ptab_in")
        consts_in, wcmp_in, lt_in, route_in = sem("consts_in"), sem("wcmp_in"), sem("lt_in"), sem("route_in")
        lt_clear, rb_mask, eps_set, rstd_ready = sem("lt_clear"), sem("rb_mask"), sem("eps_set"), sem("rstd_ready")
        sq_ready, a_ready = sem("sq_ready"), sem("a_ready")
        conv_staged, win_stored = sem("conv_staged"), sem("win_stored")
        sig_ready, hff_ready, hsq_ready = sem("sig_ready"), sem("hff_ready"), sem("hsq_ready")
        kcn_ready, kn_ready, q_ready = sem("kcn_ready"), sem("kn_ready"), sem("q_ready")
        kvp_in, gates_out, gates_in = sem("kvp_in"), sem("gates_out"), sem("gates_in")
        qb_ready = sem("qb_ready")
        pmax_ready, pexp_ready, pscaled = sem("pmax_ready"), sem("pexp_ready"), sem("pscaled")
        smax_ready, sexp_ready, cprob_ready, sscaled = sem("smax_ready"), sem("sexp_ready"), sem("cprob_ready"), sem("sscaled")
        ksq_ready, so_ready = sem("ksq_ready"), sem("so_ready")
        rmax_ready, rexp_ready = sem("rmax_ready"), sem("rexp_ready")
        routed_ready, items_ready, picks_ready, item_cleared = sem("routed_ready"), sem("items_ready"), sem("picks_ready"), sem("item_cleared")
        down_used, silu_ready = sem("down_used"), sem("silu_ready")
        stored, rows_stored = sem("stored"), sem("rows_stored")
        dve_step, act_step = sem("dve_step"), sem("act_step")

        NTABLE, NCONST = 5, 16

        def bank(label, k=0):
            return banks[(RES[label] + k) % PS]

        def turn(label, e=0, k=0):
            return (RES[label] + k) // PS + (PER // PS if label[0] == "f" else MR // PS) * e

        def full(eng, label, e=0, k=0):
            eng.wait_ge(psum_full[(RES[label] + k) % PS], turn(label, e, k) + 1)

        def drained(eng, label, e=0, k=0):
            eng.wait_ge(psum_drained[(RES[label] + k) % PS], turn(label, e, k) + 1)

        def bank_free(eng, label, e=0, k=0):
            if RES[label] + k >= PS:
                eng.wait_ge(psum_drained[(RES[label] + k) % PS], turn(label, e, k))

        def fill(ins, label, k=0):
            ins.then_inc(psum_full[(RES[label] + k) % PS], 1)

        def drain(ins, label, k=0):
            ins.then_inc(psum_drained[(RES[label] + k) % PS], 1)

        def gslot(label, k=0):
            s = (GN[label] + k) % GS
            return gring[:, s * GT:(s + 1) * GT]

        def g_arrived(eng, label, e=0, k=0):
            n = GN[label] + k
            eng.wait_ge(g_in[n % GS], landed[n] + 16 * ((2 * FC if label[0] == "f" else MT) // GS) * e)

        landed = []
        for n, label in enumerate(GN):
            landed.append((landed[n - GS] if n >= GS else 0) + (64 if label[0] == "sk" else 16))

        def g_released(eng, label, e=0):
            kind = label[0]
            if kind == "pp":
                full(eng, ("pp", label[1], 4 * label[2] + 3), e)
            elif kind == "m":
                f = label[1] - 2 * FC
                if f < 0:
                    full(eng, ("m", M_GU + label[1] // 2), e)
                elif f < FC - 1:
                    eng.wait_ge(down_used, f + 1 + (FC - 1) * e)
                else:
                    full(eng, ("m", M_DOWN + 1), e)
            elif kind == "vt":
                full(eng, ("vt", 2))
            elif kind == "f":
                full(eng, ("f", label[1], label[2] // (2 * FC) * PER + label[2] % (2 * FC)))
            elif kind == "wk":
                full(eng, ("wss", label[1]))
            elif kind == "sk":
                full(eng, ("sss", label[1], label[2]))
            elif kind == "wv":
                eng.wait_ge(values_used, 10 * label[1] + 5 * label[2] + 1)
            else:
                full(eng, label, e)

        def update_of(kind, c):
            return [None, ("co", c), None, ("pp", 0, c), ("wo", c), ("fs", c)][kind]

        def h_updated(eng, kind, c, more=0):
            if kind == 0:
                return
            if kind == 2:
                drained(eng, ("f", 0, 0), HALVES - 1, 2 * FC + c)
            else:
                drained(eng, update_of(kind, c), more)

        def item_count(eng):
            eng.wait_ge(items_ready, 1)
            return (eng.value_load(items[0:1, 2 * NI:2 * NI + 1], min_val=EXPERTS, max_val=NI),
                    eng.value_load(items[0:1, 2 * NI + 1:2 * NI + 2], min_val=EXPERTS - 1, max_val=NI - 1))

        def item_value(eng, row, i, top):
            return eng.value_load(items[0:1, bass.ds(i + NI * row, 1)], min_val=0, max_val=top)

        def page(eng, b, i):
            return eng.value_load(ptab[0:1, b * PAGES + i:b * PAGES + i + 1], min_val=0, max_val=POOL - 1)

        def cmp_pages(eng, b, first, count):
            for i in range(first, first + count):
                src = A["cache_cmp"][bass.ds(page(eng, b, i), 1), :, :].rearrange("a p n -> (a p) n")
                eng.dma_start(cbufs[b % 2][:, i * 512:(i + 1) * 512], src).then_inc(c_in[b % 2], 16)

        block = ctx.enter_context(nc.Block())

        @block.sync
        def _(sp):
            sp.dma_start(ptab[:, :], A["page_table"]).then_inc(ptab_in, 16)
            for k in range(4):
                sp.dma_start(wc[:, 32 * k:32 * k + 32, :], A["w_cmp"][:, 32 * k:32 * k + 32, :]).then_inc(wcmp_in, 16)
            sp.wait_ge(ptab_in, 16)
            for b in range(B):
                if b >= 2:
                    full(sp, ("cv", b - 2))
                cmp_pages(sp, b, 0, PAGES // 2)
            full(sp, ("cv", B - 2))
            g_labels = list(GN)

            def g_load(label, src, more=0):
                n = GN[label]
                if n >= GS:
                    g_released(sp, g_labels[n - GS], more)
                sp.dma_start(gslot(label)[:, :], src).then_inc(g_in[n % GS], 16)

            def key_pages(label, b, first):
                n = GN[label]
                g_released(sp, g_labels[n - GS])
                for i in range(4):
                    src = A["cache_selk"][bass.ds(page(sp, b, first + i), 1), :, :].rearrange("a p n -> (a p) n")
                    sp.dma_start(gslot(label)[:, i * 256:(i + 1) * 256], src).then_inc(g_in[n % GS], 16)

            for c in range(C):
                for i, name in enumerate(("gc", "v", "gb")):
                    g_load((name, c), A["conv_in"][3 * c + i])
            for c in range(C):
                g_load(("co", c), A["conv_out"][c])

            def dense_loads(turns, gu, down):
                L = ("f", 0, 0)
                with sp.Fori(0, turns) as e:
                    for k in range(2 * FC):
                        full(sp, L, e, k - GS if k >= GS else k + GS - PER)
                        sp.dma_start(gslot(L, k)[:, :], gu[bass.ds(e, 1), k].rearrange("a p n -> (a p) n"))\
                          .then_inc(g_in[(GN[L] + k) % GS], 16)
                    for k in range(C):
                        n = k
                        full(sp, L, e, 2 * FC + (k - DS if k >= DS else k + C - DS - PER))
                        sp.dma_start(dring[:, (n % DS) * DT:(n % DS + 1) * DT],
                                     down[bass.ds(e, 1), k].rearrange("a p n -> (a p) n")).then_inc(d_in[n % DS], 16)

            full(sp, ("css", 1))
            full(sp, ("co", C - 1))
            dense_loads(HALVES, A["dense_gu"], A["dense_down"])

            def ple_loads(layer, more=0):
                for i in range(2):
                    g_load(("pp", layer, i), A["ple_proj"][layer, i], more)
                    for k in range(4):
                        g_load(("pg", layer, 4 * i + k), A["ple_gate"][layer, 4 * i + k], more)

            ple_loads(0)
            for c in range(8):
                g_load(("kv", c), A["nsa_kv"][c])
            for i in range(4):
                g_load(("vt", i), A["nsa_vt"][i])
            for j in range(8):
                g_load(("q", j), A["nsa_q"][j])
            for p in range(4):
                for b2 in range(2):
                    g_load(("wk", p, b2), A["win_k"][2 * p + b2])
                for t in range(4):
                    for b2 in range(2):
                        key_pages(("sk", p, t, b2), 2 * p + b2, 4 * t)
                for b2 in range(2):
                    g_load(("wv", p, b2), A["win_v"][2 * p + b2])
            for c in range(C):
                g_load(("wo", c), A["nsa_out"][c])
            drained(sp, ("wo", 0))
            for dst, name in ((before[:, :], "before"), (count[:, :], "count"), (xtab, "xtab")):
                sp.dma_start(dst, A[name]).then_inc(route_in, 16)

            def item_loads(i, e, tiles, before=None):
                for k in tiles:
                    sp_label = ("m", k)
                    n = GN[sp_label]
                    if k >= GS:
                        g_released(sp, ("m", k - GS), i)
                    elif before is not None:
                        g_released(sp, ("m", k - GS + MT), before)
                    else:
                        g_released(sp, g_labels[n - GS])
                    sp.dma_start(gslot(sp_label)[:, :], A["moe"][bass.ds(e, 1), k].rearrange("a p n -> (a p) n"))\
                      .then_inc(g_in[n % GS], 16)

            item_loads(0, 0, range(GS))
            n_items, more = item_count(sp)
            with sp.Fori(0, more) as i:
                item_loads(i, item_value(sp, 0, i, EXPERTS - 1), range(GS, MT))
                item_loads(i + 1, item_value(sp, 0, i + 1, EXPERTS - 1), range(GS), before=i)
            item_loads(more, item_value(sp, 0, more, EXPERTS - 1), range(GS, MT))
            ple_loads(1, more)
            sp.wait_ge(rows_stored, 16 * 4)
            for c in range(C):
                drained(sp, ("pp", 1, c), more)
                sp.dma_start(O["h"][:, c, :], hT[:, c, :]).then_inc(stored, 16)
            sp.wait_ge(stored, 16 * C)
            sp.wait_ge(win_stored, 16 * B)

        @block.gpsimd
        def _(pool):
            pool.memset(lt[:, :], 0.0).then_inc(lt_clear, 1)
            pool.wait_ge(lt_clear, 1)
            for t in range(STEPS):
                for b2 in range(2):
                    dst = lt[32 * t:32 * t + 32, 64 * b2 + t:64 * b2 + 64:4]
                    pool.dma_start(dst, A["rel_bias"][:, :], allow_slow_non_contiguous=True).then_inc(lt_in, 16)
            drained(pool, ("co", 0))
            for b in range(B):
                n = (WIN - STEPS) * 512
                src = A["state_win"][b, STEPS:WIN, :].rearrange("s n -> (s n)").rearrange("(a n) -> a n", a=16)
                dst = O["win_old"][b].rearrange("s n -> (s n)").rearrange("(a n) -> a n", a=16)
                pool.dma_start(dst, src).then_inc(win_stored, 16)
            pool.wait_ge(conv_staged, 2)
            pool.dma_start(O["conv"][:, :], cstage[:, :]).then_inc(rows_stored, 16)
            for c4 in range(4):
                drained(pool, ("kv", c4))
            for c in range(2):
                for g in range(GROUPS):
                    for l2 in range(2):
                        pool.dma_start(kvp[64 * l2:64 * l2 + 64, 4 * c + g, 0:TP - l2],
                                       kvT[64 * (g % 2):64 * (g % 2) + 64, 2 * c + g // 2, l2:TP]).then_inc(kvp_in, 16)
            for c in range(4, 8):
                drained(pool, ("kv", c))
            pool.dma_start(O["kvT"][:, :, :], kvT[:, :, :]).then_inc(rows_stored, 16)
            for i in range(3):
                drained(pool, ("vt", i))
            pool.dma_start(O["vtok"][:, 0:2, :], vtok[:, 0:2, :]).then_inc(rows_stored, 16)
            pool.dma_start(O["vtok"][0:32, 2, :], vtok[0:32, 2, :]).then_inc(rows_stored, 16)
            drained(pool, ("gt",))
            for b in range(B):
                src = gtok[STEPS * b:STEPS * b + STEPS, 2, :].rearrange("t (r h) -> t r h", r=3)
                pool.dma_start(A["gscratch"][b].rearrange("h t r -> t r h"), src,
                               allow_slow_non_contiguous=True).then_inc(gates_out, 16)
            pool.wait_ge(gates_out, 16 * B)
            for p in range(4):
                src = A["gscratch"][2 * p:2 * p + 2].rearrange("b h t r -> (b h t) r")
                pool.dma_start(grow[:, p, :], src).then_inc(gates_in, 16)
            pool.wait_ge(rows_stored, 16 * 4)
            pool.wait_ge(qb_ready, 12)
            full(pool, ("po", 15))
            drained(pool, ("pc", 15))
            pool.wait_ge(ptab_in, 16)
            for p in range(4):
                for b2 in range(2):
                    for t in range(4):
                        k = 4 * b2 + t
                        if p:
                            pool.wait_ge(values_used, 10 * (p - 1) + 5 * b2 + 2 + t)
                        for i in range(4):
                            src = A["cache_selv"][bass.ds(page(pool, 2 * p + b2, 4 * t + i), 1), :, :].rearrange("a p n -> (a p) n")
                            pool.dma_start(vbufs[k][:, i * 256:(i + 1) * 256], src).then_inc(v_in[k], 16)

        @block.scalar
        def _(act):
            step = [0]

            def chain(ins):
                step[0] += 1
                ins.then_inc(act_step, 1)

            loads = [(ohv, A["ohv"]), (rbx[0:BUCKETS, :], A["rel_bias"]), (ohs[0], A["ohs"][:, 0:KEYS]),
                     (ohs[1], A["ohs"][:, KEYS:KEYS + 672]), (masks[:, :], A["masks"])]
            assert len(loads) == NTABLE
            for dst, src in loads:
                act.dma_start(dst, src).then_inc(tables_in, 16)
            act.wait_ge(ptab_in, 16)
            for b in range(2):
                cmp_pages(act, b, PAGES // 2, PAGES // 2)
            loads = [(ident[:, :], "ident"), (ones[:, :], "ones"), (bones[:, :], "bones"), (bo32[:, :], "bo32"), (rsum[:, :], "rsum"),
                     (hT, "x"), (state, "state"), (gains[:, :], "gains"), (convw[:, :], "convw"), (gq[:, :], "gq"), (gk[:, :], "gk"),
                     (tri, "tri"), (pmask, "pmask"), (pT, "p"), (wgate, "wgate"), (rout, "rout")]
            assert len(loads) == NCONST
            for dst, name in loads:
                act.dma_start(dst, A[name]).then_inc(consts_in, 16)

            act.wait_ge(eps_set, 1)

            def rstd(dst, src, label, more=0):
                full(act, label, more)
                drain(act.activation(dst, src, ACT.Ln, bias=epsc[:, :]), label)
                drained(act, label, more)
                act.activation(dst, dst, ACT.Exp, scale=-0.5).then_inc(rstd_ready, 1)

            def row_scale(m):
                if 2 <= m < 6:
                    act.wait_ge(kn_ready, 2 * (m - 1))
                elif m >= 6:
                    act.wait_ge(q_ready, m - 5)
                label = ("kss", m + 4) if m < 4 else ("qss", m - 4) if m < 12 else ("kcps",)
                n = T if m < 12 else 16
                rstd(rs[:, m % 2, 0:n], bank(label)[:, 0:n], label)

            for i in range(8):
                full(act, ("tp", i))
                drain(act.activation(tabP[:, :, 32 * i:32 * i + 32],
                                     bank(("tp", i))[:, :].rearrange("p (k h) -> p h k", h=16), ACT.Copy), ("tp", i))
            full(act, ("tc",))
            drain(act.activation(tabC, bank(("tc",))[:, 0:256].rearrange("p (i n h) -> p i n h", i=2, n=8), ACT.Copy), ("tc",))
            for i in range(4):
                full(act, ("ts", i))
                drain(act.activation(tS[:, 512 * i:512 * i + 512], bank(("ts", i))[:, :], ACT.Copy), ("ts", i))

            for b in range(B):
                full(act, ("ck", b))
                src = bank(("ck", b))[:, 0:128].rearrange("p (a n) -> p a n", a=2)
                chain(act.activation(kcn[:, :, NB * b:NB * b + NB], src, ACT.Copy))
                drain(act.activation(kcsq[:, :, NB * b:NB * b + NB], src, ACT.Square), ("ck", b))
                full(act, ("cv", b))
                drain(act.activation(vraw[:, :, NB * b:NB * b + NB], bank(("cv", b))[:, 0:128].rearrange("p (a n) -> p a n", a=2),
                                     ACT.Copy), ("cv", b))
                if b + 2 < B:
                    cmp_pages(act, b + 2, PAGES // 2, PAGES // 2)
            drained(act, ("ts", 4))
            drained(act, ("ts", 5))
            for a in range(2):
                rstd(kcscale[a], bank(("css", a))[:, :], ("css", a))
            for p in range(4):
                full(act, ("ct", p))
                drain(act.activation(vcs[:, p, :], bank(("ct", p))[:, 0:256], ACT.Copy), ("ct", p))

            def norm_squares(i, more=0):
                for c in range(C):
                    h_updated(act, i, c, more)
                    if i == 0 and c == 0:
                        act.wait_ge(consts_in, 16 * NCONST)
                        full(act, ("css", 1))
                    act.activation(sqs[i][:, c, :], hT[:, c, :], ACT.Square).then_inc(sq_ready, 1)
                rstd(rs[:, 0, :], bank(("norm", i))[:, 0:T], ("norm", i), more)

            norm_squares(0)
            for c in range(C):
                full(act, ("gc", c))
                if c >= 2:
                    drained(act, ("v", c - 2))
                drain(act.activation(sg[:, c % 2, :], bank(("gc", c))[:, 0:T], ACT.Copy), ("gc", c))
            norm_squares(1)

            def dense_gates(turns):
                with act.Fori(0, turns) as e:
                    for f in range(FC):
                        full(act, ("f", 0, 0), e, 2 * f)
                        drained(act, ("f", 0, 0), e, 2 * (f - 2) + 1 if f >= 2 else 2 * (f % 2 + FC - 2 + (FC % 2) * (1 - 2 * f)) + 1 - PER)
                        act.activation(sg[:, f % 2, :],
                                       bank(("f", 0, 0), 2 * f)[:, 0:T], ACT.Sigmoid).then_inc(sig_ready, 1)

            def ple_gates(layer, more=0):
                for c in range(C):
                    full(act, ("pg", layer, c), more)
                    if c >= 2:
                        drained(act, ("pp", layer, c - 2), more)
                    drain(act.activation(sg[:, c % 2, :], bank(("pg", layer, c))[:, 0:T], ACT.Sigmoid), ("pg", layer, c))

            dense_gates(HALVES)
            norm_squares(2)
            ple_gates(0)
            norm_squares(3)

            def square(label, n, half):
                if n >= 2:
                    full(act, half)
                chain_ready = act.activation(tmp[:, n % 2, :], bank(label)[:, 0:T], ACT.Square)
                chain_ready.then_inc(hsq_ready, 1)

            for c in range(8):
                full(act, ("kv", c))
                if c < 4:
                    drain(act.activation(kvT[:, c, :], bank(("kv", c))[:, 0:T], ACT.Copy), ("kv", c))
                else:
                    square(("kv", c), c - 4, ("kss", c - 2) if c >= 6 else None)
                    drain(act.activation(kvT[:, c, :], bank(("kv", c))[:, 0:T], ACT.Copy), ("kv", c))
                    if c > 4:
                        row_scale(c - 5)
            for i in range(3):
                n = 128 if i < 2 else 32
                full(act, ("vt", i))
                drain(act.activation(vtok[0:n, i, :], bank(("vt", i))[0:n, :], ACT.Copy), ("vt", i))
            row_scale(3)
            full(act, ("gt",))
            chain(act.activation(gtok[0:32, 2, :], bank(("gt",))[0:32, 96:144], ACT.Sigmoid))
            act.wait_ge(act_step, step[0])
            drain(act.activation(gtok[:, 0:2, :], bank(("gt",))[:, 0:96].rearrange("p (i n) -> p i n", i=2),
                                 ACT.Sigmoid), ("gt",))
            for j in range(8):
                full(act, ("q", j))
                square(("q", j), 4 + j, ("qss", j - 2) if j >= 2 else ("kss", 6 + j))
                drain(act.activation(qraw[:, j, :], bank(("q", j))[:, 0:T], ACT.Copy), ("q", j))
                if j:
                    row_scale(3 + j)
            full(act, ("kcp",))
            full(act, ("qss", 6))
            src = bank(("kcp",))[:, 0:16].rearrange("p (a n) -> p a n", a=2)
            act.activation(tmp_[:, 0:16].rearrange("p (a n) -> p a n", a=2), src, ACT.Square).then_inc(hsq_ready, 1)
            drain(act.activation(kcp, src, ACT.Copy), ("kcp",))
            row_scale(11)
            full(act, ("vcp",))
            drain(act.activation(vcp, bank(("vcp",))[0:8, 0:256], ACT.Copy), ("vcp",))

            row_scale(12)

            for u in range(17):
                if u < 16:
                    w = u % 2
                    for i in range(2):
                        nk = 128 * (i + 1)
                        act.wait_ge(pmax_ready, 3 * u + 1 + i)
                        o = 256 * i
                        for r in range(2):
                            ins = act.activation(Sp[:, w, o + r * nk:o + (r + 1) * nk], Sp[:, w, o + r * nk:o + (r + 1) * nk],
                                                 ACT.Exp, bias=nmp[:, w, i, r + 1:r + 2], accum_out=smp[:, w, i, r + 1:r + 2])
                            ins.then_inc(pexp_ready, 1)
                    act.wait_ge(pmax_ready, 3 * u + 3)
                    for i in range(2):
                        act.activation(Scp[:, w, i, :], Scp[:, w, i, :], ACT.Exp, bias=nmp[:, w, i, 0:1],
                                       accum_out=smp[:, w, i, 0:1]).then_inc(pexp_ready, 1)
                if u:
                    w = (u - 1) % 2
                    full(act, ("ptc", u - 1))
                    drain(act.activation(PTc[:, w, :], bank(("ptc", u - 1))[0:8, 0:256], ACT.Copy), ("ptc", u - 1))
                    for i in range(2):
                        full(act, ("ptp", u - 1, i))
                        n = 128 * (i + 1)
                        drain(act.activation(PTp[:, w, :, 128 * i:128 * i + n],
                                             bank(("ptp", u - 1, i))[:, 0:2 * n].rearrange("p (r n) -> p r n", r=2),
                                             ACT.Copy), ("ptp", u - 1, i))
            full(act, ("po", 15))

            def exps(p, r, view):
                act.wait_ge(smax_ready, 3 * p + 1 + {0: 0, 2: 1, 1: 2}[r])
                act.activation(view, view, ACT.Exp, bias=mxs[:, r:r + 1], accum_out=sms[:, r:r + 1]).then_inc(sexp_ready, 1)

            for p in range(4):
                def key_squares(label, n):
                    g_arrived(act, label)
                    if n % 2 == 0:
                        if p or n:
                            act.wait_ge(keys_used, 5 * p + n // 2)
                    elif n == 1:
                        if p:
                            full(act, ("sss", p - 1, 3))
                    else:
                        full(act, ("sss", p, (n - 5) // 2) if n > 3 else ("wss", p))
                    act.activation(ksq[:, n % 2, :], gslot(label)[:, :], ACT.Square).then_inc(ksq_ready, 1)

                before = [("wk", p, 0), ("wk", p, 1)] + [("sk", p, t, b2) for t in range(4) for b2 in range(2)]
                key_squares(before[0], 0)
                key_squares(before[1], 1)
                exps(p, 0, SC[:, :])

                def key_scale(i):
                    label = ("sss", p, i - 1) if i else ("wss", p)
                    if i > 1:
                        drained(act, ("sq", p, i - 3) if i > 2 else ("wq", p))
                    elif p:
                        drained(act, ("sq", p - 1, 2 + i))
                    rstd(rsb[(5 * p + i) % 2], bank(label)[:, :], label)

                key_scale(0)
                key_squares(before[2], 2)
                key_squares(before[3], 3)
                full(act, ("imp", p))
                ins = act.activation(SCg[:, :], bank(("imp", p))[:, 0:128], ACT.Copy)
                drain(ins, ("imp", p))
                exps(p, 2, SW[:, :])
                for t in range(4):
                    if t < 3:
                        key_squares(before[2 * t + 4], 2 * t + 4)
                    key_scale(t + 1)
                    if t < 3:
                        key_squares(before[2 * t + 5], 2 * t + 5)
                exps(p, 1, S[:, :])
                for i in range(6):
                    full(act, ("pt", p, i))
                    src = bank(("pt", p, i))
                    if i == 0:
                        ins = act.activation(PT[:, 0:4, :], src[:, :].rearrange("p (k m) -> p k m", k=4), ACT.Copy)
                    elif i == 1:
                        chain(act.activation(PT[:, 4, :], src[:, 0:128], ACT.Copy))
                        act.wait_ge(act_step, step[0])
                        ins = act.activation(PT[0:32, 5:7, :], src[0:32, 128:384].rearrange("p (k m) -> p k m", k=2), ACT.Copy)
                    else:
                        k = 7 + 4 * (i - 2)
                        ins = act.activation(PT[:, k:k + 4, :], src[:, :].rearrange("p (k m) -> p k m", k=4), ACT.Copy)
                    drain(ins, ("pt", p, i))

            norm_squares(4)
            for k in range(6):
                i, h, n = k // 2, k % 2, 128 if k < 4 else 32
                full(act, ("at", k))
                drain(act.activation(atok[0:n, i, 512 * h:512 * h + 512], bank(("at", k))[0:n, :], ACT.Copy), ("at", k))
            act.wait_ge(rmax_ready, 1)
            for i in range(3):
                act.activation(rg[:, i, :], rl[:, i, :], ACT.Exp, bias=rmx[:, i:i + 1]).then_inc(rexp_ready, 1)
            n_items, more = item_count(act)
            act.wait_ge(item_cleared, 2)
            with act.Fori(0, n_items) as i:
                M = ("m", 0)
                for h in range(2):
                    full(act, M, i, h)
                    drain(act.activation(ae[:, 4 * h:4 * h + 4, :], bank(M, h)[:, 0:4 * CAP].rearrange("p (c m) -> p c m", m=CAP),
                                         ACT.Copy), M, h)
                full(act, M, i, M_SEL)
                drain(act.activation(scat, bank(M, M_SEL)[0:CAP, 0:T], ACT.Copy), M, M_SEL)
                for f in range(FC):
                    full(act, M, i, M_GU + f)
                    if f == 0:
                        drained(act, M, i, M_GU + FC - 1 - MR)
                    act.activation(sige[:, f, :], bank(M, M_GU + f)[:, 0:CAP], ACT.Sigmoid).then_inc(sig_ready, 1)
                for h in range(2):
                    full(act, M, i, M_DOWN + h)
                    drain(act.activation(ye[:, 512 * h:512 * h + 512], bank(M, M_DOWN + h)[0:CAP, :], ACT.Copy), M, M_DOWN + h)
            norm_squares(5, more)
            ple_gates(1, more)

        @block.vector
        def _(dve):
            step = [0]

            def chain(ins):
                step[0] += 1
                ins.then_inc(dve_step, 1)

            def settled():
                dve.wait_ge(dve_step, step[0])

            def scaled_by(label):
                dve.wait_ge(rstd_ready, RN[label] + 1)

            dve.memset(epsc[:, :], EPS).then_inc(eps_set, 1)
            dve.memset(rbx[BUCKETS:BUCKETS + 1, :], NEG).then_inc(rb_mask, 1)
            dve.wait_ge(tables_in, 16 * NTABLE)
            full(dve, ("ts", 4))
            drain(dve.tensor_tensor(tW[:, :], bank(("ts", 4))[:, :], masks[:, 0:512], ALU.add), ("ts", 4))
            full(dve, ("ts", 5))
            chain(dve.tensor_tensor(tN, bank(("ts", 5))[:, 0:32].unsqueeze(1).to_broadcast([128, 4, 32]),
                                    masks[:, 512:640].rearrange("p (a k) -> p a k", a=4), ALU.add))
            drain(dve.tensor_tensor(tCs[:, :], bank(("ts", 5))[:, 32:160], masks[:, 640:768], ALU.add), ("ts", 5))
            dve.wait_ge(consts_in, 16 * NCONST)
            chain(dve.tensor_scalar(gqs[:, :], gq[:, :], HD ** -0.5, None, ALU.mult))

            for a in range(2):
                scaled_by(("css", a))
                dve.scalar_tensor_tensor(kcn[:, a, :], kcn[:, a, :], gk[:, 0:1], kcscale[a], ALU.mult, ALU.mult).then_inc(kcn_ready, 1)

            def norm(i):
                scaled_by(("norm", i))
                for c in range(C):
                    dve.scalar_tensor_tensor(aT[:, c, :], hT[:, c, :], gains[:, C * i + c:C * i + c + 1], rs[:, 0, :],
                                             ALU.mult, ALU.mult).then_inc(a_ready, 1)

            norm(0)
            chain(dve.memset(uext[:, :, 0:2], 0.0))
            us = uext[:, :, 258:UE].rearrange("p c (b k) -> p c b k", b=B)
            for c in range(C):
                chain(dve.tensor_copy(us[:, c, :, 0:2], state[:, c, :, :]))
            for c in range(C):
                drained(dve, ("gc", c))
                full(dve, ("v", c))
                v = bank(("v", c))
                chain(dve.tensor_tensor(uext[:, c, 2:258], sg[:, c % 2, 0:TP], v[:, 0:TP], ALU.mult))
                drain(dve.tensor_tensor(us[:, c, :, 2:6], sg[:, c % 2, TP:T].rearrange("p (b k) -> p b k", b=B),
                                        v[:, TP:T].rearrange("p (b k) -> p b k", b=B), ALU.mult), ("v", c))
                settled()
                drained(dve, ("v", c))
                cw = [convw[:, C * k + c:C * k + c + 1] for k in range(3)]
                tp, tsm = tmp[:, c % 2, 0:TP], tmp[:, c % 2, TP:T].rearrange("p (b k) -> p b k", b=B)
                chain(dve.tensor_scalar(tp, uext[:, c, 0:256], cw[0], None, ALU.mult))
                chain(dve.tensor_scalar(tsm, us[:, c, :, 0:4], cw[0], None, ALU.mult))
                for k in (1, 2):
                    settled()
                    chain(dve.scalar_tensor_tensor(tp, uext[:, c, k:k + 256], cw[k], tp, ALU.mult, ALU.add))
                    chain(dve.scalar_tensor_tensor(tsm, us[:, c, :, k:k + 4], cw[k], tsm, ALU.mult, ALU.add))
                settled()
                full(dve, ("gb", c))
                drain(dve.tensor_tensor(zT[:, c, :], bank(("gb", c))[:, 0:T], tmp[:, c % 2, :], ALU.mult), ("gb", c))
            dve.tensor_copy(cstage[:, 0:16].rearrange("p (c k) -> p c k", c=C), uext[:, :, 256:258]).then_inc(conv_staged, 1)
            dve.tensor_copy(cstage[:, 16:144].rearrange("p (c b k) -> p c b k", c=C, b=B), us[:, :, :, 4:6]).then_inc(conv_staged, 1)

            def add_to_h(label, c, e=0, k=0):
                full(dve, label, e, k)
                drain(dve.tensor_tensor(hT[:, c, :], hT[:, c, :], bank(label, k)[:, 0:T], ALU.add), label, k)

            for c in range(C):
                add_to_h(("co", c), c)
            norm(1)

            def dense(turns):
                with dve.Fori(0, turns) as e:
                    for f in range(FC):
                        gl, ul = 2 * f, 2 * f + 1
                        L = ("f", 0, 0)
                        dve.wait_ge(sig_ready, f + 1 + FC * e)
                        s = sg[:, f % 2, :]
                        drain(dve.tensor_tensor(s, s, bank(L, gl)[:, 0:T], ALU.mult), L, gl)
                        drained(dve, L, e, gl)
                        full(dve, L, e, ul)
                        drain(dve.tensor_tensor(hff[:, f, :], s, bank(L, ul)[:, 0:T], ALU.mult), L, ul)
                    for c in range(C):
                        add_to_h(L, c, e, 2 * FC + c)

            def ple(layer, more=0):
                for c in range(C):
                    drained(dve, ("pg", layer, c), more)
                    full(dve, ("pp", layer, c), more)
                    s = sg[:, c % 2, :]
                    chain(dve.tensor_tensor(s, s, bank(("pp", layer, c))[:, 0:T], ALU.mult))
                    settled()
                    drain(dve.tensor_tensor(hT[:, c, :], hT[:, c, :], s, ALU.add), ("pp", layer, c))

            dense(HALVES)
            norm(2)
            ple(0)
            norm(3)

            def key_norm(c):
                scaled_by(("kss", c))
                drained(dve, ("kv", c))
                br = 1 + (c - 4) // 2
                dve.scalar_tensor_tensor(kn[:, c - 4, 0:TP], kvT[:, c, 0:TP], gk[:, br:br + 1], rs[:, c % 2, 0:TP],
                                         ALU.mult, ALU.mult).then_inc(kn_ready, 1)
                dve.tensor_tensor(kn[:, c - 4, TP:T], kvT[:, c, TP:T], rs[:, c % 2, TP:T], ALU.mult).then_inc(kn_ready, 1)

            for c in range(4, 8):
                key_norm(c)
            for j in range(8):
                scaled_by(("qss", j))
                drained(dve, ("q", j))
                dve.scalar_tensor_tensor(q1[:, j, :], qraw[:, j, :], gqs[:, :], rs[:, j % 2, :], ALU.mult, ALU.mult).then_inc(q_ready, 1)
            chain(dve.memset(QB, 0.0))
            settled()
            dve.wait_ge(q_ready, 8)
            for r in range(3):
                for a in range(2):
                    for g2 in range(2):
                        h = slice(64 * g2, 64 * g2 + 64)
                        dst = QB[h, r, :, a, 16 * g2:16 * g2 + 16].rearrange("p b (r t) -> p b r t", r=R)
                        src = q1[h, 4 * a:4 * a + 4, TP:T].rearrange("p r (b t) -> p b r t", b=B)
                        if r:
                            ins = dve.tensor_scalar(dst, src, gk[h, r:r + 1], None, ALU.mult)
                        else:
                            ins = dve.tensor_copy(dst, src)
                        ins.then_inc(qb_ready, 1)
            scaled_by(("kcps",))
            drained(dve, ("kcp",))
            dve.scalar_tensor_tensor(kcpn, kcp, gk[:, 0:1], rs[:, 0, 0:16].rearrange("p (a n) -> p a n", a=2),
                                     ALU.mult, ALU.mult).then_inc(kcn_ready, 1)
            drained(dve, ("gt",))

            def prompt_scores(u):
                w, j, g2 = u % 2, u // 2, u % 2
                head = (2 * (j // 4) + g2) * R + j % 4
                if u >= 2:
                    full(dve, ("ptp", u - 2, 1))
                for i in range(2):
                    nk = 128 * (i + 1)
                    full(dve, ("pl", u, i))
                    s = Sp[:, w, 256 * i:256 * i + 2 * nk].rearrange("p (r k) -> p r k", r=2)
                    drain(dve.tensor_tensor(s, bank(("pl", u, i))[:, 0:2 * nk].rearrange("p (r k) -> p r k", r=2),
                                            tabP[:, head, 256 - nk:256].unsqueeze(1).to_broadcast([128, 2, nk]), ALU.add),
                          ("pl", u, i))
                    drained(dve, ("pl", u, i))
                    chain(dve.tensor_reduce(nmp[:, w, i, 1:3], s, AX.X, ALU.max))
                    settled()
                    dve.tensor_scalar(nmp[:, w, i, 1:3], nmp[:, w, i, 1:3], -1.0, None, ALU.mult).then_inc(pmax_ready, 1)
                drain_bias = tabC[:, :, :, head]
                full(dve, ("pc", u))
                drain(dve.tensor_tensor(Scp[:, w, :, :], bank(("pc", u))[:, 0:16].rearrange("p (i n) -> p i n", i=2),
                                        drain_bias, ALU.add), ("pc", u))
                drained(dve, ("pc", u))
                chain(dve.tensor_reduce(nmp[:, w, :, 0], Scp[:, w, :, :], AX.X, ALU.max))
                settled()
                dve.tensor_scalar(nmp[:, w, :, 0], nmp[:, w, :, 0], -1.0, None, ALU.mult).then_inc(pmax_ready, 1)

            def prompt_scale(u):
                w, j, g2 = u % 2, u // 2, u % 2
                head = (2 * (j // 4) + g2) * R + j % 4
                dve.wait_ge(pexp_ready, 6 * (u + 1))
                chain(dve.reciprocal(scp[:, w], smp[:, w]))
                chain(dve.tensor_tensor(Scp[:, w], Scp[:, w], pmask, ALU.mult))
                settled()
                gates = gtok[:, 0:2, head:48:16]
                chain(dve.tensor_tensor(scp[:, w], scp[:, w], gates, ALU.mult))
                settled()
                for i in range(2):
                    nk = 128 * (i + 1)
                    for r in range(2):
                        o = 256 * i + r * nk
                        dve.tensor_scalar(Sp[:, w, o:o + nk], Sp[:, w, o:o + nk], scp[:, w, i, r + 1:r + 2], None,
                                          ALU.mult).then_inc(pscaled, 1)
                    dve.tensor_scalar(Scp[:, w, i, :], Scp[:, w, i, :], scp[:, w, i, 0:1], None,
                                      ALU.mult).then_inc(pscaled, 1)

            def prompt_out(u):
                j, g2 = u // 2, u % 2
                h = slice(64 * g2, 64 * g2 + 64)
                full(dve, ("po", u))
                drain(dve.tensor_copy(oT[h, j, 0:TP], bank(("po", u))[h, 0:TP]), ("po", u))

            for u in range(18):
                if u < 16:
                    prompt_scores(u)
                if 1 <= u <= 16:
                    prompt_scale(u - 1)
                if u >= 2:
                    prompt_out(u - 2)

            dve.wait_ge(gates_in, 16 * 4)
            for p in range(4):
                def soft(r, view, count):
                    chain(dve.tensor_reduce(mxs[:, r:r + 1], view, AX.X, ALU.max))
                    settled()
                    dve.tensor_scalar(mxs[:, r:r + 1], mxs[:, r:r + 1], -1.0, None, ALU.mult).then_inc(smax_ready, 1)

                def recip(r, count):
                    dve.wait_ge(sexp_ready, 3 * p + count)
                    chain(dve.reciprocal(fac[:, r:r + 1], sms[:, r:r + 1]))
                    settled()

                def gate(r):
                    chain(dve.tensor_tensor(fac[:, r:r + 1], fac[:, r:r + 1], grow[:, p, r:r + 1], ALU.mult))
                    settled()

                if p:
                    full(dve, ("pt", p - 1, 5))
                full(dve, ("sc", p))
                drain(dve.tensor_tensor(SC[:, :], bank(("sc", p))[:, 0:128], tCs[:, :], ALU.add), ("sc", p))
                drained(dve, ("sc", p))
                soft(0, SC[:, :], 1)
                full(dve, ("sn", p))
                sn = bank(("sn", p))
                chain(dve.tensor_tensor(S[:, KEYS:KEYS + 32], sn[:, 0:32], tN[:, p, :], ALU.add))
                drain(dve.tensor_tensor(SW[:, WIN:WIN + 32], sn[:, 32:64], tN[:, p, :], ALU.add), ("sn", p))
                recip(0, 1)
                dve.tensor_scalar(SC[:, :], SC[:, :], fac[:, 0:1], None, ALU.mult).then_inc(cprob_ready, 1)
                scaled_by(("wss", p))
                full(dve, ("wq", p))
                drain(dve.tensor_tensor(SW[:, 0:WIN], bank(("wq", p))[:, :], rsb[5 * p % 2], ALU.mult), ("wq", p))
                drained(dve, ("wq", p))
                chain(dve.tensor_tensor(SW[:, 0:WIN], SW[:, 0:WIN], tW[:, :], ALU.add))
                settled()
                drained(dve, ("sn", p))
                drained(dve, ("imp", p))
                chain(dve.tensor_tensor(half[:, :], SCg[:, 0:64], SCg[:, 64:128], ALU.add))
                settled()
                hv = half[:, :].rearrange("p (k m) -> p k m", m=2)
                chain(dve.tensor_tensor(score[:, :], hv[:, :, 0], hv[:, :, 1], ALU.add))
                settled()
                chain(dve.memset(score[:, 0:1], 1e4))
                chain(dve.memset(score[:, 31:32], 1e4))
                settled()
                soft(2, SW[:, :], 2)
                other = score[:, :].unsqueeze(1).to_broadcast([128, 32, 32])
                own = score[:, :].unsqueeze(2).to_broadcast([128, 32, 32])
                chain(dve.tensor_tensor(cnt1, other, own, ALU.is_gt))
                chain(dve.tensor_tensor(cnt2, other, own, ALU.is_equal))
                settled()
                chain(dve.tensor_tensor(cnt2, cnt2, tri, ALU.mult))
                settled()
                chain(dve.tensor_tensor(cnt1, cnt1, cnt2, ALU.add))
                settled()
                chain(dve.tensor_reduce(rank[:, :], cnt1, AX.X, ALU.add))
                settled()
                chain(dve.tensor_scalar(blkm[:, :], rank[:, :], 14.5, NEG, ALU.is_gt, ALU.mult))
                dve.tensor_scalar(SCg[:, :], SC[:, :], grow[:, p, 0:1], None, ALU.mult).then_inc(sscaled, 1)
                for t in range(4):
                    scaled_by(("sss", p, t))
                    full(dve, ("sq", p, t))
                    st = S[:, 512 * t:512 * t + 512]
                    drain(dve.tensor_tensor(st, bank(("sq", p, t))[:, :], rsb[(5 * p + 1 + t) % 2], ALU.mult), ("sq", p, t))
                    drained(dve, ("sq", p, t))
                    chain(dve.tensor_tensor(st, st, tS[:, 512 * t:512 * t + 512], ALU.add))
                    settled()
                    sv = st.rearrange("p (k m) -> p k m", k=8)
                    chain(dve.tensor_tensor(sv, sv, blkm[:, 8 * t:8 * t + 8].unsqueeze(2).to_broadcast([128, 8, 64]), ALU.add))
                settled()
                soft(1, S[:, :], 3)
                recip(2, 2)
                gate(2)
                dve.tensor_scalar(SW[:, :], SW[:, :], fac[:, 2:3], None, ALU.mult).then_inc(sscaled, 1)
                recip(1, 3)
                gate(1)
                dve.tensor_scalar(S[:, :], S[:, :], fac[:, 1:2], None, ALU.mult).then_inc(sscaled, 1)
            dve.wait_ge(values_used, 40)
            for a in range(2):
                for g2 in range(2):
                    h = slice(64 * g2, 64 * g2 + 64)
                    src = oP[a][h, 0:32 * B].rearrange("p (b g r t) -> p g b r t", b=B, g=2, r=R)[:, g2]
                    dst = oT[h, 4 * a:4 * a + 4, TP:T].rearrange("p r (b t) -> p b r t", b=B)
                    dve.tensor_copy(dst, src).then_inc(so_ready, 1)
            for c in range(C):
                add_to_h(("wo", c), c)
            norm(4)

            chain(dve.memset(rl, 0.0))
            settled()
            full(dve, ("rt",))
            chain(dve.tensor_copy(rl[:, 0:2, :], bank(("rt",))[:, 0:16].rearrange("p (i e) -> p i e", i=2)))
            drain(dve.tensor_copy(rl[0:32, 2, :], bank(("rt",))[0:32, 16:24]), ("rt",))
            settled()
            drained(dve, ("rt",))
            chain(dve.tensor_reduce(rmx[:, :], rl, AX.X, ALU.max))
            settled()
            dve.tensor_scalar(rmx[:, :], rmx[:, :], -1.0, None, ALU.mult).then_inc(rmax_ready, 1)
            for i in range(3):
                other = rl[:, i, :].unsqueeze(1).to_broadcast([128, 8, 8])
                own = rl[:, i, :].unsqueeze(2).to_broadcast([128, 8, 8])
                chain(dve.tensor_tensor(cmp8[0], other, own, ALU.is_gt))
                chain(dve.tensor_tensor(cmp8[1], other, own, ALU.is_equal))
                settled()
                chain(dve.tensor_tensor(cmp8[1], cmp8[1], tri[:, 0:8, 0:8], ALU.mult))
                settled()
                chain(dve.tensor_tensor(cmp8[0], cmp8[0], cmp8[1], ALU.add))
                settled()
                chain(dve.tensor_reduce(rk[:, i, :], cmp8[0], AX.X, ALU.add))
                settled()
            dve.memset(ones1[:, :], 1.0).then_inc(routed_ready, 1)
            dve.tensor_scalar(routed, rk, 1.5, None, ALU.is_lt).then_inc(routed_ready, 1)
            dve.memset(scat, 0.0).then_inc(item_cleared, 1)
            dve.memset(ye, 0.0).then_inc(item_cleared, 1)
            dve.wait_ge(rexp_ready, 3)
            dve.wait_ge(routed_ready, 2)
            chain(dve.tensor_tensor(rg, routed, rg, ALU.mult))
            settled()
            chain(dve.tensor_reduce(rsm[:, :], rg, AX.X, ALU.add))
            settled()
            chain(dve.reciprocal(rsm[:, :], rsm[:, :]))
            settled()
            chain(dve.tensor_tensor(rg, rg, rsm[:, :].unsqueeze(2).to_broadcast([128, 3, 8]), ALU.mult))
            full(dve, ("pos",))
            pos = bank(("pos",))
            chain(dve.scalar_tensor_tensor(pos1[:, 0:2, :], pos[:, 0:16].rearrange("p (i e) -> p i e", i=2), 1.0,
                                           routed[:, 0:2, :], ALU.add, ALU.mult))
            chain(dve.scalar_tensor_tensor(pos1[0:32, 2, :], pos[0:32, 16:24], 1.0, routed[0:32, 2, :], ALU.add, ALU.mult))
            dve.wait_ge(route_in, 16 * 3)
            drain(dve.tensor_tensor(over.rearrange("p (s e) -> p s e", e=8),
                                    pos[0:1, 24:32].unsqueeze(1).to_broadcast([1, SPLITS - 1, 8]),
                                    xthr.rearrange("p (s e) -> p s e", e=8), ALU.is_gt), ("pos",))
            drained(dve, ("pos",))
            chain(dve.tensor_tensor(osq, over.unsqueeze(1).to_broadcast([1, NX, NX]), tri[0:1, 0:NX, 0:NX], ALU.mult))
            chain(dve.tensor_reduce(okey[:, 0:1], over, AX.X, ALU.add))
            settled()
            for j in range(2):
                chain(dve.tensor_scalar(items_f[:, 2 * NI + j:2 * NI + j + 1], okey[:, 0:1], float(EXPERTS - j), None, ALU.add))
            settled()
            chain(dve.tensor_reduce(okey, osq, AX.X, ALU.add))
            settled()
            chain(dve.scalar_tensor_tensor(okey, okey, float(EXPERTS + 1), over, ALU.add, ALU.mult))
            settled()
            chain(dve.tensor_tensor(ohit, okey.unsqueeze(1).to_broadcast([1, NI, NX]),
                                    slot1.unsqueeze(2).to_broadcast([1, NI, NX]), ALU.is_equal))
            settled()
            for row, value in enumerate((xe, xs)):
                chain(dve.tensor_tensor(oval, ohit, value.unsqueeze(1).to_broadcast([1, NI, NX]), ALU.mult))
                settled()
                chain(dve.tensor_reduce(items_f[:, NI * row:NI * row + NI], oval, AX.X, ALU.add))
                settled()
            chain(dve.tensor_tensor(items_f[:, 0:NI], items_f[:, 0:NI], e0, ALU.add))
            settled()
            dve.tensor_copy(items[:, :], items_f).then_inc(items_ready, 1)

            n_items, more = item_count(dve)
            with dve.Fori(0, n_items) as i:
                M = ("m", 0)
                e = item_value(dve, 0, i, EXPERTS - 1)
                split = item_value(dve, 1, i, SPLITS - 1)
                numbers = count[:, bass.ds(split * CAP, CAP)]
                for k in range(3):
                    n = 128 if k < 2 else 32
                    dve.tensor_scalar(pick[0:n, k, :], numbers[0:n], pos1[0:n, k, bass.ds(e, 1)], None,
                                      ALU.is_equal).then_inc(picks_ready, 1)
                for k in range(3):
                    n = 128 if k < 2 else 32
                    dve.tensor_scalar(wpick[0:n, k, :], numbers[0:n], pos1[0:n, k, bass.ds(e, 1)], rg[0:n, k, bass.ds(e, 1)],
                                      ALU.is_equal, ALU.mult).then_inc(picks_ready, 1)
                for c in range(C):
                    add_to_h(M, c, i, M_SCAT + c)
                for f in range(FC):
                    dve.wait_ge(sig_ready, HALVES * FC + f + 1 + FC * i)
                    g = bank(M, M_GU + f)
                    chain_ready = dve.tensor_tensor(sige[:, f, :], sige[:, f, :], g[:, 0:CAP], ALU.mult)
                    chain_ready.then_inc(silu_ready, 1)
                    dve.wait_ge(silu_ready, f + 1 + FC * i)
                    drain(dve.tensor_tensor(he[:, f, :], sige[:, f, :], g[:, CAP:2 * CAP], ALU.mult), M, M_GU + f)
            for c in range(C):
                add_to_h(("fs", c), c, more)
            norm(5)
            ple(1, more)

        @block.tensor
        def _(pe):
            def g_linear(label, rhs, e=0, k=0, ready=None):
                g_arrived(pe, label, e, k)
                bank_free(pe, label, e, k)
                tile = gslot(label, k)
                for i in range(C):
                    if ready is not None:
                        pe.wait_ge(a_ready, ready + i + 1)
                    ins = pe.matmul(bank(label, k)[:, 0:T], tile[:, 128 * i:128 * i + 128], rhs[:, i, :],
                                    start=i == 0, stop=i == C - 1)
                fill(ins, label, k)

            def norm(i, more=0):
                label = ("norm", i)
                bank_free(pe, label, more)
                for c in range(C):
                    pe.wait_ge(sq_ready, C * i + c + 1)
                    ins = pe.matmul(bank(label)[:, 0:T], ones[:, :], sqs[i][:, c, :], start=c == 0, stop=c == C - 1)
                fill(ins, label)

            pe.wait_ge(tables_in, 16 * NTABLE)
            pe.wait_ge(rb_mask, 1)
            for i in range(8):
                bank_free(pe, ("tp", i))
                for k in range(32):
                    y = 383 - (32 * i + k)
                    ins = pe.matmul(bank(("tp", i))[:, 16 * k:16 * k + 16], ohv[:, y:y + 128], rbx, start=True, stop=True)
                fill(ins, ("tp", i))
            bank_free(pe, ("tc",))
            for i in range(2):
                for n in range(8):
                    y = 128 * i - 32 * n - 31 + 255
                    ins = pe.matmul(bank(("tc",))[:, 16 * (8 * i + n):16 * (8 * i + n) + 16], ohv[:, y:y + 128], rbx,
                                    start=True, stop=True)
            fill(ins, ("tc",))
            pe.wait_ge(lt_in, 16 * 8)
            for i in range(6):
                n = 512 if i < 5 else 160
                bank_free(pe, ("ts", i))
                fill(pe.matmul(bank(("ts", i))[:, 0:n], lt, ohs[i // 4][:, 512 * (i % 4):512 * (i % 4) + n], start=True, stop=True), ("ts", i))

            pe.wait_ge(wcmp_in, 16 * 4)
            for b in range(B):
                pe.wait_ge(c_in[b % 2], 16 * PAGES * (b // 2 + 1))
                src = cbufs[b % 2].rearrange("p (i c g l n) -> p i c g l n", i=PAGES, c=2, g=GROUPS, l=16)
                for c, name in enumerate(("ck", "cv")):
                    bank_free(pe, (name, b))
                    for g in range(GROUPS):
                        h, a = 64 * (g % 2), g // 2
                        for l in range(16):
                            ins = pe.matmul(bank((name, b))[h:h + 64, NB * a:NB * a + NB], wc[:, 64 * c + 16 * g + l, :],
                                            src[:, :, c, g, l, :], start=l == 0, stop=l == 15)
                    fill(ins, (name, b))
            pe.wait_ge(consts_in, 16 * NCONST)
            for a in range(2):
                bank_free(pe, ("css", a))
                drained(pe, ("ck", 7))
                fill(pe.matmul(bank(("css", a))[:, :], bones[:, :], kcsq[:, a, :], start=True, stop=True), ("css", a))

            drained(pe, ("cv", 6))
            drained(pe, ("cv", 7))
            for p in range(4):
                bank_free(pe, ("ct", p))
                for a in range(2):
                    ins = pe.transpose(bank(("ct", p))[:, 128 * a:128 * a + 128], vraw[:, a, 128 * p:128 * p + 128], ident[:, :])
                fill(ins, ("ct", p))

            norm(0)
            for c in range(C):
                for name in ("gc", "v", "gb"):
                    g_linear((name, c), aT, ready=0 if c == 0 and name == "gc" else None)
            for c in range(C):
                if c == 0:
                    for k in range(C):
                        drained(pe, ("gb", k))
                g_linear(("co", c), zT)
            norm(1)

            def dense(turns, ready):
                pe.wait_ge(a_ready, ready)
                with pe.Fori(0, turns) as e:
                    L = ("f", 0, 0)
                    for k in range(2 * FC):
                        g_linear(L, aT, e, k)
                    for c in range(C):
                        n = c
                        pe.wait_ge(d_in[n % DS], 16 * (n // DS + 1) + 16 * (C // DS) * e)
                        tile = dring[:, (n % DS) * DT:(n % DS + 1) * DT]
                        bank_free(pe, L, e, 2 * FC + c)
                        for f in range(FC):
                            if c == 0:
                                drained(pe, L, e, 2 * f + 1)
                            ins = pe.matmul(bank(L, 2 * FC + c)[:, 0:T], tile[:, 128 * f:128 * f + 128], hff[:, f, :],
                                            start=f == 0, stop=f == FC - 1)
                        fill(ins, L, 2 * FC + c)

            def ple(layer, ready, more=0):
                for c in range(C):
                    g_arrived(pe, ("pp", layer, c // 4), more)
                    g_linear(("pg", layer, c), aT, more, ready=ready if c == 0 else None)
                    bank_free(pe, ("pp", layer, c), more)
                    tile = gslot(("pp", layer, c // 4))
                    for k in range(2):
                        o = (2 * (c % 4) + k) * 128
                        ins = pe.matmul(bank(("pp", layer, c))[:, 0:T], tile[:, o:o + 128], pT[:, layer, k, :],
                                        start=k == 0, stop=k == 1)
                    fill(ins, ("pp", layer, c))

            dense(HALVES, 2 * C)
            norm(2)
            ple(0, 2 * C)
            norm(3)

            def block_sums(label, n):
                bank_free(pe, label)
                pe.wait_ge(hsq_ready, n + 1)
                fill(pe.matmul(bank(label)[:, 0:T], bones[:, :], tmp[:, n % 2, :], start=True, stop=True), label)

            for c in range(8):
                g_linear(("kv", c), aT, ready=3 * C if c == 0 else None)
                if c > 4:
                    block_sums(("kss", c - 1), c - 5)
            for i in range(3):
                bank_free(pe, ("vt", i))
            for q in range(4):
                g_arrived(pe, ("vt", q))
                tile = gslot(("vt", q))
                for k in range(2):
                    for i in range(3):
                        n = 128 if i < 2 else 32
                        ins = pe.matmul(bank(("vt", i))[0:n, :], aT[:, 2 * q + k, 128 * i:128 * i + n],
                                        tile[:, 512 * k:512 * k + 512], start=q == 0 and k == 0, stop=q == 3 and k == 1)
                        if q == 3 and k == 1:
                            fill(ins, ("vt", i))
            block_sums(("kss", 7), 3)
            bank_free(pe, ("gt",))
            for i in range(3):
                n = 128 if i < 2 else 32
                for c in range(C):
                    ins = pe.matmul(bank(("gt",))[0:n, 48 * i:48 * i + 48], aT[:, c, 128 * i:128 * i + n], wgate[:, c, :],
                                    start=c == 0, stop=c == C - 1)
            fill(ins, ("gt",))
            for j in range(8):
                g_linear(("q", j), aT)
                if j:
                    block_sums(("qss", j - 1), 4 + j - 1)
            pe.wait_ge(kvp_in, 16 * 16)
            bank_free(pe, ("kcp",))
            for g in range(GROUPS):
                h, a = 64 * (g % 2), g // 2
                for l in range(16):
                    ins = pe.matmul(bank(("kcp",))[h:h + 64, 8 * a:8 * a + 8], wc[:, 16 * g + l, :], kvp[:, g, 2 * l:TP:32],
                                    start=l == 0, stop=l == 15)
            fill(ins, ("kcp",))
            block_sums(("qss", 7), 11)
            bank_free(pe, ("vcp",))
            for g in range(GROUPS):
                for l in range(16):
                    ins = pe.matmul(bank(("vcp",))[0:8, 64 * g:64 * g + 64], kvp[:, 4 + g, 2 * l:TP:32], wc[:, 64 + 16 * g + l, :],
                                    start=l == 0, stop=l == 15)
            fill(ins, ("vcp",))
            bank_free(pe, ("kcps",))
            pe.wait_ge(hsq_ready, 13)
            fill(pe.matmul(bank(("kcps",))[:, 0:16], bones[:, :], tmp_[:, 0:16], start=True, stop=True), ("kcps",))

            pe.wait_ge(kn_ready, 8)
            pe.wait_ge(q_ready, 8)
            pe.wait_ge(kcn_ready, 3)
            for u in range(17):
                if u < 16:
                    j, g2 = u // 2, u % 2
                    a = j // 4
                    h = slice(64 * g2, 64 * g2 + 64)
                    bank_free(pe, ("pc", u))
                    for i in range(2):
                        ins = pe.matmul(bank(("pc", u))[:, 8 * i:8 * i + 8], q1[h, j, 128 * i:128 * i + 128], kcpn[h, a, :],
                                        start=True, stop=True)
                    fill(ins, ("pc", u))
                    for i in range(2):
                        nk = 128 * (i + 1)
                        bank_free(pe, ("pl", u, i))
                        for r in range(2):
                            ins = pe.matmul(bank(("pl", u, i))[:, r * nk:(r + 1) * nk], q1[h, j, 128 * i:128 * i + 128],
                                            kn[h, 2 * r + a, 0:nk], start=True, stop=True)
                        fill(ins, ("pl", u, i))
                if u:
                    v = u - 1
                    w, j, g2 = v % 2, v // 2, v % 2
                    g = 2 * (j // 4) + g2
                    pe.wait_ge(pscaled, 6 * (v + 1))
                    bank_free(pe, ("ptc", v))
                    for i in range(2):
                        ins = pe.transpose(bank(("ptc", v))[0:8, 128 * i:128 * i + 128], Scp[:, w, i, :], ident[:, :])
                    fill(ins, ("ptc", v))
                    for i in range(2):
                        bank_free(pe, ("ptp", v, i))
                        for k in range(2 * (i + 1)):
                            ins = pe.transpose(bank(("ptp", v, i))[:, 128 * k:128 * k + 128],
                                               Sp[:, w, 256 * i + 128 * k:256 * i + 128 * k + 128], ident[:, :])
                        fill(ins, ("ptp", v, i))
                    bank_free(pe, ("po", v))
                    drained(pe, ("ptc", v))
                    drained(pe, ("ptp", v, 0))
                    drained(pe, ("ptp", v, 1))
                    drained(pe, ("vcp",))
                    o = bank(("po", v))
                    h = slice(64 * g2, 64 * g2 + 64)
                    for r in range(2):
                        pe.matmul(o[h, 0:256], vtok[:, 0, 256 * r + 64 * g:256 * r + 64 * g + 64], PTp[:, w, r, 0:256],
                                  start=r == 0, stop=False)
                        pe.matmul(o[h, 128:256], vtok[:, 1, 256 * r + 64 * g:256 * r + 64 * g + 64], PTp[:, w, r, 256:384],
                                  start=False, stop=False)
                    fill(pe.matmul(o[h, 0:256], vcp[:, 64 * g:64 * g + 64], PTc[:, w, :], start=False, stop=True), ("po", v))

            pe.wait_ge(qb_ready, 12)
            for p in range(4):
                def rows(b2, a):
                    return slice(64 * b2 + 32 * a, 64 * b2 + 32 * a + 32)

                bank_free(pe, ("sc", p))
                for b2 in range(2):
                    for a in range(2):
                        ins = pe.matmul(bank(("sc", p))[rows(b2, a), 0:128], QB[:, 0, 2 * p + b2, a, :],
                                        kcn[:, a, 128 * p:128 * p + 128], start=True, stop=True)
                fill(ins, ("sc", p))
                bank_free(pe, ("sn", p))
                for b2 in range(2):
                    for a in range(2):
                        for r in range(2):
                            ins = pe.matmul(bank(("sn", p))[rows(b2, a), 32 * r:32 * r + 32], QB[:, 1 + r, 2 * p + b2, a, :],
                                            kn[:, 2 * r + a, TP:T], start=True, stop=True)
                fill(ins, ("sn", p))

                def key_tile(q, s, tile, n, b2, r, view, last):
                    pe.wait_ge(ksq_ready, 10 * p + n + 1)
                    g_arrived(pe, tile)
                    for a in range(2):
                        i1 = pe.matmul(bank(q)[rows(b2, a), :], QB[:, r, 2 * p + b2, a, :], view(gslot(tile), a),
                                       start=True, stop=True)
                        i2 = pe.matmul(bank(s)[rows(b2, a), :], bo32[:, :], view(ksq[:, n % 2, :], a), start=True, stop=True)
                        if a == 0:
                            continue
                        if last:
                            fill(i1, q)
                            fill(i2, s)
                        else:
                            i2.then_inc(keys_used, 1)

                def win_view(t, a):
                    return t[:, 512 * a:512 * a + 512]

                def page_view(t, a):
                    return t.rearrange("p (i a n) -> p i a n", i=4, a=2)[:, :, a, :]

                bank_free(pe, ("wq", p))
                bank_free(pe, ("wss", p))
                for b2 in range(2):
                    key_tile(("wq", p), ("wss", p), ("wk", p, b2), b2, b2, 2, win_view, b2 == 1)
                bank_free(pe, ("imp", p))
                pe.wait_ge(cprob_ready, p + 1)
                fill(pe.matmul(bank(("imp", p))[:, 0:128], rsum[:, :], SC[:, :], start=True, stop=True), ("imp", p))
                for t in range(4):
                    bank_free(pe, ("sq", p, t))
                    bank_free(pe, ("sss", p, t))
                    for b2 in range(2):
                        key_tile(("sq", p, t), ("sss", p, t), ("sk", p, t, b2), 2 + 2 * t + b2, b2, 1, page_view, b2 == 1)
                pe.wait_ge(sscaled, 3 * p + 2)
                for i in range(6):
                    if i == 1:
                        pe.wait_ge(sscaled, 3 * p + 3)
                    bank_free(pe, ("pt", p, i))
                    o = bank(("pt", p, i))
                    if i == 0:
                        parts = [(0, SCg[:, :])] + [(128 * (k + 1), SW[:, 128 * k:128 * k + 128]) for k in range(3)]
                    elif i == 1:
                        parts = [(0, SW[:, 384:512]), (128, SW[:, 512:544]), (256, S[:, KEYS:KEYS + 32])]
                    else:
                        parts = [(128 * k, S[:, 512 * (i - 2) + 128 * k:512 * (i - 2) + 128 * k + 128]) for k in range(4)]
                    for col, src in parts:
                        n = src.shape[1]
                        ins = pe.transpose(o[0:n, col:col + 128], src, ident[:, :])
                    fill(ins, ("pt", p, i))
                for i in range(6):
                    drained(pe, ("pt", p, i))

                for b2 in range(2):
                    b = 2 * p + b2

                    def values(k, v, first=False, last=False, parts=128):
                        for a in range(2):
                            ins = pe.matmul(oP[a][:, 32 * b:32 * b + 32], v[0:parts, 128 * a:128 * a + 128],
                                            PT[0:parts, k, rows(b2, a)], start=first, stop=last)
                        return ins

                    values(0, vcs[:, p, :], first=True)
                    values(5, vtok[:, 2, 256:512], parts=32)
                    values(6, vtok[:, 2, 0:256], parts=32)
                    g_arrived(pe, ("wv", p, b2))
                    for k in range(4):
                        ins = values(1 + k, gslot(("wv", p, b2))[:, 256 * k:256 * k + 256])
                    ins.then_inc(values_used, 1)
                    for t in range(4):
                        pe.wait_ge(v_in[4 * b2 + t], 64 * (p + 1))
                        for k in range(4):
                            ins = values(7 + 4 * t + k, vbufs[4 * b2 + t][:, 256 * k:256 * k + 256], last=t == 3 and k == 3)
                        ins.then_inc(values_used, 1)

            pe.wait_ge(so_ready, 4)
            drained(pe, ("po", 15))
            for c in range(C):
                g_linear(("wo", c), oT)
            norm(4)
            bank_free(pe, ("rt",))
            pe.wait_ge(a_ready, 5 * C)
            for i in range(3):
                n = 128 if i < 2 else 32
                for c in range(C):
                    ins = pe.matmul(bank(("rt",))[0:n, 8 * i:8 * i + 8], aT[:, c, 128 * i:128 * i + n], rout[:, c, :],
                                    start=c == 0, stop=c == C - 1)
            fill(ins, ("rt",))
            for k in range(6):
                i, h, n = k // 2, k % 2, 128 if k < 4 else 32
                bank_free(pe, ("at", k))
                for c in range(4):
                    ins = pe.transpose(bank(("at", k))[0:n, 128 * c:128 * c + 128], aT[:, 4 * h + c, 128 * i:128 * i + n], ident[:, :])
                fill(ins, ("at", k))
            pe.wait_ge(routed_ready, 2)
            pe.wait_ge(route_in, 16 * 3)
            bank_free(pe, ("pos",))
            for i in range(4):
                n = 32 if i == 2 else 128
                terms = [(ones1[:, 0:n], routed[:, j, :]) for j in range(min(i, 2))]
                terms += [(before[0:n, 0:n], routed[0:n, i, :])] if i < 3 else [(ones1[0:32, :], routed[0:32, 2, :])]
                for j, (w, r) in enumerate(terms):
                    ins = pe.matmul(bank(("pos",))[0:n, 8 * i:8 * i + 8], w, r, start=j == 0, stop=j == len(terms) - 1)
            fill(ins, ("pos",))
            for k in range(6):
                drained(pe, ("at", k))

            n_items, more = item_count(pe)
            pe.wait_ge(item_cleared, 2)
            M = ("m", 0)

            def scatter(label, k, e):
                for c in range(C):
                    bank_free(pe, label, e, k + c)
                    fill(pe.matmul(bank(label, k + c)[:, 0:T], ye[:, 128 * c:128 * c + 128], scat, start=True, stop=True),
                         label, k + c)

            with pe.Fori(0, n_items) as i:
                for h in range(2):
                    bank_free(pe, M, i, h)
                    for c in range(4 * h, 4 * h + 4):
                        for k in range(3):
                            n = 128 if k < 2 else 32
                            if c == 0:
                                pe.wait_ge(picks_ready, k + 1 + 6 * i)
                            ins = pe.matmul(bank(M, h)[:, CAP * (c % 4):CAP * (c % 4) + CAP], atok[0:n, k, 128 * c:128 * c + 128],
                                            pick[0:n, k, :], start=k == 0, stop=k == 2)
                    fill(ins, M, h)
                for k in (M_DOWN, M_DOWN + 1):
                    drained(pe, M, i, k - MR)
                scatter(M, M_SCAT, i)
                bank_free(pe, M, i, M_SEL)
                pe.wait_ge(picks_ready, 6 + 6 * i)
                for k in range(3):
                    n = 128 if k < 2 else 32
                    ins = pe.transpose(bank(M, M_SEL)[0:CAP, 128 * k:128 * k + n], wpick[0:n, k, :], ident[0:n, 0:n])
                fill(ins, M, M_SEL)
                for h in range(2):
                    drained(pe, M, i, h)
                for f in range(FC):
                    bank_free(pe, M, i, M_GU + f)
                    for u in range(2):
                        g_arrived(pe, M, i, 2 * f + u)
                        for c in range(C):
                            ins = pe.matmul(bank(M, M_GU + f)[:, CAP * u:CAP * u + CAP],
                                            gslot(M, 2 * f + u)[:, 128 * c:128 * c + 128], ae[:, c, :], start=c == 0, stop=c == C - 1)
                    fill(ins, M, M_GU + f)
                for h in range(2):
                    bank_free(pe, M, i, M_DOWN + h)
                for f in range(FC):
                    if f:
                        drained(pe, M, i, M_GU + f)
                    g_arrived(pe, M, i, 2 * FC + f)
                    for h in range(2):
                        ins = pe.matmul(bank(M, M_DOWN + h)[0:CAP, :], he[:, f, :], gslot(M, 2 * FC + f)[:, 512 * h:512 * h + 512],
                                        start=f == 0, stop=f == FC - 1)
                        if f == FC - 1:
                            fill(ins, M, M_DOWN + h)
                    if f < FC - 1:
                        ins.then_inc(down_used, 1)
            for k in (M_DOWN, M_DOWN + 1):
                drained(pe, M, more, k)
            scatter(("fs", 0), 0, more)
            norm(5, more)
            ple(1, 5 * C, more)


def constants():
    f = np.float32
    eye = np.eye(128, dtype=f)
    k = {"ident": eye, "ones": np.full((128, 128), 1.0 / D, f)}
    half = np.arange(128) // 64
    k["bones"] = (half[:, None] == half[None, :]).astype(f) / f(HD)
    k["bo32"] = (half[:, None] == (np.arange(32) // 16)[None, :]).astype(f) / f(HD)
    row = np.arange(128)
    b2, head, step = row // 64, row // 4 % 16, row % 4
    key = (b2 * 4 + head // R) * 4 + step
    k["rsum"] = (key[:, None] == key[None, :]).astype(f)
    i = np.arange(32)
    k["tri"] = np.ascontiguousarray(np.broadcast_to((i[None, :] < i[:, None]).astype(f), (128, 32, 32)))
    q = np.arange(256).reshape(2, 128).T
    k["pmask"] = (q[:, :, None] >= np.arange(8) * 32 + 31).astype(f)
    k["before"] = np.triu(np.ones((128, 128), f), 1)
    k["count"] = np.tile(np.arange(1, T + 1, dtype=f), (128, 1))
    s, e = np.divmod(np.arange(EXPERTS * (SPLITS - 1)), EXPERTS)
    slot = np.arange(EXPERTS * SPLITS)
    k["xtab"] = np.concatenate([CAP * (s + 1), e, s + 1, slot + 1, np.where(slot < EXPERTS, slot, 0)]).astype(f)[None]
    dist = np.arange(OHL) - 255
    oh = np.zeros((BUCKETS + 1, OHL), f)
    oh[np.where(dist < 0, BUCKETS, bucket(dist)), np.arange(OHL)] = 1
    k["ohv"] = oh
    t = np.arange(STEPS)[:, None]
    new = np.tile(np.arange(STEPS), B)
    ends = np.tile((np.arange(NB) + 1) * 32 - 1, 2)
    rel = np.concatenate([KEYS + t - np.arange(KEYS), KEYS + t - (KEYS - WIN + np.arange(WIN)),
                          np.maximum(t - new, 0), KEYS + t - ends], axis=1)
    k["ohs"] = (bucket(rel)[:, None, :] == np.arange(BUCKETS)[None, :, None]).astype(f).reshape(128, -1)
    m = np.zeros((128, 768), bool)
    m[:, 0:WIN] = WIN + step[:, None] - np.arange(WIN) < WIN
    tok = np.arange(32)
    for p in range(4):
        m[:, WIN + 32 * p:WIN + 32 * p + 32] = (tok // 4 == 2 * p + b2[:, None]) & (tok % 4 <= step[:, None])
    m[:, 640:768] = np.arange(128) // NB == b2[:, None]
    k["masks"] = np.where(m, f(0), f(NEG))
    return k


def kernel(x_prompt, x_sample, state_conv, cache_cmp, cache_sel, state_win, page_table, p_prompt, p_sample, norm_mix,
           norm_ffn, norm_ple, conv_w_in, conv_w, conv_w_out, nsa_w_in, nsa_w_cmp, nsa_q_norm, nsa_k_norm, nsa_w_out,
           rel_bias, ffn_w_gate, ffn_w_up, ffn_w_down, moe_router, moe_w_gate, moe_w_up, moe_w_down, ple_w_proj, ple_w_gate):
    import concourse.bacc as bacc
    from concourse.bass_utils import run_bass_kernel_spmd

    def chunks(w):
        w = np.asarray(w)
        return w.reshape(w.shape[0] // 128, 128, w.shape[1] // 128, 128).transpose(2, 1, 0, 3).reshape(w.shape[1] // 128, 128, -1)

    def features(a):
        a = np.asarray(a)
        return a.reshape(a.shape[0], -1, 128).transpose(2, 1, 0)

    def gate_up(g, u):
        g, u = chunks(g), chunks(u)
        return np.stack([g, u], axis=1).reshape(2 * g.shape[0], 128, -1)

    a = {k: np.asarray(v) for k, v in constants().items()}
    x = np.concatenate([np.asarray(x_prompt).reshape(TP, D), np.asarray(x_sample).reshape(32, D)])
    a["x"] = features(x)
    p = np.concatenate([np.asarray(p_prompt).reshape(2, TP, 256), np.asarray(p_sample).reshape(2, 32, 256)], axis=1)
    a["p"] = np.stack([features(p[0]), features(p[1])], axis=1)
    a["state"] = np.asarray(state_conv)[0].reshape(B, 2, C, 128).transpose(3, 2, 0, 1)
    order = [norm_mix[0], norm_ffn[0], norm_ple[0], norm_mix[1], norm_ffn[1], norm_ple[1]]
    a["gains"] = np.concatenate([np.asarray(g).reshape(C, 128).T for g in order], axis=1)
    a["convw"] = np.asarray(conv_w)[0].reshape(3, C, 128).transpose(2, 0, 1).reshape(128, 24)
    a["gq"] = np.tile(np.asarray(nsa_q_norm)[0], 2).reshape(128, 1)
    a["gk"] = np.tile(np.asarray(nsa_k_norm)[0], (1, 2)).T
    a["rel_bias"] = np.asarray(rel_bias)
    w = chunks(np.asarray(conv_w_in)[0]).reshape(3, C, 128, 1024)
    a["conv_in"] = w[[1, 2, 0]].transpose(1, 0, 2, 3).reshape(3 * C, 128, 1024)
    a["conv_out"] = chunks(np.asarray(conv_w_out)[0])
    g, u, d = (np.asarray(t)[0] for t in (ffn_w_gate, ffn_w_up, ffn_w_down))
    a["dense_gu"] = np.stack([gate_up(g[:, FE * i:FE * i + FE], u[:, FE * i:FE * i + FE]) for i in range(HALVES)])
    a["dense_down"] = np.stack([chunks(d[FE * i:FE * i + FE]) for i in range(HALVES)])
    g, u, d = (np.asarray(t)[0] for t in (moe_w_gate, moe_w_up, moe_w_down))
    a["moe"] = np.stack([np.concatenate([gate_up(g[e], u[e]), d[e].reshape(FC, 128, D)]) for e in range(EXPERTS)])
    a["ple_gate"] = np.stack([chunks(t) for t in np.asarray(ple_w_gate)])
    a["ple_proj"] = np.stack([chunks(t).reshape(2, 4, 128, 256).transpose(0, 2, 1, 3).reshape(2, 128, 1024)
                              for t in np.asarray(ple_w_proj)])
    w = np.asarray(nsa_w_in)[0]
    q = w[:, :1024].reshape(D, 2, 2, R, HD).transpose(0, 1, 3, 2, 4).reshape(D, 1024)
    a["nsa_q"] = chunks(q)
    kv = w[:, 1024:2560].reshape(D, 3, 4, 2, HD)
    cols = [kv[:, 0, :, 0], kv[:, 0, :, 1], kv[:, 1, :, 0], kv[:, 2, :, 0]]
    a["nsa_kv"] = chunks(np.concatenate([t.reshape(D, 256) for t in cols], axis=1))
    vt = kv[:, 1:3, :, 1].reshape(4, 2, 128, 512)
    a["nsa_vt"] = vt.transpose(0, 2, 1, 3).reshape(4, 128, 1024)
    a["wgate"] = w[:, 2560:].reshape(C, 128, 48).transpose(1, 0, 2)
    a["rout"] = np.asarray(moe_router)[0].reshape(C, 128, 8).transpose(1, 0, 2)
    wo = np.asarray(nsa_w_out)[0].reshape(2, 2, R, HD, D).transpose(0, 2, 1, 3, 4).reshape(1024, D)
    a["nsa_out"] = chunks(wo)
    a["w_cmp"] = np.asarray(nsa_w_cmp)[0].reshape(16, 2, 4, 2, HD, HD).transpose(1, 4, 3, 2, 0, 5).reshape(128, 128, 64)
    c = np.asarray(cache_cmp)[0].reshape(POOL, 4, 16, 2, 4, 2, HD)
    a["cache_cmp"] = c.transpose(0, 3, 6, 5, 4, 2, 1).reshape(POOL, 128, 512)
    c = np.asarray(cache_sel)[0]
    a["cache_selk"] = c[:, :, :, 0].reshape(POOL, 128, 2, 2, HD).transpose(0, 3, 4, 2, 1).reshape(POOL, 128, 256)
    a["cache_selv"] = c[:, :, :, 1].reshape(POOL, 128, 256)
    c = np.asarray(state_win)[0]
    a["win_k"] = c[:, :, :, 0].reshape(B, WIN, 2, 2, HD).transpose(0, 3, 4, 2, 1).reshape(B, 128, 1024)
    a["win_v"] = c[:, :, :, 1].reshape(B, 4, 128, 256).transpose(0, 2, 1, 3).reshape(B, 128, 1024)
    a["state_win"] = c.reshape(B, WIN, 512)
    a["page_table"] = np.asarray(page_table).reshape(1, B * PAGES)

    nc = bacc.Bacc("TRN2", target_bir_lowering=False, num_devices=1)
    arrays, A, O = {}, {}, {}
    for name, v in a.items():
        v = np.ascontiguousarray(v)
        arrays["in_" + name] = v
        A[name] = nc.dram_tensor("in_" + name, v.shape, mybir.dt.from_np(v.dtype), kind="ExternalInput").ap()
    A["gscratch"] = nc.dram_tensor("gscratch", (B, HEADS, STEPS, 3), mybir.dt.float32, kind="Internal").ap()
    outs = {"h": (128, C, T), "conv": (128, 144), "kvT": (128, 8, T), "vtok": (128, 3, 512), "win_old": (B, WIN - STEPS, 512)}
    for name, shape in outs.items():
        O[name] = nc.dram_tensor("out_" + name, shape, mybir.dt.float32, kind="ExternalOutput").ap()
    trunk(nc, A, O)
    r = run_bass_kernel_spmd(nc, [arrays], core_ids=[0]).results[0]

    h = r["out_h"].transpose(2, 1, 0).reshape(T, D)
    conv = r["out_conv"]
    conv_p = conv[:, :16].reshape(128, C, 2).transpose(2, 1, 0).reshape(1, 1, 2, D)
    conv_s = conv[:, 16:].reshape(128, C, B, 2).transpose(2, 3, 1, 0).reshape(1, B, 2, D)
    kvt = r["out_kvT"].reshape(2, HD, 4, 2, T).transpose(4, 2, 3, 0, 1).reshape(T, 4, GROUPS, HD)
    vt = r["out_vtok"].transpose(1, 0, 2)
    v = np.concatenate([vt[0], vt[1], vt[2][:32]]).reshape(T, 2, GROUPS, HD)
    cmp_ = np.stack([kvt[:, 0], kvt[:, 1]], axis=2)
    sel = np.stack([kvt[:, 2], v[:, 0]], axis=2)
    win = np.stack([kvt[:, 3], v[:, 1]], axis=2)

    def prompt(t):
        return np.ascontiguousarray(t[:TP]).reshape(1, 1, TP, GROUPS, 2, HD)

    def sample(t):
        return np.ascontiguousarray(t[TP:]).reshape(1, B, STEPS, GROUPS, 2, HD)

    win_old = r["out_win_old"].reshape(1, B, WIN - STEPS, GROUPS, 2, HD)
    return (h[:TP].reshape(1, TP, D), h[TP:].reshape(B, STEPS, D), conv_p, conv_s, prompt(cmp_), sample(cmp_),
            prompt(sel), sample(sel), prompt(win), np.concatenate([win_old, sample(win)], axis=2))
```

```python
import math
from contextlib import ExitStack

import numpy as np
import concourse.bass as bass
from concourse import mybir

D = 1024
T = 288
TP = 256
B = 8
STEPS = 4
C = D // 128
HEADS = 16
GROUPS = 4
R = 4
HD = 64
PAGES = 16
POOL = 160
FE = 1408
FC = FE // 128
EXPERTS = 8
HALVES = 2
BUCKETS = 32
EPS = 1e-6
NEG = -1e30
KEYS = 2048
WIN = 512
NB = 64
CAP = 128
SPLITS = -(-T // CAP)
MT = 3 * FC
GS, DS, PS = 11, 4, 6
GT = 1024
DT = FC * 128
OHL = 511


def bucket(dist):
    n = np.maximum(dist, 0)
    nf = np.maximum(n, 1).astype(np.float32)
    large = 16 + (np.log(nf / np.float32(16)) / np.float32(math.log(8.0)) * np.float32(16)).astype(np.int32)
    return np.where(n < 16, n, np.minimum(large, BUCKETS - 1))


TABLES = [("ts", i) for i in range(6)] + [("tc",)] + [("tp", i) for i in range(8)]
M_SCAT = 2
M_SEL = M_SCAT + C
M_GU = M_SEL + 1
M_DOWN = M_GU + FC
MR = M_DOWN + 2


def result_order():
    o = [("bv",)]
    for b in range(B):
        o += [("ck", b), ("cv", b)] + TABLES[2 * b:2 * b + 2]
    o += [("css", 0), ("css", 1)] + [("ct", p) for p in range(4)]
    o += [("norm", 0)]
    for c in range(C):
        o += [("gc", c), ("v", c), ("gb", c)]
    o += [("co", c) for c in range(C)]
    o.insert(len(o) - 5, ("norm", 1))
    o += [("f", 0, k) for k in range(HALVES * (2 * FC + C))]
    o += [("norm", 2)]
    for c in range(C):
        o += [("pg", 0, c), ("pp", 0, c)]
    o += [("norm", 3)]
    o += [("kv", c) for c in range(4)]
    for c in range(4, 8):
        o += [("kv", c)]
        if c > 4:
            o += [("kss", c - 1)]
    o += [("vt", 0), ("vt", 1), ("vt", 2), ("kss", 7), ("gt",)]
    for j in range(8):
        o += [("q", j)]
        if j:
            o += [("qss", j - 1)]
    o += [("kcp",), ("qss", 7), ("vcp",), ("kcps",)]
    for u in range(18):
        if u < 16:
            o += [("pl", u, 0), ("pl", u, 1)]
        if 1 <= u <= 16:
            o += [("ptp", u - 1, 0), ("ptp", u - 1, 1)]
        if u >= 2:
            o += [("po", u - 2)]
    for p in range(4):
        o += [("sc", p), ("sn", p)] + ([("pvt", p - 1)] if p else []) + [("wq", p), ("wss", p), ("imp", p)]
        for t in range(4):
            o += [("sq", p, t), ("sss", p, t)]
        o += [("pt", p, i) for i in range(6)] + [("pv", p)]
    o += [("pvt", 3)]
    o += [("wo", c) for c in range(C)]
    o.insert(len(o) - 5, ("norm", 4))
    o += [("rt",)] + [("at", i) for i in range(6)] + [("pos",)]
    o += [("m", k) for k in range(MR)]
    o += [("fs", c) for c in range(C)] + [("norm", 5)]
    for c in range(C):
        o += [("pg", 1, c), ("pp", 1, c)]
    return {label: n for n, label in enumerate(o)}


def rstd_order():
    o = [("css", 0), ("css", 1)] + [("norm", i) for i in range(4)] + [("kss", c) for c in range(4, 8)]
    o += [("qss", j) for j in range(8)] + [("kcps",)]
    for p in range(4):
        o += [("wss", p)] + [("sss", p, t) for t in range(4)]
    o += [("norm", 4), ("norm", 5)]
    return {label: n for n, label in enumerate(o)}


def g_tile_order():
    o = []
    for c in range(C):
        o += [("gc", c), ("v", c), ("gb", c)]
    o += [("co", c) for c in range(C)]
    o += [("f", 0, k) for k in range(HALVES * 2 * FC)]
    for i in range(2):
        o += [("pp", 0, i)] + [("pg", 0, 4 * i + k) for k in range(4)]
    o += [("kv", c) for c in range(8)] + [("vt", i) for i in range(4)] + [("q", j) for j in range(8)]
    for p in range(4):
        o += [("wk", p, 0), ("wk", p, 1)]
        o += [("sk", p, t, b2) for t in range(4) for b2 in range(2)]
        for b2 in range(2):
            o += [("wv", p, b2)]
    o += [("wo", c) for c in range(C)]
    o += [("m", k) for k in range(MT)]
    for i in range(2):
        o += [("pp", 1, i)] + [("pg", 1, 4 * i + k) for k in range(4)]
    return {label: n for n, label in enumerate(o)}


def trunk(nc, A, O):
    f32 = mybir.dt.float32
    ALU = mybir.AluOpType
    ACT = mybir.ActivationFunctionType
    AX = mybir.AxisListType
    RES = result_order()
    GN = g_tile_order()
    RN = rstd_order()
    PER = 2 * FC + C
    assert PER % PS == 0 and (2 * FC) % GS == 0 and C % DS == 0
    assert MR % PS == 0 and MT % GS == 0 and (M_DOWN - M_SEL) % PS == 0 and (M_DOWN + 1 - M_GU) % PS == 0

    with ExitStack() as ctx:
        def sem(name):
            return ctx.enter_context(nc.semaphore(name))

        used = [0]

        def region(name, n):
            t = ctx.enter_context(nc.sbuf_tensor(name, [128, n], f32))
            used[0] += n
            return t

        hT = region("hT", C * T)[:, :].rearrange("p (c t) -> p c t", t=T)
        aT_ = region("aT", C * T)
        aT = aT_[:, :].rearrange("p (c t) -> p c t", t=T)
        gring = region("gring", GS * GT)
        ident = region("ident", 128)
        ones = region("ones", 128)
        bones = region("bones", 128)
        bo32 = region("bo32", 32)
        rsum = region("rsum", 128)
        tri = region("tri", 1024)[:, :].rearrange("p (i j) -> p i j", j=32)
        pmask = region("pmask", 16)[:, :].rearrange("p (i n) -> p i n", n=8)
        wgate = region("wgate", C * 48)[:, :].rearrange("p (c n) -> p c n", n=48)
        rout = region("rout", C * 8)[:, :].rearrange("p (c n) -> p c n", n=8)
        gains = region("gains", 6 * C)
        convw = region("convw", 3 * C)
        state = region("state", C * 16)[:, :].rearrange("p (c b k) -> p c b k", b=B, k=2)
        gq = region("gq", 1)
        gqs = region("gqs", 1)
        gk = region("gk", 3)
        pT = region("pT", 2 * 2 * T)[:, :].rearrange("p (l k t) -> p l k t", l=2, k=2)
        sg_ = region("sg", 2 * T)
        sg = sg_[:, :].rearrange("p (i t) -> p i t", t=T)
        tmp_ = region("tmp", 2 * T)
        tmp = tmp_[:, :].rearrange("p (i t) -> p i t", t=T)
        rs_ = region("rs", 2 * T)
        rs = rs_[:, :].rearrange("p (i t) -> p i t", t=T)
        epsc = region("epsc", 1)
        small = region("small", 416)
        tabP_ = region("tabP", HEADS * 256)
        tabP = tabP_[:, :].rearrange("p (h k) -> p h k", k=256)
        tabC = region("tabC", 256)[:, :].rearrange("p (i n h) -> p i n h", i=2, n=8)
        tS = region("tS", KEYS)
        tW = region("tW", WIN)
        tN = region("tN", 4 * 32)[:, :].rearrange("p (a k) -> p a k", k=32)
        tCs = region("tCs", 128)
        kcn_ = region("kcn", 2 * B * NB)
        kcn = kcn_[:, :].rearrange("p (a n) -> p a n", a=2)
        vcs = region("vcs", 4 * 256)[:, :].rearrange("p (a n) -> p a n", a=4)
        gtok = region("gtok", 3 * 48)[:, :].rearrange("p (i n) -> p i n", n=48)
        grow = region("grow", 12)[:, :].rearrange("p (a n) -> p a n", n=3)
        Q = region("Q", 11136)
        q1 = Q[:, 0:2304].rearrange("p (c t) -> p c t", t=T)
        kvT = Q[:, 2304:4608].rearrange("p (c t) -> p c t", t=T)
        kn = Q[:, 4608:5760].rearrange("p (c t) -> p c t", t=T)
        vtok = Q[:, 5760:7296].rearrange("p (i n) -> p i n", n=512)
        QB = Q[:, 7296:8832].rearrange("p (r b a m) -> p r b a m", r=3, b=B, a=2)
        oT = Q[:, 8832:11136].rearrange("p (c t) -> p c t", t=T)
        qraw = oT
        dring = Q[:, 0:DS * DT]
        hff = Q[:, 5632:5632 + FC * T].rearrange("p (c t) -> p c t", t=T)
        sqn = Q[:, 5632:5632 + C * T].rearrange("p (c t) -> p c t", t=T)
        zT = Q[:, 8800:8800 + C * T].rearrange("p (c t) -> p c t", t=T)
        sqs = [zT if i in (2, 5) else sqn for i in range(6)]
        cbufs = [gring[:, 0:8192], Q[:, 0:8192]]
        vbufs = [t[:, 1024 * i:1024 * i + 1024] for t in (Q, tabP_) for i in range(4)]
        kcscale = [Q[:, 9216 + 512 * a:9728 + 512 * a] for a in range(2)]
        kcsq = Q[:, 8192:8192 + 1024].rearrange("p (a n) -> p a n", a=2)
        ohs = [aT_[:, 0:KEYS], Q[:, 9216:9216 + 672]]
        masks = Q[:, 9888:10656]
        lt = Q[:, 10656:10784]
        rbx = Q[0:BUCKETS + 1, 10784:10800]
        X = region("X", 10816)
        wc = X[:, 0:8192].rearrange("p (k e) -> p k e", e=64)
        UE = 2 + TP + B * 6
        uext = X[:, 8192:8192 + C * UE].rearrange("p (c t) -> p c t", t=UE)
        vraw = X[:, 8192:8192 + 1024].rearrange("p (a n) -> p a n", a=2)
        cstage = X[:, 10640:10784]
        ohv = X[0:BUCKETS + 1, 9216:9216 + OHL]
        ohr = X[0:BUCKETS + 1, 9728:9728 + OHL]
        bvs = X[0:HEADS, 10240:10240 + OHL]
        flip = Q[:, 10800:10928]
        kvp = X[:, 8192:8192 + 8 * TP].rearrange("p (c t) -> p c t", t=TP)
        S = X[:, 0:KEYS + 32]
        SW = X[:, 2080:2080 + WIN + 32]
        SC = X[:, 2624:2752]
        SCg = X[:, 2752:2880]
        ksqs = [X[:, 2880:3904], X[:, 3904:4928], X[:, 9024:10048]]
        rsb = [X[:, 4928:5440], X[:, 8384:8896]]
        PT = X[:, 5440:8384].rearrange("p (k m) -> p k m", m=128)
        pvs = X[:, 8896:9024]
        Sp = X[:, 2880:4416].rearrange("p (i n) -> p i n", i=2)
        PTp = X[:, 4416:5952].rearrange("p (i r n) -> p i r n", i=2, r=2)
        PTc = X[0:8, 5952:6464].rearrange("p (i n) -> p i n", i=2)
        Scp = X[:, 6464:6496].rearrange("p (u i n) -> p u i n", u=2, i=2)
        atok = X[:, 0:3072].rearrange("p (i n) -> p i n", i=3)
        at = [3072]

        def taken(n, parts=128):
            at[0] += n
            return X[0:parts, at[0] - n:at[0]]

        ae = taken(C * CAP).rearrange("p (c m) -> p c m", m=CAP)
        pick = taken(3 * CAP).rearrange("p (i m) -> p i m", m=CAP)
        wpick = taken(3 * CAP).rearrange("p (i m) -> p i m", m=CAP)
        scat = taken(T, CAP)
        he = taken(FC * CAP).rearrange("p (f m) -> p f m", m=CAP)
        sige = taken(FC * CAP).rearrange("p (f m) -> p f m", m=CAP)
        ye = taken(D, CAP)
        before = taken(128)
        count = taken(SPLITS * CAP)
        ones1 = taken(128)
        routed = taken(24).rearrange("p (i e) -> p i e", e=8)
        pos1 = taken(24).rearrange("p (i e) -> p i e", e=8)
        NI = EXPERTS * SPLITS
        NX = EXPERTS * (SPLITS - 1)
        xtab = taken(3 * NX + 2 * NI, 1)
        xthr, xe, xs = (xtab[:, NX * i:NX * i + NX] for i in range(3))
        slot1, e0 = (xtab[:, 3 * NX + NI * i:3 * NX + NI * i + NI] for i in range(2))
        over, okey, items_f = taken(NX, 1), taken(NX, 1), taken(2 * NI + 2, 1)
        osq, ohit, oval = (Q[0:1, o:o + n * NX].rearrange("p (i j) -> p i j", j=NX) for o, n in ((0, NX), (1024, NI), (2048, NI)))
        assert at[0] <= 10816
        cnt1 = aT_[:, 0:1024].rearrange("p (i j) -> p i j", j=32)
        cnt2 = aT_[:, 1024:2048].rearrange("p (i j) -> p i j", j=32)
        vcp = sg_[0:8, 0:256]
        kcp = sg_[:, 256:272].rearrange("p (a n) -> p a n", a=2)
        kcpn = sg_[:, 272:288].rearrange("p (a n) -> p a n", a=2)
        nmp = small[:, 0:12].rearrange("p (u i r) -> p u i r", u=2, i=2)
        smp = small[:, 12:24].rearrange("p (u i r) -> p u i r", u=2, i=2)
        scp = small[:, 24:36].rearrange("p (u i r) -> p u i r", u=2, i=2)
        mxs = small[:, 36:39]
        sms = small[:, 40:43]
        fac = small[:, 44:47]
        smt = small[:, 400:405]
        mxt = small[:, 406:411]
        score = small[:, 48:80]
        rank = small[:, 80:112]
        blkm = small[:, 112:144]
        half = small[:, 144:208]
        rl = small[:, 208:232].rearrange("p (i e) -> p i e", e=8)
        rk = small[:, 232:256].rearrange("p (i e) -> p i e", e=8)
        rmx = small[:, 256:259]
        rsm = small[:, 260:263]
        rg = small[:, 264:288].rearrange("p (i e) -> p i e", e=8)
        cmp8 = [small[:, 288 + 64 * i:352 + 64 * i].rearrange("p (i j) -> p i j", j=8) for i in range(2)]

        ptab = ctx.enter_context(nc.sbuf_tensor("ptab", [1, B * PAGES], mybir.dt.int32))
        items = ctx.enter_context(nc.sbuf_tensor("items", [1, 2 * NI + 2], mybir.dt.int32))

        banks = [ctx.enter_context(nc.psum_tensor(f"bank{i}", [128, 512], f32)) for i in range(PS)]

        psum_full = [sem(f"psum_full{i}") for i in range(PS)]
        psum_drained = [sem(f"psum_drained{i}") for i in range(PS)]
        g_in = [sem(f"g_in{i}") for i in range(GS)]
        d_in = [sem(f"d_in{i}") for i in range(DS)]
        c_in = [sem(f"c_in{i}") for i in range(2)]
        v_in = [sem(f"v_in{i}") for i in range(8)]
        keys_used, values_used = sem("keys_used"), sem("values_used")
        tables_in, ptab_in = sem("tables_in"), sem("ptab_in")
        distance_in, flip_in, bias_out, bias_in = sem("distance_in"), sem("flip_in"), sem("bias_out"), sem("bias_in")
        consts_in, wcmp_in, lt_in, route_in = sem("consts_in"), sem("wcmp_in"), sem("lt_in"), sem("route_in")
        lt_clear, rb_mask, eps_set, rstd_ready = sem("lt_clear"), sem("rb_mask"), sem("eps_set"), sem("rstd_ready")
        sq_ready, a_ready = sem("sq_ready"), sem("a_ready")
        conv_staged, win_stored = sem("conv_staged"), sem("win_stored")
        sig_ready, hsq_ready = sem("sig_ready"), sem("hsq_ready")
        kcn_ready, kn_ready, q_ready = sem("kcn_ready"), sem("kn_ready"), sem("q_ready")
        kvp_in, gates_out, gates_in = sem("kvp_in"), sem("gates_out"), sem("gates_in")
        qb_ready = sem("qb_ready")
        pmax_ready, pexp_ready, pscaled = sem("pmax_ready"), sem("pexp_ready"), sem("pscaled")
        smax_ready, sexp_ready, cprob_ready, sscaled = sem("smax_ready"), sem("sexp_ready"), sem("cprob_ready"), sem("sscaled")
        ksq_ready, so_ready = sem("ksq_ready"), sem("so_ready")
        rmax_ready, rexp_ready = sem("rmax_ready"), sem("rexp_ready")
        routed_ready, items_ready, picks_ready, item_cleared = sem("routed_ready"), sem("items_ready"), sem("picks_ready"), sem("item_cleared")
        down_used, silu_ready = sem("down_used"), sem("silu_ready")
        stored, rows_stored = sem("stored"), sem("rows_stored")
        dve_step, act_step = sem("dve_step"), sem("act_step")

        NTABLE, NCONST = 4, 16

        def bank(label, k=0):
            return banks[(RES[label] + k) % PS]

        def turn(label, e=0, k=0):
            return (RES[label] + k) // PS + (PER // PS if label[0] == "f" else MR // PS) * e

        def full(eng, label, e=0, k=0):
            eng.wait_ge(psum_full[(RES[label] + k) % PS], turn(label, e, k) + 1)

        def drained(eng, label, e=0, k=0):
            eng.wait_ge(psum_drained[(RES[label] + k) % PS], turn(label, e, k) + 1)

        def bank_free(eng, label, e=0, k=0):
            if RES[label] + k >= PS:
                eng.wait_ge(psum_drained[(RES[label] + k) % PS], turn(label, e, k))

        def fill(ins, label, k=0):
            ins.then_inc(psum_full[(RES[label] + k) % PS], 1)

        def drain(ins, label, k=0):
            ins.then_inc(psum_drained[(RES[label] + k) % PS], 1)

        def gslot(label, k=0):
            s = (GN[label] + k) % GS
            return gring[:, s * GT:(s + 1) * GT]

        def g_arrived(eng, label, e=0, k=0):
            n = GN[label] + k
            eng.wait_ge(g_in[n % GS], landed[n] + 16 * ((2 * FC if label[0] == "f" else MT) // GS) * e)

        landed = []
        for n, label in enumerate(GN):
            landed.append((landed[n - GS] if n >= GS else 0) + (64 if label[0] == "sk" else 16))

        def g_released(eng, label, e=0):
            kind = label[0]
            if kind == "pp":
                full(eng, ("pp", label[1], 4 * label[2] + 3), e)
            elif kind == "m":
                f = label[1] - 2 * FC
                if f < 0:
                    full(eng, ("m", M_GU + label[1] // 2), e)
                elif f < FC - 1:
                    eng.wait_ge(down_used, f + 1 + (FC - 1) * e)
                else:
                    full(eng, ("m", M_DOWN + 1), e)
            elif kind == "vt":
                full(eng, ("vt", 2))
            elif kind == "f":
                full(eng, ("f", label[1], label[2] // (2 * FC) * PER + label[2] % (2 * FC)))
            elif kind == "wk":
                full(eng, ("wss", label[1]))
            elif kind == "sk":
                full(eng, ("sss", label[1], label[2]))
            elif kind == "wv":
                eng.wait_ge(values_used, 9 * label[1] + label[2] + 1)
            else:
                full(eng, label, e)

        def update_of(kind, c):
            return [None, ("co", c), None, ("pp", 0, c), ("wo", c), ("fs", c)][kind]

        def h_updated(eng, kind, c, more=0):
            if kind == 0:
                return
            if kind == 2:
                drained(eng, ("f", 0, 0), HALVES - 1, 2 * FC + c)
            else:
                drained(eng, update_of(kind, c), more)

        def item_count(eng):
            eng.wait_ge(items_ready, 1)
            return (eng.value_load(items[0:1, 2 * NI:2 * NI + 1], min_val=EXPERTS, max_val=NI),
                    eng.value_load(items[0:1, 2 * NI + 1:2 * NI + 2], min_val=EXPERTS - 1, max_val=NI - 1))

        def item_value(eng, row, i, top):
            return eng.value_load(items[0:1, bass.ds(i + NI * row, 1)], min_val=0, max_val=top)

        def page(eng, b, i):
            return eng.value_load(ptab[0:1, b * PAGES + i:b * PAGES + i + 1], min_val=0, max_val=POOL - 1)

        def cmp_pages(eng, b, first, count):
            for i in range(first, first + count):
                src = A["cache_cmp"][bass.ds(page(eng, b, i), 1), :, :].rearrange("a p n -> (a p) n")
                eng.dma_start(cbufs[b % 2][:, i * 512:(i + 1) * 512], src).then_inc(c_in[b % 2], 16)

        def value_buffers_free(eng):
            eng.wait_ge(rows_stored, 16 * 4)
            eng.wait_ge(qb_ready, 12)
            full(eng, ("po", 15))
            drained(eng, ("pl", 15, 0))
            drained(eng, ("pl", 15, 1))

        def value_pages(eng, p, b2, t):
            k = 4 * b2 + t
            if p and k == 7:
                full(eng, ("pv", p - 1))
            elif p:
                eng.wait_ge(values_used, 9 * (p - 1) + 3 + 2 * t + b2)
            for i in range(4):
                src = A["cache_selv"][bass.ds(page(eng, 2 * p + b2, 4 * t + i), 1), :, :].rearrange("a p n -> (a p) n")
                eng.dma_start(vbufs[k][:, i * 256:(i + 1) * 256], src).then_inc(v_in[k], 16)

        block = ctx.enter_context(nc.Block())

        @block.sync
        def _(sp):
            sp.dma_start(ptab[:, :], A["page_table"]).then_inc(ptab_in, 16)
            for k in range(4):
                sp.dma_start(wc[:, 32 * k:32 * k + 32, :], A["w_cmp"][:, 32 * k:32 * k + 32, :]).then_inc(wcmp_in, 16)
            sp.wait_ge(ptab_in, 16)
            for b in range(B):
                if b >= 2:
                    full(sp, ("cv", b - 2))
                cmp_pages(sp, b, 0, PAGES // 2)
            full(sp, ("cv", B - 2))
            g_labels = list(GN)

            def g_load(label, src, more=0):
                n = GN[label]
                if n >= GS:
                    g_released(sp, g_labels[n - GS], more)
                sp.dma_start(gslot(label)[:, :], src).then_inc(g_in[n % GS], 16)

            def key_pages(label, b, first):
                n = GN[label]
                g_released(sp, g_labels[n - GS])
                for i in range(4):
                    src = A["cache_selk"][bass.ds(page(sp, b, first + i), 1), :, :].rearrange("a p n -> (a p) n")
                    sp.dma_start(gslot(label)[:, i * 256:(i + 1) * 256], src).then_inc(g_in[n % GS], 16)

            for c in range(C):
                for i, name in enumerate(("gc", "v", "gb")):
                    g_load((name, c), A["conv_in"][3 * c + i])
            for c in range(C):
                g_load(("co", c), A["conv_out"][c])

            def dense_loads(turns, gu, down):
                L = ("f", 0, 0)
                with sp.Fori(0, turns) as e:
                    for k in range(2 * FC):
                        full(sp, L, e, k - GS if k >= GS else k + GS - PER)
                        sp.dma_start(gslot(L, k)[:, :], gu[bass.ds(e, 1), k].rearrange("a p n -> (a p) n"))\
                          .then_inc(g_in[(GN[L] + k) % GS], 16)
                    for k in range(C):
                        n = k
                        full(sp, L, e, 2 * FC + (k - DS if k >= DS else k + C - DS - PER))
                        sp.dma_start(dring[:, (n % DS) * DT:(n % DS + 1) * DT],
                                     down[bass.ds(e, 1), k].rearrange("a p n -> (a p) n")).then_inc(d_in[n % DS], 16)

            full(sp, ("css", 1))
            full(sp, ("co", C - 1))
            dense_loads(HALVES, A["dense_gu"], A["dense_down"])

            def ple_loads(layer, more=0):
                for i in range(2):
                    g_load(("pp", layer, i), A["ple_proj"][layer, i], more)
                    for k in range(4):
                        g_load(("pg", layer, 4 * i + k), A["ple_gate"][layer, 4 * i + k], more)

            ple_loads(0)
            for c in range(8):
                g_load(("kv", c), A["nsa_kv"][c])
            for i in range(4):
                g_load(("vt", i), A["nsa_vt"][i])
            for j in range(8):
                g_load(("q", j), A["nsa_q"][j])
            for p in range(4):
                for b2 in range(2):
                    g_load(("wk", p, b2), A["win_k"][2 * p + b2])
                for t in range(4):
                    for b2 in range(2):
                        key_pages(("sk", p, t, b2), 2 * p + b2, 4 * t)
                for b2 in range(2):
                    g_load(("wv", p, b2), A["win_v"][2 * p + b2])
            for c in range(C):
                g_load(("wo", c), A["nsa_out"][c])
            drained(sp, ("wo", 0))
            for dst, name in ((before[:, :], "before"), (count[:, :], "count"), (xtab, "xtab")):
                sp.dma_start(dst, A[name]).then_inc(route_in, 16)

            def item_loads(i, e, tiles, before=None):
                for k in tiles:
                    sp_label = ("m", k)
                    n = GN[sp_label]
                    if k >= GS:
                        g_released(sp, ("m", k - GS), i)
                    elif before is not None:
                        g_released(sp, ("m", k - GS + MT), before)
                    else:
                        g_released(sp, g_labels[n - GS])
                    sp.dma_start(gslot(sp_label)[:, :], A["moe"][bass.ds(e, 1), k].rearrange("a p n -> (a p) n"))\
                      .then_inc(g_in[n % GS], 16)

            item_loads(0, 0, range(GS))
            n_items, more = item_count(sp)
            with sp.Fori(0, more) as i:
                item_loads(i, item_value(sp, 0, i, EXPERTS - 1), range(GS, MT))
                item_loads(i + 1, item_value(sp, 0, i + 1, EXPERTS - 1), range(GS), before=i)
            item_loads(more, item_value(sp, 0, more, EXPERTS - 1), range(GS, MT))
            ple_loads(1, more)
            sp.wait_ge(rows_stored, 16 * 4)
            for c in range(C):
                drained(sp, ("pp", 1, c), more)
                sp.dma_start(O["h"][:, c, :], hT[:, c, :]).then_inc(stored, 16)
            sp.wait_ge(stored, 16 * C)
            sp.wait_ge(win_stored, 16 * B)

        @block.gpsimd
        def _(pool):
            pool.memset(lt[:, :], 0.0).then_inc(lt_clear, 1)
            pool.wait_ge(lt_clear, 1)
            for t in range(STEPS):
                for b2 in range(2):
                    dst = lt[32 * t:32 * t + 32, 64 * b2 + t:64 * b2 + 64:4]
                    pool.dma_start(dst, A["rel_bias"][:, :], allow_slow_non_contiguous=True).then_inc(lt_in, 16)
            drained(pool, ("co", 0))
            for b in range(B):
                n = (WIN - STEPS) * 512
                src = A["state_win"][b, STEPS:WIN, :].rearrange("s n -> (s n)").rearrange("(a n) -> a n", a=16)
                dst = O["win_old"][b].rearrange("s n -> (s n)").rearrange("(a n) -> a n", a=16)
                pool.dma_start(dst, src).then_inc(win_stored, 16)
            pool.wait_ge(conv_staged, 2)
            pool.dma_start(O["conv"][:, :], cstage[:, :]).then_inc(rows_stored, 16)
            for c4 in range(4):
                drained(pool, ("kv", c4))
            for c in range(2):
                for g in range(GROUPS):
                    for l2 in range(2):
                        pool.dma_start(kvp[64 * l2:64 * l2 + 64, 4 * c + g, 0:TP - l2],
                                       kvT[64 * (g % 2):64 * (g % 2) + 64, 2 * c + g // 2, l2:TP]).then_inc(kvp_in, 16)
            for c in range(4, 8):
                drained(pool, ("kv", c))
            pool.dma_start(O["kvT"][:, :, :], kvT[:, :, :]).then_inc(rows_stored, 16)
            for i in range(3):
                drained(pool, ("vt", i))
            pool.dma_start(O["vtok"][:, 0:2, :], vtok[:, 0:2, :]).then_inc(rows_stored, 16)
            pool.dma_start(O["vtok"][0:32, 2, :], vtok[0:32, 2, :]).then_inc(rows_stored, 16)
            drained(pool, ("gt",))
            for b in range(B):
                src = gtok[STEPS * b:STEPS * b + STEPS, 2, :].rearrange("t (r h) -> t r h", r=3)
                pool.dma_start(A["gscratch"][b].rearrange("h t r -> t r h"), src,
                               allow_slow_non_contiguous=True).then_inc(gates_out, 16)
            pool.wait_ge(gates_out, 16 * B)
            for p in range(4):
                src = A["gscratch"][2 * p:2 * p + 2].rearrange("b h t r -> (b h t) r")
                pool.dma_start(grow[:, p, :], src).then_inc(gates_in, 16)
            value_buffers_free(pool)
            for p in range(4):
                for t in range(4):
                    for b2 in range(2):
                        value_pages(pool, p, b2, t)

        @block.scalar
        def _(act):
            step = [0]

            def chain(ins):
                step[0] += 1
                ins.then_inc(act_step, 1)

            act.dma_start(ohr, A["ohr"]).then_inc(distance_in, 16)
            act.dma_start(rbx[0:BUCKETS, :], A["rel_bias"]).then_inc(distance_in, 16)
            act.wait_ge(ptab_in, 16)
            cmp_pages(act, 0, PAGES // 2, PAGES // 2)
            act.dma_start(flip[:, :], A["flip"]).then_inc(flip_in, 16)
            loads = [(ohs[0], A["ohs"][:, 0:KEYS]), (ohs[1], A["ohs"][:, KEYS:KEYS + 672]), (masks[:, :], A["masks"]), (ohv, A["ohv"])]
            assert len(loads) == NTABLE
            for dst, src in loads:
                act.dma_start(dst, src).then_inc(tables_in, 16)
            full(act, ("bv",))
            drain(act.activation(bvs, bank(("bv",))[0:HEADS, 0:OHL], ACT.Copy), ("bv",))
            drained(act, ("bv",))
            act.dma_start(A["bias_by_distance"], bvs).then_inc(bias_out, 16)
            act.wait_ge(bias_out, 16)
            shifted = A["bias_by_distance"]
            shifted = bass.AP(shifted.tensor, 0, [[1, 128], [OHL, HEADS], [1, 256]])
            act.dma_start(tabP, shifted).then_inc(bias_in, 16)
            cmp_pages(act, 1, PAGES // 2, PAGES // 2)
            loads = [(ident[:, :], "ident"), (ones[:, :], "ones"), (bones[:, :], "bones"), (bo32[:, :], "bo32"), (rsum[:, :], "rsum"),
                     (hT, "x"), (state, "state"), (gains[:, :], "gains"), (convw[:, :], "convw"), (gq[:, :], "gq"), (gk[:, :], "gk"),
                     (tri, "tri"), (pmask, "pmask"), (pT, "p"), (wgate, "wgate"), (rout, "rout")]
            assert len(loads) == NCONST

            act.wait_ge(eps_set, 1)
            both = "natural_log_exp_and_others"
            act.preload_act_table_set(both)

            def rstd(dst, src, label, more=0):
                full(act, label, more)
                drain(act.activation(dst, src, ACT.Ln, bias=epsc[:, :]), label)
                drained(act, label, more)
                act.activation(dst, dst, ACT.Exp, scale=-0.5).then_inc(rstd_ready, 1)

            def row_scale(m):
                if 2 <= m < 6:
                    act.wait_ge(kn_ready, 2 * (m - 1))
                elif m >= 6:
                    act.wait_ge(q_ready, m - 5)
                label = ("kss", m + 4) if m < 4 else ("qss", m - 4) if m < 12 else ("kcps",)
                n = T if m < 12 else 16
                rstd(rs[:, m % 2, 0:n], bank(label)[:, 0:n], label)

            def table(label):
                kind, i = (label + (0,))[:2]
                if kind == "ts" and i >= 4:
                    return
                full(act, label)
                if kind == "tp":
                    drain(act.activation(tabP_[:, 512 * i:512 * i + 512], bank(label)[:, :], ACT.Copy), label)
                elif kind == "tc":
                    drain(act.activation(tabC, bank(label)[:, 0:256].rearrange("p (i n h) -> p i n h", i=2, n=8), ACT.Copy), label)
                else:
                    drain(act.activation(tS[:, 512 * i:512 * i + 512], bank(label)[:, :], ACT.Copy), label)

            for b in range(B):
                full(act, ("ck", b))
                src = bank(("ck", b))[:, 0:128].rearrange("p (a n) -> p a n", a=2)
                chain(act.activation(kcn[:, :, NB * b:NB * b + NB], src, ACT.Copy))
                drain(act.activation(kcsq[:, :, NB * b:NB * b + NB], src, ACT.Square), ("ck", b))
                full(act, ("cv", b))
                drain(act.activation(vraw[:, :, NB * b:NB * b + NB], bank(("cv", b))[:, 0:128].rearrange("p (a n) -> p a n", a=2),
                                     ACT.Copy), ("cv", b))
                if b + 2 < B:
                    cmp_pages(act, b + 2, PAGES // 2, PAGES // 2)
                for label in TABLES[2 * b:2 * b + 2]:
                    table(label)
                if 2 <= b < 6:
                    for dst, name in loads[4 * (b - 2):4 * (b - 1)]:
                        act.dma_start(dst, A[name]).then_inc(consts_in, 16)
            drained(act, ("ts", 4))
            drained(act, ("ts", 5))
            for a in range(2):
                rstd(kcscale[a], bank(("css", a))[:, :], ("css", a))
            for p in range(4):
                full(act, ("ct", p))
                drain(act.activation(vcs[:, p, :], bank(("ct", p))[:, 0:256], ACT.Copy), ("ct", p))

            def norm_squares(i, more=0):
                for c in range(C):
                    h_updated(act, i, c, more)
                    if i == 0 and c == 0:
                        act.wait_ge(consts_in, 16 * NCONST)
                        full(act, ("css", 1))
                    act.activation(sqs[i][:, c, :], hT[:, c, :], ACT.Square).then_inc(sq_ready, 1)
                rstd(rs[:, 0, :], bank(("norm", i))[:, 0:T], ("norm", i), more)

            norm_squares(0)
            for c in range(C):
                full(act, ("gc", c))
                if c >= 2:
                    drained(act, ("v", c - 2))
                drain(act.activation(sg[:, c % 2, :], bank(("gc", c))[:, 0:T], ACT.Copy), ("gc", c))
            norm_squares(1)

            def dense_gates(turns):
                with act.Fori(0, turns) as e:
                    for f in range(FC):
                        full(act, ("f", 0, 0), e, 2 * f)
                        drained(act, ("f", 0, 0), e, 2 * (f - 2) + 1 if f >= 2 else 2 * (f % 2 + FC - 2 + (FC % 2) * (1 - 2 * f)) + 1 - PER)
                        act.activation(sg[:, f % 2, :],
                                       bank(("f", 0, 0), 2 * f)[:, 0:T], ACT.Sigmoid).then_inc(sig_ready, 1)

            def ple_gates(layer, more=0):
                for c in range(C):
                    full(act, ("pg", layer, c), more)
                    if c >= 2:
                        drained(act, ("pp", layer, c - 2), more)
                    drain(act.activation(sg[:, c % 2, :], bank(("pg", layer, c))[:, 0:T], ACT.Sigmoid), ("pg", layer, c))

            dense_gates(HALVES)
            act.preload_act_table_set(both)
            norm_squares(2)
            ple_gates(0)
            act.preload_act_table_set(both)
            norm_squares(3)

            def square(label, n, half):
                if n >= 2:
                    full(act, half)
                act.activation(tmp[:, n % 2, :], bank(label)[:, 0:T], ACT.Square).then_inc(hsq_ready, 1)

            for c in range(8):
                full(act, ("kv", c))
                if c < 4:
                    drain(act.activation(kvT[:, c, :], bank(("kv", c))[:, 0:T], ACT.Copy), ("kv", c))
                else:
                    square(("kv", c), c - 4, ("kss", c - 2) if c >= 6 else None)
                    drain(act.activation(kvT[:, c, :], bank(("kv", c))[:, 0:T], ACT.Copy), ("kv", c))
                    if c > 4:
                        row_scale(c - 5)
            for i in range(3):
                n = 128 if i < 2 else 32
                full(act, ("vt", i))
                drain(act.activation(vtok[0:n, i, :], bank(("vt", i))[0:n, :], ACT.Copy), ("vt", i))
            row_scale(3)
            full(act, ("gt",))
            chain(act.activation(gtok[0:32, 2, :], bank(("gt",))[0:32, 96:144], ACT.Sigmoid))
            act.wait_ge(act_step, step[0])
            drain(act.activation(gtok[:, 0:2, :], bank(("gt",))[:, 0:96].rearrange("p (i n) -> p i n", i=2),
                                 ACT.Sigmoid), ("gt",))
            act.preload_act_table_set(both)
            for j in range(8):
                full(act, ("q", j))
                square(("q", j), 4 + j, ("qss", j - 2) if j >= 2 else ("kss", 6 + j))
                drain(act.activation(qraw[:, j, :], bank(("q", j))[:, 0:T], ACT.Copy), ("q", j))
                if j:
                    row_scale(3 + j)
            full(act, ("kcp",))
            full(act, ("qss", 6))
            src = bank(("kcp",))[:, 0:16].rearrange("p (a n) -> p a n", a=2)
            act.activation(tmp_[:, 0:16].rearrange("p (a n) -> p a n", a=2), src, ACT.Square).then_inc(hsq_ready, 1)
            drain(act.activation(kcp, src, ACT.Copy), ("kcp",))
            row_scale(11)
            full(act, ("vcp",))
            drain(act.activation(vcp, bank(("vcp",))[0:8, 0:256], ACT.Copy), ("vcp",))

            row_scale(12)

            for u in range(17):
                if u:
                    w = (u - 1) % 2
                    if u >= 3:
                        full(act, ("po", u - 3))
                    full(act, ("ptp", u - 1, 0))
                    o = bank(("ptp", u - 1, 0))
                    chain(act.activation(PTc[:, w, :], o[0:8, 256:512], ACT.Copy))
                    act.wait_ge(act_step, step[0])
                    for i in range(2):
                        full(act, ("ptp", u - 1, i))
                        n = 128 * (i + 1)
                        drain(act.activation(PTp[:, w, :, 128 * i:128 * i + n],
                                             bank(("ptp", u - 1, i))[:, 0:2 * n].rearrange("p (r n) -> p r n", r=2),
                                             ACT.Copy), ("ptp", u - 1, i))
                if u < 16:
                    w = u % 2
                    act.wait_ge(pmax_ready, u + 1)
                    for i in range(2):
                        nk = 128 * (i + 1)
                        o = 256 * i
                        for r in range(2):
                            ins = act.activation(Sp[:, w, o + r * nk:o + (r + 1) * nk], Sp[:, w, o + r * nk:o + (r + 1) * nk],
                                                 ACT.Exp, bias=nmp[:, w, i, r + 1:r + 2], accum_out=smp[:, w, i, r + 1:r + 2])
                            ins.then_inc(pexp_ready, 1)
                        act.activation(Scp[:, w, i, :], Scp[:, w, i, :], ACT.Exp, bias=nmp[:, w, i, 0:1],
                                       accum_out=smp[:, w, i, 0:1]).then_inc(pexp_ready, 1)
            full(act, ("po", 15))

            def exps(p, r, view, total, first=True):
                if first:
                    act.wait_ge(smax_ready, 3 * p + 1 + {0: 0, 2: 1, 1: 2}[r])
                act.activation(view, view, ACT.Exp, bias=mxs[:, r:r + 1], accum_out=total).then_inc(sexp_ready, 1)

            for p in range(4):
                def key_squares(label, n):
                    g_arrived(act, label)
                    m = 10 * p + n - 3
                    if m >= 0 and m % 2 == 0:
                        act.wait_ge(keys_used, m // 2 + 1)
                    elif m >= 0:
                        full(act, ("sss", m // 10, (m % 10 - 3) // 2) if m % 10 > 1 else ("wss", m // 10))
                    act.activation(ksqs[(10 * p + n) % 3], gslot(label)[:, :], ACT.Square).then_inc(ksq_ready, 1)

                before = [("wk", p, 0), ("wk", p, 1)] + [("sk", p, t, b2) for t in range(4) for b2 in range(2)]
                key_squares(before[0], 0)
                key_squares(before[1], 1)
                exps(p, 0, SC[:, :], sms[:, 0:1])

                def key_scale(i):
                    label = ("sss", p, i - 1) if i else ("wss", p)
                    if i > 1:
                        drained(act, ("sq", p, i - 3) if i > 2 else ("wq", p))
                    elif p:
                        drained(act, ("sq", p - 1, 2 + i))
                    rstd(rsb[(5 * p + i) % 2], bank(label)[:, :], label)

                key_scale(0)
                key_squares(before[2], 2)
                key_squares(before[3], 3)
                full(act, ("imp", p))
                ins = act.activation(SCg[:, :], bank(("imp", p))[:, 0:128], ACT.Copy)
                drain(ins, ("imp", p))
                exps(p, 2, SW[:, :], sms[:, 2:3])
                for t in range(4):
                    if t < 3:
                        key_squares(before[2 * t + 4], 2 * t + 4)
                        key_squares(before[2 * t + 5], 2 * t + 5)
                    key_scale(t + 1)
                exps(p, 1, S[:, KEYS:KEYS + 32], smt[:, 4:5])
                for t in range(4):
                    exps(p, 1, S[:, 512 * t:512 * t + 512], smt[:, t:t + 1], first=False)
                for i in range(6):
                    full(act, ("pt", p, i))
                    src = bank(("pt", p, i))
                    if i == 0:
                        ins = act.activation(PT[:, 0:4, :], src[:, :].rearrange("p (k m) -> p k m", k=4), ACT.Copy)
                    elif i == 1:
                        chain(act.activation(PT[:, 4, :], src[:, 0:128], ACT.Copy))
                        act.wait_ge(act_step, step[0])
                        ins = act.activation(PT[0:32, 5:7, :], src[0:32, 128:384].rearrange("p (k m) -> p k m", k=2), ACT.Copy)
                    else:
                        k = 7 + 4 * (i - 2)
                        ins = act.activation(PT[:, k:k + 4, :], src[:, :].rearrange("p (k m) -> p k m", k=4), ACT.Copy)
                    drain(ins, ("pt", p, i))

            norm_squares(4)
            for k in range(6):
                i, h, n = k // 2, k % 2, 128 if k < 4 else 32
                full(act, ("at", k))
                drain(act.activation(atok[0:n, i, 512 * h:512 * h + 512], bank(("at", k))[0:n, :], ACT.Copy), ("at", k))
            act.wait_ge(rmax_ready, 1)
            for i in range(3):
                act.activation(rg[:, i, :], rl[:, i, :], ACT.Exp, bias=rmx[:, i:i + 1]).then_inc(rexp_ready, 1)
            n_items, more = item_count(act)
            act.wait_ge(item_cleared, 2)
            with act.Fori(0, n_items) as i:
                M = ("m", 0)
                for h in range(2):
                    full(act, M, i, h)
                    drain(act.activation(ae[:, 4 * h:4 * h + 4, :], bank(M, h)[:, 0:4 * CAP].rearrange("p (c m) -> p c m", m=CAP),
                                         ACT.Copy), M, h)
                full(act, M, i, M_SEL)
                drain(act.activation(scat, bank(M, M_SEL)[0:CAP, 0:T], ACT.Copy), M, M_SEL)
                for f in range(FC):
                    full(act, M, i, M_GU + f)
                    if f == 0:
                        drained(act, M, i, M_GU + FC - 1 - MR)
                    act.activation(sige[:, f, :], bank(M, M_GU + f)[:, 0:CAP], ACT.Sigmoid).then_inc(sig_ready, 1)
                for h in range(2):
                    full(act, M, i, M_DOWN + h)
                    drain(act.activation(ye[:, 512 * h:512 * h + 512], bank(M, M_DOWN + h)[0:CAP, :], ACT.Copy), M, M_DOWN + h)
            act.preload_act_table_set(both)
            norm_squares(5, more)
            ple_gates(1, more)

        @block.vector
        def _(dve):
            step = [0]

            def chain(ins):
                step[0] += 1
                ins.then_inc(dve_step, 1)

            def settled():
                dve.wait_ge(dve_step, step[0])

            def scaled_by(label):
                dve.wait_ge(rstd_ready, RN[label] + 1)

            dve.memset(epsc[:, :], EPS).then_inc(eps_set, 1)
            dve.memset(rbx[BUCKETS:BUCKETS + 1, :], NEG).then_inc(rb_mask, 1)
            dve.wait_ge(tables_in, 16 * NTABLE)
            full(dve, ("ts", 4))
            drain(dve.tensor_tensor(tW[:, :], bank(("ts", 4))[:, :], masks[:, 0:512], ALU.add), ("ts", 4))
            full(dve, ("ts", 5))
            chain(dve.tensor_tensor(tN, bank(("ts", 5))[:, 0:32].unsqueeze(1).to_broadcast([128, 4, 32]),
                                    masks[:, 512:640].rearrange("p (a k) -> p a k", a=4), ALU.add))
            drain(dve.tensor_tensor(tCs[:, :], bank(("ts", 5))[:, 32:160], masks[:, 640:768], ALU.add), ("ts", 5))
            dve.wait_ge(consts_in, 16 * NCONST)
            chain(dve.tensor_scalar(gqs[:, :], gq[:, :], HD ** -0.5, None, ALU.mult))

            for a in range(2):
                scaled_by(("css", a))
                dve.scalar_tensor_tensor(kcn[:, a, :], kcn[:, a, :], gk[:, 0:1], kcscale[a], ALU.mult, ALU.mult).then_inc(kcn_ready, 1)

            def norm(i):
                scaled_by(("norm", i))
                for c in range(C):
                    dve.scalar_tensor_tensor(aT[:, c, :], hT[:, c, :], gains[:, C * i + c:C * i + c + 1], rs[:, 0, :],
                                             ALU.mult, ALU.mult).then_inc(a_ready, 1)

            norm(0)
            chain(dve.memset(uext[:, :, 0:2], 0.0))
            us = uext[:, :, 258:UE].rearrange("p c (b k) -> p c b k", b=B)
            for c in range(C):
                chain(dve.tensor_copy(us[:, c, :, 0:2], state[:, c, :, :]))
            for c in range(C):
                drained(dve, ("gc", c))
                full(dve, ("v", c))
                v = bank(("v", c))
                chain(dve.tensor_tensor(uext[:, c, 2:258], sg[:, c % 2, 0:TP], v[:, 0:TP], ALU.mult))
                drain(dve.tensor_tensor(us[:, c, :, 2:6], sg[:, c % 2, TP:T].rearrange("p (b k) -> p b k", b=B),
                                        v[:, TP:T].rearrange("p (b k) -> p b k", b=B), ALU.mult), ("v", c))
                settled()
                drained(dve, ("v", c))
                cw = [convw[:, C * k + c:C * k + c + 1] for k in range(3)]
                tp, tsm = tmp[:, c % 2, 0:TP], tmp[:, c % 2, TP:T].rearrange("p (b k) -> p b k", b=B)
                chain(dve.tensor_scalar(tp, uext[:, c, 0:256], cw[0], None, ALU.mult))
                chain(dve.tensor_scalar(tsm, us[:, c, :, 0:4], cw[0], None, ALU.mult))
                for k in (1, 2):
                    settled()
                    chain(dve.scalar_tensor_tensor(tp, uext[:, c, k:k + 256], cw[k], tp, ALU.mult, ALU.add))
                    chain(dve.scalar_tensor_tensor(tsm, us[:, c, :, k:k + 4], cw[k], tsm, ALU.mult, ALU.add))
                settled()
                full(dve, ("gb", c))
                drain(dve.tensor_tensor(zT[:, c, :], bank(("gb", c))[:, 0:T], tmp[:, c % 2, :], ALU.mult), ("gb", c))
            dve.tensor_copy(cstage[:, 0:16].rearrange("p (c k) -> p c k", c=C), uext[:, :, 256:258]).then_inc(conv_staged, 1)
            dve.tensor_copy(cstage[:, 16:144].rearrange("p (c b k) -> p c b k", c=C, b=B), us[:, :, :, 4:6]).then_inc(conv_staged, 1)

            def add_to_h(label, c, e=0, k=0):
                full(dve, label, e, k)
                drain(dve.tensor_tensor(hT[:, c, :], hT[:, c, :], bank(label, k)[:, 0:T], ALU.add), label, k)

            for c in range(C):
                add_to_h(("co", c), c)
            norm(1)

            def dense(turns):
                with dve.Fori(0, turns) as e:
                    for f in range(FC):
                        gl, ul = 2 * f, 2 * f + 1
                        L = ("f", 0, 0)
                        dve.wait_ge(sig_ready, f + 1 + FC * e)
                        s = sg[:, f % 2, :]
                        drain(dve.tensor_tensor(s, s, bank(L, gl)[:, 0:T], ALU.mult), L, gl)
                        drained(dve, L, e, gl)
                        full(dve, L, e, ul)
                        drain(dve.tensor_tensor(hff[:, f, :], s, bank(L, ul)[:, 0:T], ALU.mult), L, ul)
                    for c in range(C):
                        add_to_h(L, c, e, 2 * FC + c)

            def ple(layer, more=0):
                for c in range(C):
                    drained(dve, ("pg", layer, c), more)
                    full(dve, ("pp", layer, c), more)
                    s = sg[:, c % 2, :]
                    chain(dve.tensor_tensor(s, s, bank(("pp", layer, c))[:, 0:T], ALU.mult))
                    settled()
                    drain(dve.tensor_tensor(hT[:, c, :], hT[:, c, :], s, ALU.add), ("pp", layer, c))

            dense(HALVES)
            norm(2)
            ple(0)
            norm(3)

            def key_norm(c):
                scaled_by(("kss", c))
                drained(dve, ("kv", c))
                br = 1 + (c - 4) // 2
                dve.scalar_tensor_tensor(kn[:, c - 4, 0:TP], kvT[:, c, 0:TP], gk[:, br:br + 1], rs[:, c % 2, 0:TP],
                                         ALU.mult, ALU.mult).then_inc(kn_ready, 1)
                dve.tensor_tensor(kn[:, c - 4, TP:T], kvT[:, c, TP:T], rs[:, c % 2, TP:T], ALU.mult).then_inc(kn_ready, 1)

            for c in range(4, 8):
                key_norm(c)
            for j in range(8):
                scaled_by(("qss", j))
                drained(dve, ("q", j))
                dve.scalar_tensor_tensor(q1[:, j, :], qraw[:, j, :], gqs[:, :], rs[:, j % 2, :], ALU.mult, ALU.mult).then_inc(q_ready, 1)
            chain(dve.memset(QB, 0.0))
            settled()
            dve.wait_ge(q_ready, 8)
            for r in range(3):
                for a in range(2):
                    for g2 in range(2):
                        h = slice(64 * g2, 64 * g2 + 64)
                        dst = QB[h, r, :, a, 16 * g2:16 * g2 + 16].rearrange("p b (r t) -> p b r t", r=R)
                        src = q1[h, 4 * a:4 * a + 4, TP:T].rearrange("p r (b t) -> p b r t", b=B)
                        if r:
                            ins = dve.tensor_scalar(dst, src, gk[h, r:r + 1], None, ALU.mult)
                        else:
                            ins = dve.tensor_copy(dst, src)
                        ins.then_inc(qb_ready, 1)
            scaled_by(("kcps",))
            drained(dve, ("kcp",))
            dve.scalar_tensor_tensor(kcpn, kcp, gk[:, 0:1], rs[:, 0, 0:16].rearrange("p (a n) -> p a n", a=2),
                                     ALU.mult, ALU.mult).then_inc(kcn_ready, 1)
            drained(dve, ("gt",))

            def prompt_scores(u):
                w, j, g2 = u % 2, u // 2, u % 2
                head = (2 * (j // 4) + g2) * R + j % 4
                if u >= 2:
                    full(dve, ("ptp", u - 2, 1))
                s = [Sp[:, w, 256 * i:256 * i + 256 * (i + 1)].rearrange("p (r k) -> p r k", r=2) for i in range(2)]
                full(dve, ("pl", u, 0))
                chain(dve.tensor_tensor(Scp[:, w, :, :], bank(("pl", u, 0))[:, 256:272].rearrange("p (i n) -> p i n", i=2),
                                        tabC[:, :, :, head], ALU.add))
                settled()
                for i in range(2):
                    nk = 128 * (i + 1)
                    full(dve, ("pl", u, i))
                    drain(dve.tensor_tensor(s[i], bank(("pl", u, i))[:, 0:2 * nk].rearrange("p (r k) -> p r k", r=2),
                                            tabP[:, head, 256 - nk:256].unsqueeze(1).to_broadcast([128, 2, nk]), ALU.add),
                          ("pl", u, i))
                chain(dve.tensor_reduce(nmp[:, w, :, 0], Scp[:, w, :, :], AX.X, ALU.max))
                for i in range(2):
                    drained(dve, ("pl", u, i))
                    chain(dve.tensor_reduce(nmp[:, w, i, 1:3], s[i], AX.X, ALU.max))
                settled()
                dve.tensor_scalar(nmp[:, w], nmp[:, w], -1.0, None, ALU.mult).then_inc(pmax_ready, 1)

            def prompt_scale(u):
                w, j, g2 = u % 2, u // 2, u % 2
                head = (2 * (j // 4) + g2) * R + j % 4
                dve.wait_ge(pexp_ready, 6 * (u + 1))
                chain(dve.reciprocal(scp[:, w], smp[:, w]))
                settled()
                chain(dve.tensor_tensor(scp[:, w], scp[:, w], gtok[:, 0:2, head:48:16], ALU.mult))
                settled()
                for i in range(2):
                    nk = 128 * (i + 1)
                    dve.scalar_tensor_tensor(Scp[:, w, i, :], Scp[:, w, i, :], scp[:, w, i, 0:1], pmask[:, i, :],
                                             ALU.mult, ALU.mult).then_inc(pscaled, 1)
                    for r in range(2):
                        o = 256 * i + r * nk
                        dve.tensor_scalar(Sp[:, w, o:o + nk], Sp[:, w, o:o + nk], scp[:, w, i, r + 1:r + 2], None,
                                          ALU.mult).then_inc(pscaled, 1)

            def prompt_out(u):
                j, g2 = u // 2, u % 2
                h = slice(64 * g2, 64 * g2 + 64)
                full(dve, ("po", u))
                drain(dve.tensor_copy(oT[h, j, 0:TP], bank(("po", u))[h, 0:TP]), ("po", u))

            for u in range(19):
                if 1 <= u <= 16:
                    prompt_scale(u - 1)
                if u < 16:
                    prompt_scores(u)
                if u >= 3:
                    prompt_out(u - 3)

            dve.wait_ge(gates_in, 16 * 4)

            def sample_out(p):
                full(dve, ("pvt", p))
                for a in range(2):
                    for g2 in range(2):
                        h = slice(64 * g2, 64 * g2 + 64)
                        src = bank(("pvt", p))[h, 0:128].rearrange("p (b a g r t) -> p a g r b t", b=2, a=2, g=2, r=R)[:, a, g2]
                        dst = oT[h, 4 * a:4 * a + 4, TP + 8 * p:TP + 8 * p + 8].rearrange("p r (b t) -> p r b t", b=2)
                        ins = dve.tensor_copy(dst, src)
                        if a == 1 and g2 == 1:
                            drain(ins, ("pvt", p))
                        else:
                            ins.then_inc(so_ready, 1)

            for p in range(4):
                def soft(r, view):
                    chain(dve.tensor_reduce(mxs[:, r:r + 1], view, AX.X, ALU.max))
                    settled()
                    dve.tensor_scalar(mxs[:, r:r + 1], mxs[:, r:r + 1], -1.0, None, ALU.mult).then_inc(smax_ready, 1)

                def recip(r):
                    chain(dve.reciprocal(fac[:, r:r + 1], sms[:, r:r + 1]))
                    settled()

                if p:
                    full(dve, ("pt", p - 1, 5))
                full(dve, ("sc", p))
                drain(dve.tensor_tensor(SC[:, :], bank(("sc", p))[:, 0:128], tCs[:, :], ALU.add), ("sc", p))
                drained(dve, ("sc", p))
                soft(0, SC[:, :])
                full(dve, ("sn", p))
                sn = bank(("sn", p))
                chain(dve.tensor_tensor(S[:, KEYS:KEYS + 32], sn[:, 0:32], tN[:, p, :], ALU.add))
                drain(dve.tensor_tensor(SW[:, WIN:WIN + 32], sn[:, 32:64], tN[:, p, :], ALU.add), ("sn", p))
                dve.wait_ge(sexp_ready, 7 * p + 1)
                recip(0)
                dve.tensor_scalar(SC[:, :], SC[:, :], fac[:, 0:1], None, ALU.mult).then_inc(cprob_ready, 1)
                if p:
                    sample_out(p - 1)
                scaled_by(("wss", p))
                full(dve, ("wq", p))
                drain(dve.tensor_tensor(SW[:, 0:WIN], bank(("wq", p))[:, :], rsb[5 * p % 2], ALU.mult), ("wq", p))
                drained(dve, ("wq", p))
                chain(dve.tensor_tensor(SW[:, 0:WIN], SW[:, 0:WIN], tW[:, :], ALU.add))
                settled()
                drained(dve, ("sn", p))
                drained(dve, ("imp", p))
                chain(dve.tensor_tensor(half[:, :], SCg[:, 0:64], SCg[:, 64:128], ALU.add))
                settled()
                hv = half[:, :].rearrange("p (k m) -> p k m", m=2)
                chain(dve.tensor_tensor(score[:, :], hv[:, :, 0], hv[:, :, 1], ALU.add))
                settled()
                chain(dve.memset(score[:, 0:1], 1e4))
                chain(dve.memset(score[:, 31:32], 1e4))
                settled()
                soft(2, SW[:, :])
                chain(dve.tensor_reduce(mxt[:, 4:5], S[:, KEYS:KEYS + 32], AX.X, ALU.max))
                other = score[:, :].unsqueeze(1).to_broadcast([128, 32, 32])
                own = score[:, :].unsqueeze(2).to_broadcast([128, 32, 32])
                chain(dve.tensor_tensor(cnt1, other, own, ALU.is_gt))
                chain(dve.tensor_tensor(cnt2, other, own, ALU.is_equal))
                settled()
                chain(dve.tensor_tensor(cnt2, cnt2, tri, ALU.mult))
                settled()
                chain(dve.tensor_tensor(cnt1, cnt1, cnt2, ALU.add))
                settled()
                chain(dve.tensor_reduce(rank[:, :], cnt1, AX.X, ALU.add))
                settled()
                chain(dve.tensor_scalar(blkm[:, :], rank[:, :], 14.5, NEG, ALU.is_gt, ALU.mult))
                dve.tensor_scalar(SCg[:, :], SC[:, :], grow[:, p, 0:1], None, ALU.mult).then_inc(sscaled, 1)
                for t in range(4):
                    scaled_by(("sss", p, t))
                    full(dve, ("sq", p, t))
                    st = S[:, 512 * t:512 * t + 512]
                    drain(dve.tensor_tensor(st, bank(("sq", p, t))[:, :], rsb[(5 * p + 1 + t) % 2], ALU.mult), ("sq", p, t))
                    drained(dve, ("sq", p, t))
                    chain(dve.tensor_tensor(st, st, tS[:, 512 * t:512 * t + 512], ALU.add))
                    settled()
                    sv = st.rearrange("p (k m) -> p k m", k=8)
                    chain(dve.tensor_tensor(sv, sv, blkm[:, 8 * t:8 * t + 8].unsqueeze(2).to_broadcast([128, 8, 64]), ALU.add))
                    settled()
                    chain(dve.tensor_reduce(mxt[:, t:t + 1], st, AX.X, ALU.max))
                settled()
                soft(1, mxt[:, :])
                dve.wait_ge(sexp_ready, 7 * p + 7)
                chain(dve.tensor_reduce(sms[:, 1:2], smt[:, :], AX.X, ALU.add))
                settled()
                chain(dve.reciprocal(fac[:, 1:3], sms[:, 1:3]))
                settled()
                chain(dve.tensor_tensor(fac[:, 1:3], fac[:, 1:3], grow[:, p, 1:3], ALU.mult))
                settled()
                full(dve, ("pv", p))
                if p:
                    full(dve, ("pvt", p - 1))
                pv = bank(("pv", p))
                chain(dve.tensor_scalar(pvs[:, :], pv[:, 128:256], fac[:, 1:2], None, ALU.mult))
                settled()
                chain(dve.scalar_tensor_tensor(pvs[:, :], pv[:, 256:384], fac[:, 2:3], pvs[:, :], ALU.mult, ALU.add))
                settled()
                drain(dve.tensor_tensor(pvs[:, :], pvs[:, :], pv[:, 0:128], ALU.add), ("pv", p))
            sample_out(3)
            for c in range(C):
                add_to_h(("wo", c), c)
            norm(4)
            dve.memset(ones1[:, :], 1.0).then_inc(routed_ready, 1)
            dve.memset(scat, 0.0).then_inc(item_cleared, 1)
            dve.memset(ye, 0.0).then_inc(item_cleared, 1)

            chain(dve.memset(rl, 0.0))
            settled()
            full(dve, ("rt",))
            chain(dve.tensor_copy(rl[:, 0:2, :], bank(("rt",))[:, 0:16].rearrange("p (i e) -> p i e", i=2)))
            drain(dve.tensor_copy(rl[0:32, 2, :], bank(("rt",))[0:32, 16:24]), ("rt",))
            settled()
            drained(dve, ("rt",))
            chain(dve.tensor_reduce(rmx[:, :], rl, AX.X, ALU.max))
            settled()
            dve.tensor_scalar(rmx[:, :], rmx[:, :], -1.0, None, ALU.mult).then_inc(rmax_ready, 1)
            for i in range(3):
                other = rl[:, i, :].unsqueeze(1).to_broadcast([128, 8, 8])
                own = rl[:, i, :].unsqueeze(2).to_broadcast([128, 8, 8])
                chain(dve.tensor_tensor(cmp8[0], other, own, ALU.is_gt))
                chain(dve.tensor_tensor(cmp8[1], other, own, ALU.is_equal))
                settled()
                chain(dve.tensor_tensor(cmp8[1], cmp8[1], tri[:, 0:8, 0:8], ALU.mult))
                settled()
                chain(dve.tensor_tensor(cmp8[0], cmp8[0], cmp8[1], ALU.add))
                settled()
                chain(dve.tensor_reduce(rk[:, i, :], cmp8[0], AX.X, ALU.add))
                settled()
            dve.tensor_scalar(routed, rk, 1.5, None, ALU.is_lt).then_inc(routed_ready, 1)
            dve.wait_ge(rexp_ready, 3)
            dve.wait_ge(routed_ready, 2)
            chain(dve.tensor_tensor(rg, routed, rg, ALU.mult))
            settled()
            chain(dve.tensor_reduce(rsm[:, :], rg, AX.X, ALU.add))
            settled()
            chain(dve.reciprocal(rsm[:, :], rsm[:, :]))
            settled()
            chain(dve.tensor_tensor(rg, rg, rsm[:, :].unsqueeze(2).to_broadcast([128, 3, 8]), ALU.mult))
            full(dve, ("pos",))
            pos = bank(("pos",))
            chain(dve.scalar_tensor_tensor(pos1[:, 0:2, :], pos[:, 0:16].rearrange("p (i e) -> p i e", i=2), 1.0,
                                           routed[:, 0:2, :], ALU.add, ALU.mult))
            chain(dve.scalar_tensor_tensor(pos1[0:32, 2, :], pos[0:32, 16:24], 1.0, routed[0:32, 2, :], ALU.add, ALU.mult))
            dve.wait_ge(route_in, 16 * 3)
            drain(dve.tensor_tensor(over.rearrange("p (s e) -> p s e", e=8),
                                    pos[0:1, 24:32].unsqueeze(1).to_broadcast([1, SPLITS - 1, 8]),
                                    xthr.rearrange("p (s e) -> p s e", e=8), ALU.is_gt), ("pos",))
            drained(dve, ("pos",))
            chain(dve.tensor_tensor(osq, over.unsqueeze(1).to_broadcast([1, NX, NX]), tri[0:1, 0:NX, 0:NX], ALU.mult))
            chain(dve.tensor_reduce(okey[:, 0:1], over, AX.X, ALU.add))
            settled()
            for j in range(2):
                chain(dve.tensor_scalar(items_f[:, 2 * NI + j:2 * NI + j + 1], okey[:, 0:1], float(EXPERTS - j), None, ALU.add))
            settled()
            chain(dve.tensor_reduce(okey, osq, AX.X, ALU.add))
            settled()
            chain(dve.scalar_tensor_tensor(okey, okey, float(EXPERTS + 1), over, ALU.add, ALU.mult))
            settled()
            chain(dve.tensor_tensor(ohit, okey.unsqueeze(1).to_broadcast([1, NI, NX]),
                                    slot1.unsqueeze(2).to_broadcast([1, NI, NX]), ALU.is_equal))
            settled()
            for row, value in enumerate((xe, xs)):
                chain(dve.tensor_tensor(oval, ohit, value.unsqueeze(1).to_broadcast([1, NI, NX]), ALU.mult))
                settled()
                chain(dve.tensor_reduce(items_f[:, NI * row:NI * row + NI], oval, AX.X, ALU.add))
                settled()
            chain(dve.tensor_tensor(items_f[:, 0:NI], items_f[:, 0:NI], e0, ALU.add))
            settled()
            dve.tensor_copy(items[:, :], items_f).then_inc(items_ready, 1)

            n_items, more = item_count(dve)
            with dve.Fori(0, n_items) as i:
                M = ("m", 0)
                e = item_value(dve, 0, i, EXPERTS - 1)
                split = item_value(dve, 1, i, SPLITS - 1)
                numbers = count[:, bass.ds(split * CAP, CAP)]
                for k in range(3):
                    n = 128 if k < 2 else 32
                    dve.tensor_scalar(pick[0:n, k, :], numbers[0:n], pos1[0:n, k, bass.ds(e, 1)], None,
                                      ALU.is_equal).then_inc(picks_ready, 1)
                for k in range(3):
                    n = 128 if k < 2 else 32
                    dve.tensor_scalar(wpick[0:n, k, :], numbers[0:n], pos1[0:n, k, bass.ds(e, 1)], rg[0:n, k, bass.ds(e, 1)],
                                      ALU.is_equal, ALU.mult).then_inc(picks_ready, 1)
                for c in range(C):
                    add_to_h(M, c, i, M_SCAT + c)
                for f in range(FC):
                    dve.wait_ge(sig_ready, HALVES * FC + f + 1 + FC * i)
                    g = bank(M, M_GU + f)
                    dve.tensor_tensor(sige[:, f, :], sige[:, f, :], g[:, 0:CAP], ALU.mult).then_inc(silu_ready, 1)
                    dve.wait_ge(silu_ready, f + 1 + FC * i)
                    drain(dve.tensor_tensor(he[:, f, :], sige[:, f, :], g[:, CAP:2 * CAP], ALU.mult), M, M_GU + f)
            for c in range(C):
                add_to_h(("fs", c), c, more)
            norm(5)
            ple(1, more)

        @block.tensor
        def _(pe):
            def g_linear(label, rhs, e=0, k=0, ready=None):
                g_arrived(pe, label, e, k)
                bank_free(pe, label, e, k)
                tile = gslot(label, k)
                for i in range(C):
                    if ready is not None:
                        pe.wait_ge(a_ready, ready + i + 1)
                    ins = pe.matmul(bank(label, k)[:, 0:T], tile[:, 128 * i:128 * i + 128], rhs[:, i, :],
                                    start=i == 0, stop=i == C - 1)
                fill(ins, label, k)

            def norm_step(i, c, more=0):
                if c == 0:
                    bank_free(pe, ("norm", i), more)
                pe.wait_ge(sq_ready, C * i + c + 1)
                ins = pe.matmul(bank(("norm", i))[:, 0:T], ones[:, :], sqs[i][:, c, :], start=c == 0, stop=c == C - 1)
                if c == C - 1:
                    fill(ins, ("norm", i))

            def norm(i, more=0):
                for c in range(C):
                    norm_step(i, c, more)

            def norm_beside(i, c, first):
                if c == first:
                    for k in range(first):
                        norm_step(i, k)
                elif c > first:
                    norm_step(i, c - 1)
                if c == C - 1:
                    norm_step(i, c)

            pe.wait_ge(distance_in, 16 * 2)
            pe.wait_ge(rb_mask, 1)
            fill(pe.matmul(bank(("bv",))[0:HEADS, 0:OHL], rbx, ohr, start=True, stop=True), ("bv",))

            def table(label):
                bank_free(pe, label)
                kind, i = (label + (0,))[:2]
                if kind == "ts":
                    if i == 0:
                        pe.wait_ge(lt_in, 16 * 8)
                        pe.wait_ge(tables_in, 16 * NTABLE)
                    n = 512 if i < 5 else 160
                    ins = pe.matmul(bank(label)[:, 0:n], lt, ohs[i // 4][:, 512 * (i % 4):512 * (i % 4) + n], start=True, stop=True)
                elif kind == "tp":
                    if i == 0:
                        pe.wait_ge(flip_in, 16)
                        pe.wait_ge(bias_in, 16)
                    ins = pe.matmul(bank(label)[:, :], flip[:, :], tabP_[:, 512 * i:512 * i + 512], start=True, stop=True)
                else:
                    for i in range(2):
                        for n in range(8):
                            y = 128 * i - 32 * n - 31 + 255
                            ins = pe.matmul(bank(label)[:, 16 * (8 * i + n):16 * (8 * i + n) + 16], ohv[:, y:y + 128], rbx,
                                            start=True, stop=True)
                fill(ins, label)

            pe.wait_ge(wcmp_in, 16 * 4)
            for b in range(B):
                pe.wait_ge(c_in[b % 2], 16 * PAGES * (b // 2 + 1))
                src = cbufs[b % 2].rearrange("p (i c g l n) -> p i c g l n", i=PAGES, c=2, g=GROUPS, l=16)
                for c, name in enumerate(("ck", "cv")):
                    bank_free(pe, (name, b))
                    for g in range(GROUPS):
                        h, a = 64 * (g % 2), g // 2
                        for l in range(16):
                            ins = pe.matmul(bank((name, b))[h:h + 64, NB * a:NB * a + NB], wc[:, 64 * c + 16 * g + l, :],
                                            src[:, :, c, g, l, :], start=l == 0, stop=l == 15)
                    fill(ins, (name, b))
                for label in TABLES[2 * b:2 * b + 2]:
                    table(label)
            pe.wait_ge(consts_in, 16 * NCONST)
            for a in range(2):
                bank_free(pe, ("css", a))
                drained(pe, ("ck", 7))
                fill(pe.matmul(bank(("css", a))[:, :], bones[:, :], kcsq[:, a, :], start=True, stop=True), ("css", a))

            drained(pe, ("cv", 6))
            drained(pe, ("cv", 7))
            for p in range(4):
                bank_free(pe, ("ct", p))
                for a in range(2):
                    ins = pe.transpose(bank(("ct", p))[:, 128 * a:128 * a + 128], vraw[:, a, 128 * p:128 * p + 128], ident[:, :])
                fill(ins, ("ct", p))

            norm(0)
            for c in range(C):
                for name in ("gc", "v", "gb"):
                    g_linear((name, c), aT, ready=0 if c == 0 and name == "gc" else None)
            for c in range(C):
                if c == 0:
                    for k in range(C):
                        drained(pe, ("gb", k))
                g_linear(("co", c), zT)
                norm_beside(1, c, 3)

            def dense(turns, ready):
                pe.wait_ge(a_ready, ready)
                with pe.Fori(0, turns) as e:
                    L = ("f", 0, 0)
                    for k in range(2 * FC):
                        g_linear(L, aT, e, k)
                    for c in range(C):
                        n = c
                        pe.wait_ge(d_in[n % DS], 16 * (n // DS + 1) + 16 * (C // DS) * e)
                        tile = dring[:, (n % DS) * DT:(n % DS + 1) * DT]
                        bank_free(pe, L, e, 2 * FC + c)
                        for f in range(FC):
                            if c == 0:
                                drained(pe, L, e, 2 * f + 1)
                            ins = pe.matmul(bank(L, 2 * FC + c)[:, 0:T], tile[:, 128 * f:128 * f + 128], hff[:, f, :],
                                            start=f == 0, stop=f == FC - 1)
                        fill(ins, L, 2 * FC + c)

            def ple(layer, ready, more=0):
                for c in range(C):
                    g_arrived(pe, ("pp", layer, c // 4), more)
                    g_linear(("pg", layer, c), aT, more, ready=ready if c == 0 else None)
                    bank_free(pe, ("pp", layer, c), more)
                    tile = gslot(("pp", layer, c // 4))
                    for k in range(2):
                        o = (2 * (c % 4) + k) * 128
                        ins = pe.matmul(bank(("pp", layer, c))[:, 0:T], tile[:, o:o + 128], pT[:, layer, k, :],
                                        start=k == 0, stop=k == 1)
                    fill(ins, ("pp", layer, c))

            dense(HALVES, 2 * C)
            norm(2)
            ple(0, 2 * C)
            norm(3)

            def block_sums(label, n):
                bank_free(pe, label)
                pe.wait_ge(hsq_ready, n + 1)
                fill(pe.matmul(bank(label)[:, 0:T], bones[:, :], tmp[:, n % 2, :], start=True, stop=True), label)

            for c in range(8):
                g_linear(("kv", c), aT, ready=3 * C if c == 0 else None)
                if c > 4:
                    block_sums(("kss", c - 1), c - 5)
            for i in range(3):
                bank_free(pe, ("vt", i))
            for q in range(4):
                g_arrived(pe, ("vt", q))
                tile = gslot(("vt", q))
                for k in range(2):
                    for i in range(3):
                        n = 128 if i < 2 else 32
                        ins = pe.matmul(bank(("vt", i))[0:n, :], aT[:, 2 * q + k, 128 * i:128 * i + n],
                                        tile[:, 512 * k:512 * k + 512], start=q == 0 and k == 0, stop=q == 3 and k == 1)
                        if q == 3 and k == 1:
                            fill(ins, ("vt", i))
            block_sums(("kss", 7), 3)
            bank_free(pe, ("gt",))
            for i in range(3):
                n = 128 if i < 2 else 32
                for c in range(C):
                    ins = pe.matmul(bank(("gt",))[0:n, 48 * i:48 * i + 48], aT[:, c, 128 * i:128 * i + n], wgate[:, c, :],
                                    start=c == 0, stop=c == C - 1)
            fill(ins, ("gt",))
            for j in range(8):
                g_linear(("q", j), aT)
                if j:
                    block_sums(("qss", j - 1), 4 + j - 1)
            pe.wait_ge(kvp_in, 16 * 16)
            bank_free(pe, ("kcp",))
            for g in range(GROUPS):
                h, a = 64 * (g % 2), g // 2
                for l in range(16):
                    ins = pe.matmul(bank(("kcp",))[h:h + 64, 8 * a:8 * a + 8], wc[:, 16 * g + l, :], kvp[:, g, 2 * l:TP:32],
                                    start=l == 0, stop=l == 15)
            fill(ins, ("kcp",))
            block_sums(("qss", 7), 11)
            bank_free(pe, ("vcp",))
            for g in range(GROUPS):
                for l in range(16):
                    ins = pe.matmul(bank(("vcp",))[0:8, 64 * g:64 * g + 64], kvp[:, 4 + g, 2 * l:TP:32], wc[:, 64 + 16 * g + l, :],
                                    start=l == 0, stop=l == 15)
            fill(ins, ("vcp",))
            bank_free(pe, ("kcps",))
            pe.wait_ge(hsq_ready, 13)
            fill(pe.matmul(bank(("kcps",))[:, 0:16], bones[:, :], tmp_[:, 0:16], start=True, stop=True), ("kcps",))

            pe.wait_ge(kn_ready, 8)
            pe.wait_ge(q_ready, 8)
            pe.wait_ge(kcn_ready, 3)
            for u in range(18):
                if u < 16:
                    j, g2 = u // 2, u % 2
                    a = j // 4
                    h = slice(64 * g2, 64 * g2 + 64)
                    for i in range(2):
                        nk = 128 * (i + 1)
                        bank_free(pe, ("pl", u, i))
                        if i == 0:
                            for k in range(2):
                                pe.matmul(bank(("pl", u, 0))[:, 256 + 8 * k:264 + 8 * k], q1[h, j, 128 * k:128 * k + 128],
                                          kcpn[h, a, :], start=True, stop=True)
                        for r in range(2):
                            ins = pe.matmul(bank(("pl", u, i))[:, r * nk:(r + 1) * nk], q1[h, j, 128 * i:128 * i + 128],
                                            kn[h, 2 * r + a, 0:nk], start=True, stop=True)
                        fill(ins, ("pl", u, i))
                if 1 <= u <= 16:
                    v = u - 1
                    w = v % 2
                    pe.wait_ge(pscaled, 6 * (v + 1))
                    for i in range(2):
                        bank_free(pe, ("ptp", v, i))
                        if i == 0:
                            for k in range(2):
                                pe.transpose(bank(("ptp", v, 0))[0:8, 256 + 128 * k:384 + 128 * k], Scp[:, w, k, :], ident[:, :])
                        for k in range(2 * (i + 1)):
                            ins = pe.transpose(bank(("ptp", v, i))[:, 128 * k:128 * k + 128],
                                               Sp[:, w, 256 * i + 128 * k:256 * i + 128 * k + 128], ident[:, :])
                        fill(ins, ("ptp", v, i))
                if u >= 2:
                    v = u - 2
                    w, j, g2 = v % 2, v // 2, v % 2
                    g = 2 * (j // 4) + g2
                    bank_free(pe, ("po", v))
                    drained(pe, ("ptp", v, 0))
                    drained(pe, ("ptp", v, 1))
                    if v == 0:
                        drained(pe, ("vcp",))
                    o = bank(("po", v))
                    h = slice(64 * g2, 64 * g2 + 64)
                    for r in range(2):
                        pe.matmul(o[h, 0:256], vtok[:, 0, 256 * r + 64 * g:256 * r + 64 * g + 64], PTp[:, w, r, 0:256],
                                  start=r == 0, stop=False)
                        pe.matmul(o[h, 128:256], vtok[:, 1, 256 * r + 64 * g:256 * r + 64 * g + 64], PTp[:, w, r, 256:384],
                                  start=False, stop=False)
                    fill(pe.matmul(o[h, 0:256], vcp[:, 64 * g:64 * g + 64], PTc[:, w, :], start=False, stop=True), ("po", v))

            pe.wait_ge(qb_ready, 12)

            def values_transposed(p):
                bank_free(pe, ("pvt", p))
                drained(pe, ("pv", p))
                fill(pe.transpose(bank(("pvt", p))[:, 0:128], pvs[:, :], ident[:, :]), ("pvt", p))

            for p in range(4):
                def rows(b2, a):
                    return slice(64 * b2 + 32 * a, 64 * b2 + 32 * a + 32)

                bank_free(pe, ("sc", p))
                for b2 in range(2):
                    for a in range(2):
                        ins = pe.matmul(bank(("sc", p))[rows(b2, a), 0:128], QB[:, 0, 2 * p + b2, a, :],
                                        kcn[:, a, 128 * p:128 * p + 128], start=True, stop=True)
                fill(ins, ("sc", p))
                bank_free(pe, ("sn", p))
                for b2 in range(2):
                    for a in range(2):
                        for r in range(2):
                            ins = pe.matmul(bank(("sn", p))[rows(b2, a), 32 * r:32 * r + 32], QB[:, 1 + r, 2 * p + b2, a, :],
                                            kn[:, 2 * r + a, TP:T], start=True, stop=True)
                fill(ins, ("sn", p))
                if p:
                    values_transposed(p - 1)

                def key_tile(q, s, tile, n, b2, r, view, last):
                    ksq = ksqs[(10 * p + n) % 3]
                    pe.wait_ge(ksq_ready, 10 * p + n + 1)
                    g_arrived(pe, tile)
                    for a in range(2):
                        i1 = pe.matmul(bank(q)[rows(b2, a), :], QB[:, r, 2 * p + b2, a, :], view(gslot(tile), a),
                                       start=True, stop=True)
                        i2 = pe.matmul(bank(s)[rows(b2, a), :], bo32[:, :], view(ksq, a), start=True, stop=True)
                        if a == 0:
                            continue
                        if last:
                            fill(i1, q)
                            fill(i2, s)
                        else:
                            i2.then_inc(keys_used, 1)

                def win_view(t, a):
                    return t[:, 512 * a:512 * a + 512]

                def page_view(t, a):
                    return t.rearrange("p (i a n) -> p i a n", i=4, a=2)[:, :, a, :]

                bank_free(pe, ("wq", p))
                bank_free(pe, ("wss", p))
                for b2 in range(2):
                    key_tile(("wq", p), ("wss", p), ("wk", p, b2), b2, b2, 2, win_view, b2 == 1)
                bank_free(pe, ("imp", p))
                pe.wait_ge(cprob_ready, p + 1)
                fill(pe.matmul(bank(("imp", p))[:, 0:128], rsum[:, :], SC[:, :], start=True, stop=True), ("imp", p))
                for t in range(4):
                    bank_free(pe, ("sq", p, t))
                    bank_free(pe, ("sss", p, t))
                    for b2 in range(2):
                        key_tile(("sq", p, t), ("sss", p, t), ("sk", p, t, b2), 2 + 2 * t + b2, b2, 1, page_view, b2 == 1)
                pe.wait_ge(sscaled, p + 1)
                for i in range(6):
                    pe.wait_ge(sexp_ready, 7 * p + 2 + i)
                    bank_free(pe, ("pt", p, i))
                    o = bank(("pt", p, i))
                    if i == 0:
                        parts = [(0, SCg[:, :])] + [(128 * (k + 1), SW[:, 128 * k:128 * k + 128]) for k in range(3)]
                    elif i == 1:
                        parts = [(0, SW[:, 384:512]), (128, SW[:, 512:544]), (256, S[:, KEYS:KEYS + 32])]
                    else:
                        parts = [(128 * k, S[:, 512 * (i - 2) + 128 * k:512 * (i - 2) + 128 * k + 128]) for k in range(4)]
                    for col, src in parts:
                        n = src.shape[1]
                        ins = pe.transpose(o[0:n, col:col + 128], src, ident[:, :])
                    fill(ins, ("pt", p, i))
                for i in range(6):
                    drained(pe, ("pt", p, i))

                bank_free(pe, ("pv", p))

                def values(k, views, branch, first=False, last=False, parts=128, used=False):
                    col = 128 * branch
                    for b2 in range(2):
                        for a in range(2):
                            ins = pe.matmul(bank(("pv", p))[rows(b2, a), col:col + 128], PT[0:parts, k, rows(b2, a)],
                                            views[b2][0:parts, 128 * a:128 * a + 128], start=first, stop=last)
                        if used:
                            if last and branch == 1 and b2:
                                fill(ins, ("pv", p))
                            else:
                                ins.then_inc(values_used, 1)

                values(0, [vcs[:, p, :]] * 2, 0, first=True, last=True)
                values(5, [vtok[:, 2, 256:512]] * 2, 2, parts=32, first=True)
                for b2 in range(2):
                    g_arrived(pe, ("wv", p, b2))
                for k in range(4):
                    values(1 + k, [gslot(("wv", p, b2))[:, 256 * k:256 * k + 256] for b2 in range(2)], 2,
                           last=k == 3, used=k == 3)
                values(6, [vtok[:, 2, 0:256]] * 2, 1, parts=32, first=True)
                for t in range(4):
                    for b2 in range(2):
                        pe.wait_ge(v_in[4 * b2 + t], 64 * (p + 1))
                    for k in range(4):
                        final = t == 3 and k == 3
                        values(7 + 4 * t + k, [vbufs[4 * b2 + t][:, 256 * k:256 * k + 256] for b2 in range(2)], 1,
                               last=final, used=k == 3)

            values_transposed(3)
            pe.wait_ge(so_ready, 12)
            drained(pe, ("pvt", 3))
            drained(pe, ("po", 15))
            for c in range(C):
                g_linear(("wo", c), oT)
                norm_beside(4, c, 3)
            bank_free(pe, ("rt",))
            pe.wait_ge(a_ready, 5 * C)
            for i in range(3):
                n = 128 if i < 2 else 32
                for c in range(C):
                    ins = pe.matmul(bank(("rt",))[0:n, 8 * i:8 * i + 8], aT[:, c, 128 * i:128 * i + n], rout[:, c, :],
                                    start=c == 0, stop=c == C - 1)
            fill(ins, ("rt",))
            for k in range(6):
                i, h, n = k // 2, k % 2, 128 if k < 4 else 32
                bank_free(pe, ("at", k))
                for c in range(4):
                    ins = pe.transpose(bank(("at", k))[0:n, 128 * c:128 * c + 128], aT[:, 4 * h + c, 128 * i:128 * i + n], ident[:, :])
                fill(ins, ("at", k))
            pe.wait_ge(routed_ready, 2)
            pe.wait_ge(route_in, 16 * 3)
            bank_free(pe, ("pos",))
            for i in range(4):
                n = 32 if i == 2 else 128
                terms = [(ones1[:, 0:n], routed[:, j, :]) for j in range(min(i, 2))]
                terms += [(before[0:n, 0:n], routed[0:n, i, :])] if i < 3 else [(ones1[0:32, :], routed[0:32, 2, :])]
                for j, (w, r) in enumerate(terms):
                    ins = pe.matmul(bank(("pos",))[0:n, 8 * i:8 * i + 8], w, r, start=j == 0, stop=j == len(terms) - 1)
            fill(ins, ("pos",))
            for k in range(6):
                drained(pe, ("at", k))

            n_items, more = item_count(pe)
            pe.wait_ge(item_cleared, 2)
            M = ("m", 0)

            def scatter(label, k, e):
                for c in range(C):
                    bank_free(pe, label, e, k + c)
                    fill(pe.matmul(bank(label, k + c)[:, 0:T], ye[:, 128 * c:128 * c + 128], scat, start=True, stop=True),
                         label, k + c)

            with pe.Fori(0, n_items) as i:
                for h in range(2):
                    bank_free(pe, M, i, h)
                    for c in range(4 * h, 4 * h + 4):
                        for k in range(3):
                            n = 128 if k < 2 else 32
                            if c == 0:
                                pe.wait_ge(picks_ready, k + 1 + 6 * i)
                            ins = pe.matmul(bank(M, h)[:, CAP * (c % 4):CAP * (c % 4) + CAP], atok[0:n, k, 128 * c:128 * c + 128],
                                            pick[0:n, k, :], start=k == 0, stop=k == 2)
                    fill(ins, M, h)
                for k in (M_DOWN, M_DOWN + 1):
                    drained(pe, M, i, k - MR)
                scatter(M, M_SCAT, i)
                bank_free(pe, M, i, M_SEL)
                pe.wait_ge(picks_ready, 6 + 6 * i)
                for k in range(3):
                    n = 128 if k < 2 else 32
                    ins = pe.transpose(bank(M, M_SEL)[0:CAP, 128 * k:128 * k + n], wpick[0:n, k, :], ident[0:n, 0:n])
                fill(ins, M, M_SEL)
                for h in range(2):
                    drained(pe, M, i, h)
                for f in range(FC):
                    bank_free(pe, M, i, M_GU + f)
                    for u in range(2):
                        g_arrived(pe, M, i, 2 * f + u)
                        for c in range(C):
                            ins = pe.matmul(bank(M, M_GU + f)[:, CAP * u:CAP * u + CAP],
                                            gslot(M, 2 * f + u)[:, 128 * c:128 * c + 128], ae[:, c, :], start=c == 0, stop=c == C - 1)
                    fill(ins, M, M_GU + f)
                for h in range(2):
                    bank_free(pe, M, i, M_DOWN + h)
                for f in range(FC):
                    if f:
                        drained(pe, M, i, M_GU + f)
                    g_arrived(pe, M, i, 2 * FC + f)
                    for h in range(2):
                        ins = pe.matmul(bank(M, M_DOWN + h)[0:CAP, :], he[:, f, :], gslot(M, 2 * FC + f)[:, 512 * h:512 * h + 512],
                                        start=f == 0, stop=f == FC - 1)
                        if f == FC - 1:
                            fill(ins, M, M_DOWN + h)
                    if f < FC - 1:
                        ins.then_inc(down_used, 1)
            for k in (M_DOWN, M_DOWN + 1):
                drained(pe, M, more, k)
            scatter(("fs", 0), 0, more)
            norm(5, more)
            ple(1, 5 * C, more)


def constants():
    f = np.float32
    eye = np.eye(128, dtype=f)
    k = {"ident": eye, "ones": np.full((128, 128), 1.0 / D, f)}
    half = np.arange(128) // 64
    k["bones"] = (half[:, None] == half[None, :]).astype(f) / f(HD)
    k["bo32"] = (half[:, None] == (np.arange(32) // 16)[None, :]).astype(f) / f(HD)
    row = np.arange(128)
    b2, head, step = row // 64, row // 4 % 16, row % 4
    key = (b2 * 4 + head // R) * 4 + step
    k["rsum"] = (key[:, None] == key[None, :]).astype(f)
    i = np.arange(32)
    k["tri"] = np.ascontiguousarray(np.broadcast_to((i[None, :] < i[:, None]).astype(f), (128, 32, 32)))
    q = np.arange(256).reshape(2, 128).T
    k["pmask"] = (q[:, :, None] >= np.arange(8) * 32 + 31).astype(f)
    k["before"] = np.triu(np.ones((128, 128), f), 1)
    k["count"] = np.tile(np.arange(1, SPLITS * CAP + 1, dtype=f), (128, 1))
    s, e = np.divmod(np.arange(EXPERTS * (SPLITS - 1)), EXPERTS)
    slot = np.arange(EXPERTS * SPLITS)
    k["xtab"] = np.concatenate([CAP * (s + 1), e, s + 1, slot + 1, np.where(slot < EXPERTS, slot, 0)]).astype(f)[None]
    dist = np.arange(OHL) - 255
    oh = np.zeros((BUCKETS + 1, OHL), f)
    oh[np.where(dist < 0, BUCKETS, bucket(dist)), np.arange(OHL)] = 1
    k["ohv"] = oh
    k["ohr"] = np.ascontiguousarray(oh[:, ::-1])
    k["flip"] = np.ascontiguousarray(eye[::-1])
    t = np.arange(STEPS)[:, None]
    new = np.tile(np.arange(STEPS), B)
    ends = np.tile((np.arange(NB) + 1) * 32 - 1, 2)
    rel = np.concatenate([KEYS + t - np.arange(KEYS), KEYS + t - (KEYS - WIN + np.arange(WIN)),
                          np.maximum(t - new, 0), KEYS + t - ends], axis=1)
    k["ohs"] = (bucket(rel)[:, None, :] == np.arange(BUCKETS)[None, :, None]).astype(f).reshape(128, -1)
    m = np.zeros((128, 768), bool)
    m[:, 0:WIN] = WIN + step[:, None] - np.arange(WIN) < WIN
    tok = np.arange(32)
    for p in range(4):
        m[:, WIN + 32 * p:WIN + 32 * p + 32] = (tok // 4 == 2 * p + b2[:, None]) & (tok % 4 <= step[:, None])
    m[:, 640:768] = np.arange(128) // NB == b2[:, None]
    k["masks"] = np.where(m, f(0), f(NEG))
    return k


def kernel(x_prompt, x_sample, state_conv, cache_cmp, cache_sel, state_win, page_table, p_prompt, p_sample, norm_mix,
           norm_ffn, norm_ple, conv_w_in, conv_w, conv_w_out, nsa_w_in, nsa_w_cmp, nsa_q_norm, nsa_k_norm, nsa_w_out,
           rel_bias, ffn_w_gate, ffn_w_up, ffn_w_down, moe_router, moe_w_gate, moe_w_up, moe_w_down, ple_w_proj, ple_w_gate):
    import concourse.bacc as bacc
    from concourse.bass_utils import run_bass_kernel_spmd

    def chunks(w):
        w = np.asarray(w)
        return w.reshape(w.shape[0] // 128, 128, w.shape[1] // 128, 128).transpose(2, 1, 0, 3).reshape(w.shape[1] // 128, 128, -1)

    def features(a):
        a = np.asarray(a)
        return a.reshape(a.shape[0], -1, 128).transpose(2, 1, 0)

    def gate_up(g, u):
        g, u = chunks(g), chunks(u)
        return np.stack([g, u], axis=1).reshape(2 * g.shape[0], 128, -1)

    a = {k: np.asarray(v) for k, v in constants().items()}
    x = np.concatenate([np.asarray(x_prompt).reshape(TP, D), np.asarray(x_sample).reshape(32, D)])
    a["x"] = features(x)
    p = np.concatenate([np.asarray(p_prompt).reshape(2, TP, 256), np.asarray(p_sample).reshape(2, 32, 256)], axis=1)
    a["p"] = np.stack([features(p[0]), features(p[1])], axis=1)
    a["state"] = np.asarray(state_conv)[0].reshape(B, 2, C, 128).transpose(3, 2, 0, 1)
    order = [norm_mix[0], norm_ffn[0], norm_ple[0], norm_mix[1], norm_ffn[1], norm_ple[1]]
    a["gains"] = np.concatenate([np.asarray(g).reshape(C, 128).T for g in order], axis=1)
    a["convw"] = np.asarray(conv_w)[0].reshape(3, C, 128).transpose(2, 0, 1).reshape(128, 24)
    a["gq"] = np.tile(np.asarray(nsa_q_norm)[0], 2).reshape(128, 1)
    a["gk"] = np.tile(np.asarray(nsa_k_norm)[0], (1, 2)).T
    a["rel_bias"] = np.asarray(rel_bias)
    w = chunks(np.asarray(conv_w_in)[0]).reshape(3, C, 128, 1024)
    a["conv_in"] = w[[1, 2, 0]].transpose(1, 0, 2, 3).reshape(3 * C, 128, 1024)
    a["conv_out"] = chunks(np.asarray(conv_w_out)[0])
    g, u, d = (np.asarray(t)[0] for t in (ffn_w_gate, ffn_w_up, ffn_w_down))
    a["dense_gu"] = np.stack([gate_up(g[:, FE * i:FE * i + FE], u[:, FE * i:FE * i + FE]) for i in range(HALVES)])
    a["dense_down"] = np.stack([chunks(d[FE * i:FE * i + FE]) for i in range(HALVES)])
    g, u, d = (np.asarray(t)[0] for t in (moe_w_gate, moe_w_up, moe_w_down))
    a["moe"] = np.stack([np.concatenate([gate_up(g[e], u[e]), d[e].reshape(FC, 128, D)]) for e in range(EXPERTS)])
    a["ple_gate"] = np.stack([chunks(t) for t in np.asarray(ple_w_gate)])
    a["ple_proj"] = np.stack([chunks(t).reshape(2, 4, 128, 256).transpose(0, 2, 1, 3).reshape(2, 128, 1024)
                              for t in np.asarray(ple_w_proj)])
    w = np.asarray(nsa_w_in)[0]
    q = w[:, :1024].reshape(D, 2, 2, R, HD).transpose(0, 1, 3, 2, 4).reshape(D, 1024)
    a["nsa_q"] = chunks(q)
    kv = w[:, 1024:2560].reshape(D, 3, 4, 2, HD)
    cols = [kv[:, 0, :, 0], kv[:, 0, :, 1], kv[:, 1, :, 0], kv[:, 2, :, 0]]
    a["nsa_kv"] = chunks(np.concatenate([t.reshape(D, 256) for t in cols], axis=1))
    vt = kv[:, 1:3, :, 1].reshape(4, 2, 128, 512)
    a["nsa_vt"] = vt.transpose(0, 2, 1, 3).reshape(4, 128, 1024)
    a["wgate"] = w[:, 2560:].reshape(C, 128, 48).transpose(1, 0, 2)
    a["rout"] = np.asarray(moe_router)[0].reshape(C, 128, 8).transpose(1, 0, 2)
    wo = np.asarray(nsa_w_out)[0].reshape(2, 2, R, HD, D).transpose(0, 2, 1, 3, 4).reshape(1024, D)
    a["nsa_out"] = chunks(wo)
    a["w_cmp"] = np.asarray(nsa_w_cmp)[0].reshape(16, 2, 4, 2, HD, HD).transpose(1, 4, 3, 2, 0, 5).reshape(128, 128, 64)
    c = np.asarray(cache_cmp)[0].reshape(POOL, 4, 16, 2, 4, 2, HD)
    a["cache_cmp"] = c.transpose(0, 3, 6, 5, 4, 2, 1).reshape(POOL, 128, 512)
    c = np.asarray(cache_sel)[0]
    a["cache_selk"] = c[:, :, :, 0].reshape(POOL, 128, 2, 2, HD).transpose(0, 3, 4, 2, 1).reshape(POOL, 128, 256)
    a["cache_selv"] = c[:, :, :, 1].reshape(POOL, 128, 256)
    c = np.asarray(state_win)[0]
    a["win_k"] = c[:, :, :, 0].reshape(B, WIN, 2, 2, HD).transpose(0, 3, 4, 2, 1).reshape(B, 128, 1024)
    a["win_v"] = c[:, :, :, 1].reshape(B, 4, 128, 256).transpose(0, 2, 1, 3).reshape(B, 128, 1024)
    a["state_win"] = c.reshape(B, WIN, 512)
    a["page_table"] = np.asarray(page_table).reshape(1, B * PAGES)

    nc = bacc.Bacc("TRN2", target_bir_lowering=False, num_devices=1)
    arrays, A, O = {}, {}, {}
    for name, v in a.items():
        v = np.ascontiguousarray(v)
        arrays["in_" + name] = v
        A[name] = nc.dram_tensor("in_" + name, v.shape, mybir.dt.from_np(v.dtype), kind="ExternalInput").ap()
    A["bias_by_distance"] = nc.dram_tensor("bias_by_distance", (HEADS, OHL), mybir.dt.float32, kind="Internal").ap()
    A["gscratch"] = nc.dram_tensor("gscratch", (B, HEADS, STEPS, 3), mybir.dt.float32, kind="Internal").ap()
    outs = {"h": (128, C, T), "conv": (128, 144), "kvT": (128, 8, T), "vtok": (128, 3, 512), "win_old": (B, WIN - STEPS, 512)}
    for name, shape in outs.items():
        O[name] = nc.dram_tensor("out_" + name, shape, mybir.dt.float32, kind="ExternalOutput").ap()
    trunk(nc, A, O)
    r = run_bass_kernel_spmd(nc, [arrays], core_ids=[0]).results[0]

    h = r["out_h"].transpose(2, 1, 0).reshape(T, D)
    conv = r["out_conv"]
    conv_p = conv[:, :16].reshape(128, C, 2).transpose(2, 1, 0).reshape(1, 1, 2, D)
    conv_s = conv[:, 16:].reshape(128, C, B, 2).transpose(2, 3, 1, 0).reshape(1, B, 2, D)
    kvt = r["out_kvT"].reshape(2, HD, 4, 2, T).transpose(4, 2, 3, 0, 1).reshape(T, 4, GROUPS, HD)
    vt = r["out_vtok"].transpose(1, 0, 2)
    v = np.concatenate([vt[0], vt[1], vt[2][:32]]).reshape(T, 2, GROUPS, HD)
    cmp_ = np.stack([kvt[:, 0], kvt[:, 1]], axis=2)
    sel = np.stack([kvt[:, 2], v[:, 0]], axis=2)
    win = np.stack([kvt[:, 3], v[:, 1]], axis=2)

    def prompt(t):
        return np.ascontiguousarray(t[:TP]).reshape(1, 1, TP, GROUPS, 2, HD)

    def sample(t):
        return np.ascontiguousarray(t[TP:]).reshape(1, B, STEPS, GROUPS, 2, HD)

    win_old = r["out_win_old"].reshape(1, B, WIN - STEPS, GROUPS, 2, HD)
    return (h[:TP].reshape(1, TP, D), h[TP:].reshape(B, STEPS, D), conv_p, conv_s, prompt(cmp_), sample(cmp_),
            prompt(sel), sample(sel), prompt(win), np.concatenate([win_old, sample(win)], axis=2))
```
